# Optimizing a Trainium2 kernel written in Bass

```python
import jax, jax.numpy as jnp
from jax import lax
import numpy as np

D_MODEL = 2048
BATCH = 1
SEQ = 256
DEPTH = 1

CHUNK = 64
EPS = 1e-6
A_HEADS = 8
A_DK = 128
A_DV = 128
A_CONV = 4
A_QK = A_HEADS * A_DK
A_V = A_HEADS * A_DV
B_HEADS = 4
B_DK = 128
B_DV = 256
B_GATE_RANK = 16
B_GATE_NORM = 16.0
B_QK = B_HEADS * B_DK
B_V = B_HEADS * B_DV
N_GROUPS = 4
EXP_PER_GROUP = 8
N_EXPERTS = N_GROUPS * EXP_PER_GROUP
TOPK_IN_GROUP = 2
D_FF_EXPERT = 512
ROW_BLOCK = 128
IN_SPLITS = (A_QK, A_QK, A_V, A_V, A_HEADS, A_HEADS,
             B_QK, B_QK, B_V, B_V, B_GATE_RANK, D_MODEL, D_MODEL)
IN_COLS = 2 * A_QK + 2 * A_V + 2 * A_HEADS + 2 * B_QK + 2 * B_V + B_GATE_RANK + 2 * D_MODEL

kernel_name = "hybrid_gdn_gla_hiermoe_block"

def _rmsnorm(x, w):
    xf = x.astype(jnp.float32)
    y = xf * lax.rsqrt(jnp.mean(xf * xf, axis=-1, keepdims=True) + EPS)
    return (y * w.astype(jnp.float32)).astype(x.dtype)

def _l2norm(x):
    xf = x.astype(jnp.float32)
    return xf * lax.rsqrt(jnp.sum(xf * xf, axis=-1, keepdims=True) + EPS)

def _split_cols(z):
    idx, acc = [], 0
    for s in IN_SPLITS[:-1]:
        acc += s
        idx.append(acc)
    return jnp.split(z, idx, axis=-1)

def _heads(t, n):
    b, s, _ = t.shape
    return t.reshape(b, s, n, -1).transpose(0, 2, 1, 3)

def _causal_depthwise_conv(x, w):
    k, c = w.shape
    return lax.conv_general_dilated(
        x, w[:, None, :].astype(x.dtype), window_strides=(1,), padding=[(k - 1, 0)],
        dimension_numbers=("NWC", "WIO", "NWC"), feature_group_count=c)

def _gated_delta_rule(q, k, v, beta, g):
    bsz, nh, s, dk = q.shape
    dv = v.shape[-1]
    n, c = s // CHUNK, CHUNK
    f32 = jnp.float32
    q = q.astype(f32).reshape(bsz, nh, n, c, dk) * (dk ** -0.5)
    k = k.astype(f32).reshape(bsz, nh, n, c, dk)
    v = v.astype(f32).reshape(bsz, nh, n, c, dv)
    beta = beta.astype(f32).reshape(bsz, nh, n, c)
    gc = jnp.cumsum(g.astype(f32).reshape(bsz, nh, n, c), axis=-1)
    causal = jnp.tril(jnp.ones((c, c), bool))
    strict = jnp.tril(jnp.ones((c, c), bool), -1)
    decay = jnp.exp(jnp.where(causal, gc[..., :, None] - gc[..., None, :], -jnp.inf))
    kb = k * beta[..., None]
    a_strict = jnp.where(strict, jnp.einsum("bhnid,bhnjd->bhnij", kb, k) * decay, 0.0)
    eye = jnp.eye(c, dtype=f32)
    t_mat = lax.linalg.triangular_solve(eye + a_strict, jnp.broadcast_to(eye, a_strict.shape),
                                        left_side=True, lower=True)
    u = jnp.einsum("bhnij,bhnjd->bhnid", t_mat, v * beta[..., None])
    w = jnp.einsum("bhnij,bhnjd->bhnid", t_mat, kb * jnp.exp(gc)[..., None])
    qk = jnp.einsum("bhnid,bhnjd->bhnij", q, k) * decay
    q_dec = q * jnp.exp(gc)[..., None]
    g_last = gc[..., -1]
    k_dec = k * jnp.exp(g_last[..., None] - gc)[..., None]

    def step(state, xs):
        u_n, w_n, qk_n, qd_n, kd_n, gl_n = xs
        v_new = u_n - jnp.einsum("bhid,bhde->bhie", w_n, state)
        o = jnp.einsum("bhid,bhde->bhie", qd_n, state) + jnp.einsum("bhij,bhje->bhie", qk_n, v_new)
        state = state * jnp.exp(gl_n)[..., None, None] + jnp.einsum("bhid,bhie->bhde", kd_n, v_new)
        return state, o

    xs = tuple(jnp.moveaxis(t, 2, 0) for t in (u, w, qk, q_dec, k_dec, g_last))
    _, o = lax.scan(step, jnp.zeros((bsz, nh, dk, dv), f32), xs)
    return jnp.moveaxis(o, 0, 2).reshape(bsz, nh, s, dv)

def _gla_chunked(q, k, v, gk):
    bsz, nh, s, dk = q.shape
    dv = v.shape[-1]
    n, c = s // CHUNK, CHUNK
    f32 = jnp.float32
    def chunks(t, d):
        return jnp.moveaxis(t.astype(f32).reshape(bsz, nh, n, c, d), 2, 0)
    qs = chunks(q, dk) * (dk ** -0.5)
    ks = chunks(k, dk)
    vs = chunks(v, dv)
    bs = jnp.cumsum(chunks(gk, dk), axis=-2)
    causal = jnp.tril(jnp.ones((c, c), bool))[:, :, None]

    def step(state, xs):
        q_n, k_n, v_n, b_n = xs
        dmat = jnp.exp(jnp.where(causal, b_n[..., :, None, :] - b_n[..., None, :, :], -jnp.inf))
        attn = jnp.sum(q_n[..., :, None, :] * k_n[..., None, :, :] * dmat, axis=-1)
        o = jnp.einsum("bhij,bhje->bhie", attn, v_n) + jnp.einsum("bhid,bhde->bhie", q_n * jnp.exp(b_n), state)
        b_last = b_n[..., -1, :]
        state = state * jnp.exp(b_last)[..., None] + jnp.einsum(
            "bhid,bhie->bhde", k_n * jnp.exp(b_last[..., None, :] - b_n), v_n)
        return state, o

    _, o = lax.scan(step, jnp.zeros((bsz, nh, dk, dv), f32), (qs, ks, vs, bs))
    return jnp.moveaxis(o, 0, 2).reshape(bsz, nh, s, dv)

def _hier_moe(h, w_rg, b_rg, w_re, b_re, w1, w3, w2):
    bsz, s, d = h.shape
    t = bsz * s
    ht = h.reshape(t, d)
    lg = (ht @ w_rg).astype(jnp.float32) + b_rg.astype(jnp.float32)
    pg = jax.nn.softmax(lg, axis=-1)
    p_top, g_idx = lax.top_k(pg, 1)
    le = jnp.einsum("td,dge->tge", ht, w_re).astype(jnp.float32) + b_re.astype(jnp.float32)
    le_sel = jnp.take_along_axis(le, jnp.broadcast_to(g_idx[:, :, None], (t, 1, EXP_PER_GROUP)), axis=1)[:, 0]
    l2, e_idx = lax.top_k(le_sel, TOPK_IN_GROUP)
    gate = jax.nn.softmax(l2, axis=-1) * p_top
    expert = g_idx * EXP_PER_GROUP + e_idx

    n_assign = t * TOPK_IN_GROUP
    e_flat = expert.reshape(-1)
    tok_flat = jnp.repeat(jnp.arange(t, dtype=jnp.int32), TOPK_IN_GROUP)
    w_flat = gate.reshape(-1).astype(h.dtype)
    order = jnp.argsort(e_flat)
    e_s, tok_s, w_s = e_flat[order], tok_flat[order], w_flat[order]
    counts = jnp.bincount(e_flat, length=N_EXPERTS)
    start = jnp.cumsum(counts) - counts
    padded = (counts + ROW_BLOCK - 1) // ROW_BLOCK * ROW_BLOCK
    pad_end = jnp.cumsum(padded)
    pad_start = pad_end - padded
    dest = pad_start[e_s] + jnp.arange(n_assign) - start[e_s]
    n_rows = ((n_assign + ROW_BLOCK - 1) // ROW_BLOCK + N_EXPERTS) * ROW_BLOCK
    row_tok = jnp.zeros((n_rows,), jnp.int32).at[dest].set(tok_s)
    row_w = jnp.zeros((n_rows,), h.dtype).at[dest].set(w_s)
    n_blk = n_rows // ROW_BLOCK
    blk_exp = jnp.minimum(jnp.searchsorted(pad_end, jnp.arange(n_blk) * ROW_BLOCK, side="right"),
                          N_EXPERTS - 1)
    xs = ht[row_tok].reshape(n_blk, ROW_BLOCK, d)

    def expert_rows(args):
        xb, e = args
        return (jax.nn.silu(xb @ w1[e]) * (xb @ w3[e])) @ w2[e]

    yb = lax.map(expert_rows, (xs, blk_exp)).reshape(n_rows, d)
    out = jnp.zeros((t, d), h.dtype).at[row_tok].add(yb * row_w[:, None])
    return out.reshape(bsz, s, d)

def _layer(x, norm_mix, w_in, conv_a, a_log, dt_bias, a_norm, w_gk2, b_gk, b_norm,
           w_oa, w_ob, w_out, norm_ffn, w_rg, b_rg, w_re, b_re, w1, w3, w2):
    bsz, s, _ = x.shape
    h = _rmsnorm(x, norm_mix)
    z = h @ w_in
    aq, ak, av, az, abeta, aalpha, bq, bk, bv, bg, blr, mix_a, mix_b = _split_cols(z)

    qkv = jax.nn.silu(_causal_depthwise_conv(jnp.concatenate([aq, ak, av], axis=-1), conv_a))
    aq, ak, av = jnp.split(qkv, [A_QK, 2 * A_QK], axis=-1)
    beta = jax.nn.sigmoid(abeta.astype(jnp.float32)).transpose(0, 2, 1)
    g = (-jnp.exp(a_log.astype(jnp.float32))
         * jax.nn.softplus(aalpha.astype(jnp.float32) + dt_bias.astype(jnp.float32))).transpose(0, 2, 1)
    oa = _gated_delta_rule(_l2norm(_heads(aq, A_HEADS)), _l2norm(_heads(ak, A_HEADS)),
                           _heads(av, A_HEADS), beta, g).astype(x.dtype)
    oa = _rmsnorm(oa.transpose(0, 2, 1, 3), a_norm) * jax.nn.silu(az.reshape(bsz, s, A_HEADS, A_DV))
    ya = oa.reshape(bsz, s, A_V) @ w_oa

    gk = jax.nn.log_sigmoid((blr @ w_gk2 + b_gk).astype(jnp.float32)) / B_GATE_NORM
    ob = _gla_chunked(_heads(bq, B_HEADS), _heads(bk, B_HEADS), _heads(bv, B_HEADS),
                      _heads(gk, B_HEADS)).astype(x.dtype)
    ob = _rmsnorm(ob.transpose(0, 2, 1, 3), b_norm) * jax.nn.silu(bg.reshape(bsz, s, B_HEADS, B_DV))
    yb = ob.reshape(bsz, s, B_V) @ w_ob

    x = x + (jax.nn.sigmoid(mix_a) * ya + jax.nn.sigmoid(mix_b) * yb) @ w_out
    x = x + _hier_moe(_rmsnorm(x, norm_ffn), w_rg, b_rg, w_re, b_re, w1, w3, w2)
    return x

def setup_inputs(seed: int = 0) -> dict:
    key = jax.random.key(seed)
    ks = jax.random.split(key, 24)
    L, D = DEPTH, D_MODEL
    nrm = jax.random.normal
    dt = jnp.exp(jax.random.uniform(ks[4], (L, A_HEADS)) * (jnp.log(0.1) - jnp.log(0.001)) + jnp.log(0.001))
    return {
        "x": nrm(ks[0], (BATCH, SEQ, D), jnp.float32),
        "norm_mix": 1.0 + 0.01 * nrm(ks[1], (L, D)),
        "w_in": nrm(ks[2], (L, D, IN_COLS)) * D ** -0.5,
        "conv_a": nrm(ks[3], (L, A_CONV, 2 * A_QK + A_V)) * A_CONV ** -0.5,
        "a_log": jnp.log(jax.random.uniform(ks[5], (L, A_HEADS), minval=1.0, maxval=16.0)),
        "dt_bias": dt + jnp.log(-jnp.expm1(-dt)),
        "a_norm": 1.0 + 0.01 * nrm(ks[6], (L, A_DV)),
        "w_gk2": nrm(ks[7], (L, B_GATE_RANK, B_QK)) * B_GATE_RANK ** -0.5,
        "b_gk": 0.1 * nrm(ks[8], (L, B_QK)),
        "b_norm": 1.0 + 0.01 * nrm(ks[9], (L, B_DV)),
        "w_oa": nrm(ks[10], (L, A_V, D)) * A_V ** -0.5,
        "w_ob": nrm(ks[11], (L, B_V, D)) * B_V ** -0.5,
        "w_out": nrm(ks[12], (L, D, D)) * D ** -0.5,
        "norm_ffn": 1.0 + 0.01 * nrm(ks[13], (L, D)),
        "w_rg": nrm(ks[14], (L, D, N_GROUPS)) * D ** -0.5,
        "b_rg": 0.01 * nrm(ks[15], (L, N_GROUPS)),
        "w_re": nrm(ks[16], (L, D, N_GROUPS, EXP_PER_GROUP)) * D ** -0.5,
        "b_re": 0.01 * nrm(ks[17], (L, N_GROUPS, EXP_PER_GROUP)),
        "w1": nrm(ks[18], (L, N_EXPERTS, D, D_FF_EXPERT)) * D ** -0.5,
        "w3": nrm(ks[19], (L, N_EXPERTS, D, D_FF_EXPERT)) * D ** -0.5,
        "w2": nrm(ks[20], (L, N_EXPERTS, D_FF_EXPERT, D)) * D_FF_EXPERT ** -0.5,
        "norm_final": 1.0 + 0.01 * nrm(ks[21], (D,)),
    }

def reference(x, norm_mix, w_in, conv_a, a_log, dt_bias, a_norm, w_gk2, b_gk, b_norm,
              w_oa, w_ob, w_out, norm_ffn, w_rg, b_rg, w_re, b_re, w1, w3, w2, norm_final):
    for l in range(DEPTH):
        x = _layer(x, norm_mix[l], w_in[l], conv_a[l], a_log[l], dt_bias[l], a_norm[l], w_gk2[l],
                   b_gk[l], b_norm[l], w_oa[l], w_ob[l], w_out[l], norm_ffn[l], w_rg[l], b_rg[l],
                   w_re[l], b_re[l], w1[l], w3[l], w2[l])
    return _rmsnorm(x, norm_final)


_drawn_inputs = setup_inputs


def setup_inputs(seed=0):
    import zlib

    import numpy as np

    out = dict(_drawn_inputs(seed))
    spreads = {}
    factors = {'norm_mix': 3.005,
     'a_norm': 8.0,
     'b_norm': 4.419,
     'norm_ffn': 3.853,
     'b_rg': 64.0,
     'b_re': 39.336,
     'norm_final': 30.522}
    for name, (base, spread) in spreads.items():
        noise = np.random.default_rng([zlib.crc32(name.encode()), seed]).standard_normal(out[name].shape)
        drawn = base * np.exp(spread * noise) if base else spread * noise
        out[name] = __import__('jax').numpy.asarray(drawn.astype(out[name].dtype))
    for name, factor in factors.items():
        out[name] = (out[name] * factor).astype(out[name].dtype)
    return out
```

```python
from contextlib import ExitStack

import concourse.bass as bass
from concourse import mybir

F32 = mybir.dt.float32
I32 = mybir.dt.int32
ALU = mybir.AluOpType
ACT = mybir.ActivationFunctionType
AX = mybir.AxisListType

P = 128
D = 2048
SEQ = 256
NM = SEQ // P
KT = D // P
CB = 512
NC = D // CB
HT = KT // 2
SLOT = HT * CB
EPS = 1e-6
A_HEADS, A_D, TAPS = 8, 128, 4
B_HEADS, B_DK, B_DV, RANK = 4, 128, 256, 16
GATE_NORM = 16.0
GH = 4
NG = A_HEADS // GH
GU = GH * NM
QSCALE = float(A_D) ** -0.5
AQ = A_HEADS * A_D
BQK, BV = B_HEADS * B_DK, B_HEADS * B_DV
C_AQ, C_AK, C_AV, C_AZ = 0, AQ, 2 * AQ, 3 * AQ
C_BETA = 4 * AQ
C_BQ = C_BETA + 2 * A_HEADS
C_BK = C_BQ + BQK
C_BV = C_BK + BQK
C_BG = C_BV + BV
C_LR = C_BG + BV
C_MA = C_LR + RANK
C_MB = C_MA + D
NSM = 2 * A_HEADS + RANK
LEVELS = [1 << i for i in range(7)]
GROUPS, EPG = 4, 8
NE = GROUPS * EPG
FF = 512
FT = FF // P
CAP = 64
PAIRS = NE // 2
NEG = -3.0e38
SMALL = 16 * 12

BLOCKS = ([("gla", i, C_BQ + CB * i) for i in range(6)]
          + [("gdn0", i, c) for i, c in enumerate((C_AQ, C_AK, C_AV, C_AZ))]
          + [("gdn1", i, c + CB) for i, c in enumerate((C_AQ, C_AK, C_AV, C_AZ))]
          + [("gate", i, C_MA + CB * i) for i in range(NC)])
RING_A = 4
RING_M = 6
PER_PAIR = 12

GLA_STEPS = (["small", "cw", "blrT", "gc", "gkT", "bqT", "bkT", "lv_eye"]
             + [f"lv{b}" for b in LEVELS] + ["kd", "bS", "bo0", "bo1", "obT0", "obT1"])
GDN_STEPS = (["zqT", "zkT", "zvT", "gcb", "ssq", "ktok", "vtok", "khT", "A", "PT", "Y1"]
             + [f"{w}{b}" for b in LEVELS[1:-1] for w in ("Y", "dU", "dT")]
             + ["Y64", "dU64", "wT", "u0", "S", "v1", "oi", "o", "oaT"])
STEPS = GLA_STEPS + [f"{s}.{g}" for g in range(NG) for s in GDN_STEPS]
QUARTERS = 4
FIRST_BLOCKS = 6


def fillers():
    spans = [("blrT", "obT1", 4), ("zqT.0", "oaT.0", 4), ("zqT.1", "oaT.1", 4)]
    out = {s: [] for s in STEPS}
    q = FIRST_BLOCKS * QUARTERS
    for a, b, blocks in spans:
        names = STEPS[STEPS.index(a):STEPS.index(b) + 1]
        n, done = blocks * QUARTERS, 0
        for i, s in enumerate(names):
            upto = n * (i + 1) // len(names)
            out[s] += list(range(q + done, q + upto))
            done = upto
        q += n
    assert q == len(BLOCKS) * QUARTERS
    return out


FILL = fillers()


def build(nc, x, norm_mix, w_in, conv_a, a_log, dt_bias, a_norm, w_gk2, b_gk, b_norm, w_oa, w_ob, w_out,
          norm_ffn, w_rg, b_rg, w_re, b_re, w1, w3, w2, norm_final, y):
    x_v = x[0].rearrange("(m p) d -> p m d", p=P)
    y_v = y[0].rearrange("(m p) d -> p m d", p=P)
    win_v = w_in[0].rearrange("(p k) n -> p k n", k=KT)
    wout_v = w_out[0].rearrange("(p k) n -> p k n", k=KT)
    woa_v = w_oa[0].rearrange("(k p) n -> p k n", p=P)
    wob_v = w_ob[0].rearrange("(k p) n -> p k n", p=P)
    w1_v = w1[0].rearrange("e (p k) f -> e p (k f)", k=KT)
    w3_v = w3[0].rearrange("e (p k) f -> e p (k f)", k=KT)
    w2_v = w2[0].rearrange("e (p t) n -> e p t n", t=FT)

    with ExitStack() as ctx:
        block_of = {}

        def sem(name):
            if name not in block_of:
                block_of[name] = ctx.enter_context(nc.semaphore(name))
            return block_of[name]

        FREE = 53200
        arena = ctx.enter_context(nc.sbuf_tensor("arena", [P, FREE], F32))
        rounds_i = ctx.enter_context(nc.sbuf_tensor("rounds_i", [P, 1], I32))

        def cut(at, size):
            return arena[:, at:at + size], at + size

        hT, at = cut(0, KT * SEQ)
        hT = hT.rearrange("p (k t) -> p k t", k=KT)
        OAB = at
        oaT, at = cut(at, A_HEADS * SEQ)
        obT, at = cut(at, A_HEADS * SEQ)
        oaT = oaT.rearrange("p (k t) -> p k t", k=A_HEADS)
        obT = obT.rearrange("p (k t) -> p k t", k=A_HEADS)
        RA = at
        ringA, at = cut(at, RING_A * SLOT)
        ringA = ringA.rearrange("p (s k n) -> p s k n", s=RING_A, k=HT)
        RM = at
        ringM, at = cut(at, RING_M * SLOT)
        ringM = ringM.rearrange("p (s n) -> p s n", s=RING_M)
        consts = at
        x1 = arena[:, OAB:OAB + NM * D].rearrange("p (m d) -> p m d", m=NM)

        at = consts
        ident, at = cut(at, P)
        upT, at = cut(at, P)
        ones, at = cut(at, P)
        iota, at = cut(at, CAP)
        low = {}
        upp = {}
        for b in LEVELS:
            low[b], at = cut(at, P)
        for b in LEVELS:
            upp[b], at = cut(at, P)
        wsm, at = cut(at, KT * (GROUPS + NE))
        cw, at = cut(at, 3 * A_HEADS * TAPS)
        zs, at = cut(at, NM * NSM)
        nmix, at = cut(at, KT)
        nffn, at = cut(at, KT)
        anorm, at = cut(at, 1)
        bnorm, at = cut(at, 2)
        bgk, at = cut(at, B_HEADS)
        alog, at = cut(at, A_HEADS)
        dtb, at = cut(at, A_HEADS)
        half16 = NM * A_HEADS
        beta, at = cut(at, half16)
        gdec, at = cut(at, half16)
        xa, at = cut(at, half16)
        na, at = cut(at, half16)
        gcol, at = cut(at, half16)
        gdif, at = cut(at, half16)
        eg, at = cut(at, half16)
        ekd, at = cut(at, half16)
        bhalf, at = cut(at, half16)
        beg, at = cut(at, half16)
        ss1, at = cut(at, NM)
        rstd, at = cut(at, NM)
        rstdh, at = cut(at, NM)
        ssqk, at = cut(at, 16)
        rqk, at = cut(at, 16)
        rms, at = cut(at, 16)
        rmf, at = cut(at, 16)
        pw, at = cut(at, 16)
        ss2, at = cut(at, NM)
        rstd2, at = cut(at, NM)
        brg, at = cut(at, GROUPS)
        bre, at = cut(at, NE)
        assert at <= FREE, at
        zs3 = zs.rearrange("p (m c) -> p m c", m=NM)

        def mh(t):
            return t.rearrange("p (m h) -> p m h", m=NM)

        at = RM
        Z1, at = cut(at, 6 * NM * CB)
        TEMPS = at
        Z0, _ = cut(RM + 5 * SLOT, 4 * NM * CB)
        LAST = RM + 5 * SLOT
        xs0 = Z0.rearrange("p (m d) -> p m d", m=NM)
        gateA = xs0
        at = TEMPS
        (bqT, at), (bkT, at), (bT, at), (bE, at) = cut(at, 1024), (0, 0), (0, 0), (0, 0)
        at = TEMPS
        names = {}

        def temps(base, sizes):
            at = base
            for n, s in sizes:
                names[n], at = cut(at, s)
            assert at <= LAST, (at, LAST)

        temps(TEMPS, [("bqT", 1024), ("bkT", 1024), ("bT", 1024), ("bE", 1024), ("attn", 1024), ("btmp", 1024),
                      ("kdT", 512), ("kdtok", 512), ("bS", 1024), ("bo", 2048), ("bth", 2048), ("wgk2", 512),
                      ("blrT", 256)])
        zpad = GH * (SEQ + TAPS - 1)
        temps(TEMPS, [("zT0", zpad), ("zT1", zpad), ("zT2", zpad), ("kbg", 1024), ("kdec", 512), ("nwT", 512),
                      ("aS", 512), ("gB", 1024), ("Dm", 1024), ("DT", 1024), ("L1", 1024), ("U", 1024), ("T", 1024),
                      ("Y", 1024), ("inter", 512)])
        convw = arena[0:TAPS, TEMPS:TEMPS + 3 * AQ]
        T_ = names

        def zsl(which, i):
            base = {"gla": Z1, "gdn0": Z0, "gdn1": Z1, "gate": Z0}[which]
            if which == "gate":
                return gateA[:, :, i * CB:(i + 1) * CB]
            return base[:, i * NM * CB:(i + 1) * NM * CB].rearrange("p (m n) -> p m n", m=NM)

        at = RA
        h2, at = cut(at, NM * D)
        h2 = h2.rearrange("p (m d) -> p m d", m=NM)
        xeT, at = cut(at, KT * P)
        xeT = xeT.rearrange("p (k s) -> p k s", k=KT)
        Ysb, at = cut(at, D)
        aT, at = cut(at, FT * P)
        hid, at = cut(at, FF)
        hth, at = cut(at, FF)
        hs, at = cut(at, FF)
        comb, at = cut(at, SEQ)
        sel, at = cut(at, NM * P)
        selg, at = cut(at, NM * P)
        nfin, at = cut(at, D)
        junk, at = cut(at, D)
        pos, at = cut(at, NM * NE)
        Wt, at = cut(at, NM * NE)
        Mt, at = cut(at, NM * NE)
        rt = {}
        for n, s in [("lg", 8), ("le", 64), ("gm", 2), ("d", 8), ("ed", 8), ("den", 2), ("pt", 2), ("eq", 16),
                     ("cum", 16), ("fg", 8), ("pr", 64), ("ls", 16), ("m1", 2), ("d1", 16), ("f1", 16), ("ls2", 16),
                     ("m2", 2), ("d2", 16), ("f2", 16), ("dm", 2), ("e2", 2), ("s2", 2), ("r2", 2), ("w1", 2),
                     ("w2", 2), ("fs", 16), ("ws", 16), ("wa", 16), ("mx", 1), ("c1", 1), ("c2", 1), ("c3", 1),
                     ("rf", 1)]:
            rt[n], at = cut(at, s)
        assert at <= RM, (at, RM)
        tb = arena[:, TEMPS:TEMPS + NM * CB].rearrange("p (m n) -> p m n", m=NM)
        tyb = arena[:, TEMPS + 1024:TEMPS + 2048].rearrange("p (m n) -> p m n", m=NM)

        psum = ctx.enter_context(nc.psum_tensor("psum", [P, 8 * CB], F32))

        def bank(i, n=CB):
            return psum[:, i * CB:i * CB + n]

        def pair(step):
            return psum[:, (4 + 2 * (STEPS.index(step) % 2)) * CB:(4 + 2 * (STEPS.index(step) % 2)) * CB + 2 * CB]

        def drained(step):
            base, _, g = step.partition(".")
            g = int(g or 0)
            if base[0] == "Y" and base != "Y1":
                return "Y", g * 6 + LEVELS.index(int(base[1:]))
            if base in ("Y1",) or base[:2] == "dU":
                return "U", g * 7 + (1 if base == "Y1" else LEVELS.index(int(base[2:])) + 1)
            if base[:2] == "dT":
                return "T", g * 6 + LEVELS.index(int(base[2:])) + 1
            if base[:2] == "lv":
                return "attn_tmp", (1 if base == "lv_eye" else LEVELS.index(int(base[2:])) + 2)
            alias = {"small": "zs", "o": "a_o", "bo0": "b_o", "bo1": "b_o", "obT0": "obT", "obT1": "obT",
                     "ssq": "ssqk", "S": "a_S", "kd": "kdtok", "gc": "gcol", "oi": "inter", "gkT": "gkx"}
            n = {"bo1": 2, "obT1": 2}.get(base, 1)
            return alias.get(base, base), g + n

        def full(step):
            i = STEPS.index(step)
            return f"pair{i % 2}_full", i // 2 + 1

        def wait(eng, what):
            eng.wait_ge(sem(what[0]), what[1])

        U3 = "p (u t) -> p u t"

        def units(t, u=GU):
            return t.rearrange(U3, u=u)

        block = ctx.enter_context(nc.Block())
        NSL_A = 2 * len(BLOCKS)
        PER_C = 4
        NSL_MERGE = NSL_A + PER_C * NC
        SLOTS_A = NSL_MERGE + 2 * NC

        @block.sync
        def _(sp):
            sp.dma_start(xs0[:, 0, :], x_v[:, 0, :]).then_inc(sem("x_in0"), 16)
            sp.dma_start(xs0[:, 1, :], x_v[:, 1, :]).then_inc(sem("x_in1"), 16)

            def load(s, dst, src):
                if s >= RING_A:
                    sp.wait_ge(sem("slotA_free"), s - RING_A + 1)
                sp.dma_start(dst, src).then_inc(sem(f"slotA{s % RING_A}"), 16)

            s = 0
            for _, _, c in BLOCKS:
                for h in range(2):
                    load(s, ringA[:, s % RING_A], win_v[:, h * HT:(h + 1) * HT, c:c + CB])
                    s += 1
            for c in range(NC):
                for h in range(2):
                    load(s, ringA[:, s % RING_A], win_v[:, h * HT:(h + 1) * HT, C_MB + c * CB:C_MB + (c + 1) * CB])
                    s += 1
                for v in (woa_v, wob_v):
                    load(s, ringA[:, s % RING_A], v[:, :, c * CB:(c + 1) * CB])
                    s += 1
            for c in range(NC):
                if c == 2:
                    wait(sp, ("merged", NC))
                    for m in range(NM):
                        sp.dma_start(x1[:, m, :], x_v[:, m, :]).then_inc(sem("x_back"), 16)
                for h in range(2):
                    load(s, ringA[:, s % RING_A], wout_v[:, h * HT:(h + 1) * HT, c * CB:(c + 1) * CB])
                    s += 1
            assert s == SLOTS_A
            wait(sp, ("mT", 8))
            sp.sem_inc(sem("slotM_free"), RING_M)
            wait(sp, ("rounds_ready", 1))
            rounds = sp.value_load(rounds_i[0:1, 0:1], min_val=1, max_val=SEQ // CAP)
            with sp.Fori(0, rounds) as r:
                with sp.Fori(0, PAIRS) as p:
                    n = r * PAIRS + p
                    j = 0
                    for v in (w1_v, w3_v):
                        for h in range(2):
                            for e in range(2):
                                sp.wait_ge(sem("slotM_free"), n * PER_PAIR + j + 1)
                                sp.dma_start(ringM[:, j % RING_M, :],
                                             v[bass.ds(p * 2 + e, 1), :, h * SLOT:(h + 1) * SLOT]
                                             .rearrange("a p n -> (a p) n")).then_inc(sem(f"slotM{j % RING_M}"), 16)
                                j += 1
                    for h in range(2):
                        for e in range(2):
                            sp.wait_ge(sem("slotM_free"), n * PER_PAIR + j + 1)
                            sp.dma_start(ringM[:, j % RING_M, :].rearrange("p (t n) -> p t n", t=FT),
                                         w2_v[bass.ds(p * 2 + e, 1), :, :, h * (D // 2):(h + 1) * (D // 2)]
                                         .rearrange("a p t n -> (a p) t n")).then_inc(sem(f"slotM{j % RING_M}"), 16)
                            j += 1
            wait(sp, ("y_ready", 2))
            sp.dma_start(y_v, x1[:, :, :]).then_inc(sem("y_out"), 16)
            sp.wait_ge(sem("y_out"), 16)

        @block.gpsimd
        def _(pool):
            def small(dst, src, name):
                pool.dma_start(dst, src, allow_slow_non_contiguous=True).then_inc(sem(name), 16)

            small(nmix, norm_mix[0].rearrange("(p k) -> p k", k=KT), "nmix_in")
            w3d = wsm[:, 0:KT * NSM].rearrange("p (k c) -> p k c", k=KT)
            small(w3d[:, :, 0:2 * A_HEADS], win_v[:, :, C_BETA:C_BETA + 2 * A_HEADS], "small_in")
            small(w3d[:, :, 2 * A_HEADS:NSM], win_v[:, :, C_LR:C_LR + RANK], "small_in")
            small(convw, conv_a[0], "small_in")
            small(T_["wgk2"][0:RANK, :], w_gk2[0], "small_in")
            small(dtb, dt_bias[0].partition_broadcast(P), "small_in")
            small(alog, a_log[0].partition_broadcast(P), "small_in")
            small(bgk, b_gk[0].rearrange("(h p) -> p h", p=P), "small_in")
            small(anorm, a_norm[0].rearrange("(p a) -> p a", a=1), "small_in")
            small(bnorm, b_norm[0].rearrange("(h p) -> p h", p=P), "small_in")
            small(nffn, norm_ffn[0].rearrange("(p k) -> p k", k=KT), "small_in")
            small(brg, b_rg[0].partition_broadcast(P), "small_in")
            small(bre, b_re[0].rearrange("g e -> (g e)").partition_broadcast(P), "small_in")

            links = [0]

            def link(ins):
                links[0] += 1
                ins.then_inc(sem("pool_link"), 1)
                pool.wait_ge(sem("pool_link"), links[0])

            nc.gpsimd.memset(ident, 0.0)
            nc.gpsimd.memset(ones, 1.0)
            nc.gpsimd.memset(pw, -0.5)
            link(nc.gpsimd.memset(upT, 1.0))
            nc.gpsimd.affine_select(out=ident, in_=ident, compare_op=ALU.not_equal, fill=1.0, base=0,
                                    pattern=[[-1, P]], channel_multiplier=1).then_inc(sem("ident"), 1)
            link(nc.gpsimd.affine_select(out=upT, in_=upT, compare_op=ALU.is_ge, fill=0.0, base=0,
                                         pattern=[[1, P]], channel_multiplier=-1))
            for b in LEVELS:
                nc.gpsimd.memset(low[b], 1.0)
                link(nc.gpsimd.memset(upp[b], 1.0))
                mb = P // (2 * b)

                def cut_mask(t, base, pat, cm):
                    v = t.rearrange("p (m s r) -> p m s r", s=2, r=b)
                    return nc.gpsimd.affine_select(out=v, in_=v, compare_op=ALU.is_ge, fill=0.0, base=base,
                                                   pattern=pat, channel_multiplier=cm)

                cut_mask(low[b], -b, [[-2 * b, mb], [-1000, 2], [0, b]], 1)
                link(cut_mask(upp[b], -1000, [[-2 * b, mb], [1000, 2], [0, b]], 1))
                cut_mask(low[b], 2 * b - 1, [[2 * b, mb], [0, 2], [0, b]], -1)
                link(cut_mask(upp[b], b - 1, [[2 * b, mb], [0, 2], [0, b]], -1))
            nc.gpsimd.iota(iota, pattern=[[1, CAP]], base=0, channel_multiplier=0,
                           allow_small_or_imprecise_dtypes=True).then_inc(sem("consts"), 1)

            wait(pool, ("ss1", 2))
            link(nc.gpsimd.tensor_scalar(ss1, ss1, 1.0 / D, EPS, ALU.mult, ALU.add))
            link(nc.gpsimd.tensor_tensor(rstd, ss1, pw[:, 0:NM], ALU.pow))
            nc.gpsimd.tensor_scalar(rstdh, rstd, 0.5, None, ALU.mult).then_inc(sem("rstd"), 1)

            wait(pool, ("b_ms", 1))
            nc.gpsimd.tensor_tensor(rmf[:, 0:8], rms[:, 0:8], pw[:, 0:8], ALU.pow).then_inc(sem("b_rf"), 1)

            for g in range(NG):
                if g == 0:
                    wait(pool, ("obT", 2))
                    wait(pool, ("gdec", 1))
                else:
                    wait(pool, ("oaT", g))
                for h in range(GH):
                    for n in range(NM):
                        u = h * NM + n
                        i = nc.gpsimd.tensor_scalar(T_["gB"][:, u * P:(u + 1) * P], ones,
                                                    mh(gdec)[:, n, g * GH + h:g * GH + h + 1], None, ALU.mult)
                i.then_inc(sem("gB"), 1)
                wait(pool, ("expD", g + 1))
                Dm = units(T_["Dm"])
                bv = mh(beta)[:, :, g * GH:(g + 1) * GH].rearrange("p n h -> p h n").unsqueeze(3)\
                    .to_broadcast([P, GH, NM, P])
                nc.gpsimd.tensor_tensor(T_["Dm"].rearrange("p (h n t) -> p h n t", h=GH, n=NM),
                                        T_["Dm"].rearrange("p (h n t) -> p h n t", h=GH, n=NM), bv,
                                        ALU.mult).then_inc(sem("DA"), 1)
                wait(pool, ("expDT", g + 1))
                nc.gpsimd.tensor_tensor(units(T_["DT"]), units(T_["DT"]),
                                        upT.unsqueeze(1).to_broadcast([P, GU, P]), ALU.mult)\
                    .then_inc(sem("DTm"), 1)
                wait(pool, ("ssqk", g + 1))
                nc.gpsimd.tensor_tensor(rqk, ssqk, pw, ALU.pow).then_inc(sem("rqk"), 1)
                wait(pool, ("ktok", g + 1))
                k4 = T_["zT0"][:, 0:1024].rearrange("p (h n t) -> p h n t", h=GH, n=NM)
                nc.gpsimd.tensor_tensor(T_["kbg"].rearrange("p (h n t) -> p h n t", h=GH, n=NM), k4,
                                        mh(beg)[:, :, g * GH:(g + 1) * GH].rearrange("p n h -> p h n")
                                        .unsqueeze(3).to_broadcast([P, GH, NM, P]), ALU.mult).then_inc(sem("kbg"), 1)
                nc.gpsimd.tensor_tensor(units(T_["kdec"], GH), k4[:, :, 0, :],
                                        mh(ekd)[:, 0, g * GH:(g + 1) * GH].unsqueeze(2).to_broadcast([P, GH, P]),
                                        ALU.mult).then_inc(sem("kdec"), 1)
                wait(pool, ("A", g + 1))
                wait(pool, full(f"gcb.{g}"))
                for i, b in enumerate(LEVELS):
                    if i >= 2:
                        wait(pool, full(f"Y{LEVELS[i - 2]}.{g}"))
                        if i == 2:
                            wait(pool, ("T", g * 6 + 1))
                    dst = T_["gB"] if i % 2 == 0 else T_["L1"]
                    nc.gpsimd.tensor_tensor(units(dst), units(T_["Dm"]),
                                            low[b].unsqueeze(1).to_broadcast([P, GU, P]), ALU.mult)\
                        .then_inc(sem("L"), 1)
                wait(pool, ("a_ms", g + 1))
                link(nc.gpsimd.tensor_scalar(rqk[:, 0:8], rqk[:, 0:8], QSCALE, None, ALU.mult))
                link(nc.gpsimd.tensor_tensor(rms[:, 0:8], rms[:, 0:8], rqk[:, 0:8], ALU.mult))
                link(nc.gpsimd.tensor_tensor(rms[:, 0:8], rms[:, 0:8], rqk[:, 0:8], ALU.mult))
                link(nc.gpsimd.tensor_scalar(rms[:, 0:8], rms[:, 0:8], 1.0 / A_D, EPS, ALU.mult, ALU.add))
                link(nc.gpsimd.tensor_tensor(rmf[:, 0:8], rms[:, 0:8], pw[:, 0:8], ALU.pow))
                nc.gpsimd.tensor_tensor(rmf[:, 0:8], rmf[:, 0:8], rqk[:, 0:8], ALU.mult).then_inc(sem("a_rf"), 1)

            wait(pool, ("zs", 1))
            wr = wsm.rearrange("p (k c) -> p k c", k=KT)
            small(wr[:, :, 0:GROUPS], w_rg[0].rearrange("(p k) g -> p k g", k=KT), "wr_in")
            small(wr[:, :, GROUPS:GROUPS + NE], w_re[0].rearrange("(p k) g e -> p k (g e)", k=KT), "wr_in")
            wait(pool, ("x1", 2 * NC))
            small(nfin, norm_final.partition_broadcast(P), "nfin_in")
            wait(pool, ("ss2", 2))
            link(nc.gpsimd.tensor_scalar(ss2, ss2, 1.0 / D, EPS, ALU.mult, ALU.add))
            nc.gpsimd.tensor_tensor(rstd2, ss2, pw[:, 0:NM], ALU.pow).then_inc(sem("rstd2"), 1)

            wait(pool, ("rounds_ready", 1))
            rounds = pool.value_load(rounds_i[0:1, 0:1], min_val=1, max_val=SEQ // CAP)
            s4 = sel.rearrange("p (m e s) -> p m e s", m=NM, e=2)
            g4 = selg.rearrange("p (m e s) -> p m e s", m=NM, e=2)
            io = iota.unsqueeze(1).to_broadcast([P, 2, CAP])
            with pool.Fori(0, rounds) as r:
                with pool.Fori(0, PAIRS) as p:
                    n = r * PAIRS + p
                    pool.wait_ge(sem("combT"), n + 1)
                    for m in range(NM):
                        i = nc.gpsimd.tensor_tensor(
                            s4[:, m], io, pos[:, bass.ds(m * NE + 2 * p, 2)].unsqueeze(2).to_broadcast([P, 2, CAP]),
                            ALU.subtract)
                    pool.drain()
                    nc.gpsimd.tensor_scalar(sel, sel, 0.0, None, ALU.is_equal).then_inc(sem("sel"), 1)
                    pool.wait_ge(sem("sel"), n + 1)
                    for m in range(NM):
                        i = nc.gpsimd.tensor_tensor(
                            g4[:, m], s4[:, m],
                            Wt[:, bass.ds(m * NE + 2 * p, 2)].unsqueeze(2).to_broadcast([P, 2, CAP]), ALU.mult)
                    i.then_inc(sem("selg"), 1)
                pool.drain()
                nc.gpsimd.tensor_scalar(pos, pos, float(-CAP), None, ALU.add)
                pool.drain()
            wait(pool, ("ss3", 2))
            link(nc.gpsimd.tensor_scalar(ss2, ss2, 1.0 / D, EPS, ALU.mult, ALU.add))
            nc.gpsimd.tensor_tensor(rstd2, ss2, pw[:, 0:NM], ALU.pow).then_inc(sem("rstd3"), 1)

        @block.scalar
        def _(act):
            def evac(q):
                b, part = divmod(q, QUARTERS)
                if part != QUARTERS - 1:
                    return
                which, i, _ = BLOCKS[b]
                act.wait_ge(sem("slotA_free"), 2 * (b + 1))
                if b == 0:
                    wait(act, ("rstd", 1))
                if which == "gdn0" and i == 0:
                    wait(act, ("ss1", 2))
                if which == "gdn1" and i == 0:
                    wait(act, ("obT", 2))
                if which == "gate" and i == 0:
                    wait(act, ("oaT", 1))
                dst = zsl(which, i)
                for m in range(NM):
                    if which == "gate":
                        j = nc.scalar.activation(dst[:, m, :], bank(2 * (b % 2) + m), ACT.Tanh,
                                                 scale=rstdh[:, m:m + 1])
                    else:
                        j = nc.scalar.activation(dst[:, m, :], bank(2 * (b % 2) + m), ACT.Copy,
                                                 scale=rstd[:, m:m + 1])
                j.then_inc(sem("z"), 1)

            def after(step):
                for q in FILL[step]:
                    evac(q)

            for m in range(NM):
                act.wait_ge(sem(f"x_in{m}"), 16)
                nc.scalar.activation(Z1[:, m * D:(m + 1) * D], xs0[:, m, :], ACT.Square,
                                     accum_out=ss1[:, m:m + 1]).then_inc(sem("ss1"), 1)
            act.wait_ge(sem("small_in"), SMALL)
            for q in range(FIRST_BLOCKS * QUARTERS):
                evac(q)
            wait(act, full("small"))
            zp = pair("small")[:, 0:NM * NSM].rearrange("p (m c) -> p m c", m=NM)
            for m in range(NM):
                i = nc.scalar.activation(zs3[:, m, :], zp[:, m, :], ACT.Copy, scale=rstd[:, m:m + 1])
            i.then_inc(sem("zs"), 1)
            after("small")
            after("cw")
            act.wait_ge(sem("zs"), 1)
            nc.scalar.activation(mh(beta), zs3[:, :, 0:A_HEADS], ACT.Tanh, scale=0.5).then_inc(sem("tbeta"), 1)
            wait(act, full("blrT"))
            nc.scalar.activation(T_["blrT"][0:RANK, :], pair("blrT")[0:RANK, 0:SEQ], ACT.Copy)\
                .then_inc(sem("blrT"), 1)
            after("blrT")
            wait(act, ("na", 1))
            nc.scalar.activation(na, na, ACT.Exp).then_inc(sem("ena"), 1)
            nc.scalar.activation(alog, alog, ACT.Exp).then_inc(sem("ealog"), 1)
            act.wait_ge(sem("ena"), 1)
            nc.scalar.activation(na, na, ACT.Ln, bias=1.0).then_inc(sem("lna"), 1)
            after("gc")
            wait(act, ("gcol", 1))
            nc.scalar.activation(eg, gcol, ACT.Exp).then_inc(sem("eg"), 1)
            nc.scalar.activation(ekd, gdif, ACT.Exp).then_inc(sem("ekd"), 1)
            after("gkT")
            wait(act, ("gkn", 1))
            nc.scalar.activation(T_["bE"], T_["bE"], ACT.Exp).then_inc(sem("gke"), 1)
            act.wait_ge(sem("gke"), 1)
            nc.scalar.activation(T_["bE"], T_["bE"], ACT.Ln, bias=1.0).then_inc(sem("gkl"), 1)
            wait(act, full("bqT"))
            nc.scalar.activation(T_["bqT"], pair("bqT"), ACT.Copy, scale=QSCALE).then_inc(sem("bqT"), 1)
            after("bqT")
            after("bkT")
            after("lv_eye")
            for i, b in enumerate(LEVELS):
                wait(act, ("bdist", i + 1))
                nc.scalar.activation(T_["bE"], T_["bE"], ACT.Exp, scale=1.0 / GATE_NORM).then_inc(sem("bE"), 1)
                after(f"lv{b}")
            wait(act, ("bedge", 1))
            nc.scalar.activation(T_["bE"], T_["bE"], ACT.Exp, scale=1.0 / GATE_NORM).then_inc(sem("bE"), 1)
            wait(act, full("kd"))
            nc.scalar.activation(T_["kdtok"], pair("kd")[:, 0:512], ACT.Copy).then_inc(sem("kdtok"), 1)
            after("kd")
            wait(act, full("bS"))
            nc.scalar.activation(T_["bS"], pair("bS"), ACT.Copy).then_inc(sem("bS"), 1)
            after("bS")
            bg = Z1[:, 4 * 1024:6 * 1024]
            nc.scalar.activation(T_["bth"], bg, ACT.Tanh, scale=0.5).then_inc(sem("bth"), 1)
            for i in range(2):
                wait(act, full(f"bo{i}"))
                nc.scalar.activation(T_["bo"][:, i * 1024:(i + 1) * 1024], pair(f"bo{i}"), ACT.Copy)\
                    .then_inc(sem("b_o"), 1)
                after(f"bo{i}")
            act.wait_ge(sem("b_o"), 2)
            wait(act, ("edge", 1))
            nc.scalar.activation(T_["bqT"], T_["bo"][:, 0:1024], ACT.Square)
            nc.scalar.activation(T_["bkT"], T_["bo"][:, 1024:2048], ACT.Square).then_inc(sem("b_sq"), 1)
            after("obT0")
            after("obT1")

            for g in range(NG):
                s = f".{g}"
                zg = [T_[f"zT{i}"][:, 0:zpad].rearrange("p (h t) -> p h t", h=GH) for i in range(3)]
                Zb = Z0 if g == 0 else Z1
                c = [Zb[:, i * 1024:(i + 1) * 1024] for i in range(3)]
                for i, w in ((0, "zqT"), (2, "zvT")):
                    wait(act, full(w + s))
                    nc.scalar.activation(zg[i][:, :, TAPS - 1:], pair(w + s).rearrange("p (h t) -> p h t", h=GH),
                                         ACT.Copy).then_inc(sem(w), 1)
                    after(w + s)
                    if w == "zqT":
                        after("zkT" + s)
                after("gcb" + s)
                for i in range(3):
                    act.wait_ge(sem("conv"), 3 * g + i + 1)
                    nc.scalar.activation(T_[f"zT{i}"][:, 0:1024], c[i], ACT.Tanh, scale=0.5).then_inc(sem("tconv"), 1)
                wait(act, ("Dn", g + 1))
                nc.scalar.activation(T_["Dm"], T_["Dm"], ACT.Exp, scale=-1.0).then_inc(sem("expD"), 1)
                wait(act, ("DTn", g + 1))
                nc.scalar.activation(T_["DT"], T_["DT"], ACT.Exp).then_inc(sem("expDT"), 1)
                for i in range(2):
                    act.wait_ge(sem("silu"), 3 * g + i + 1)
                    nc.scalar.activation(T_[f"zT{i}"][:, 0:1024], c[i], ACT.Square).then_inc(sem("sq"), 1)
                after("ssq" + s)
                after("ktok" + s)
                after("vtok" + s)
                wait(act, full("khT" + s))
                nc.scalar.activation(T_["zT1"][:, 0:1024], pair("khT" + s), ACT.Copy).then_inc(sem("khT"), 1)
                for w in ("khT", "A", "PT", "Y1"):
                    after(w + s)
                for i, b in enumerate(LEVELS[1:]):
                    wait(act, full(f"Y{b}" + s))
                    nc.scalar.activation(T_["Y"], pair(f"Y{b}" + s), ACT.Copy).then_inc(sem("Y"), 1)
                    for w in ("Y", "dU", "dT"):
                        if w != "dT" or b != 64:
                            after(f"{w}{b}" + s)
                wait(act, full("wT" + s))
                nc.scalar.activation(T_["nwT"], pair("wT" + s)[:, 0:512], ACT.Copy, scale=-1.0)\
                    .then_inc(sem("wT"), 1)
                after("wT" + s)
                wait(act, full("u0" + s))
                vn = units(T_["T"])
                nc.scalar.activation(T_["T"][:, 0:512], pair("u0" + s)[:, 0:512], ACT.Copy).then_inc(sem("u0"), 1)
                after("u0" + s)
                wait(act, full("S" + s))
                nc.scalar.activation(T_["aS"], pair("S" + s)[:, 0:512], ACT.Copy).then_inc(sem("a_S"), 1)
                after("S" + s)
                wait(act, full("v1" + s))
                nc.scalar.activation(T_["T"][:, 512:1024], pair("v1" + s)[:, 0:512], ACT.Copy).then_inc(sem("v1"), 1)
                after("v1" + s)
                nc.scalar.activation(T_["L1"], Zb[:, 3 * 1024:4 * 1024], ACT.Tanh, scale=0.5).then_inc(sem("tz"), 1)
                after("oi" + s)
                after("o" + s)
                wait(act, ("a_o", g + 1))
                nc.scalar.activation(T_["zT1"][:, 0:1024], T_["Y"], ACT.Square).then_inc(sem("a_sq"), 1)
                after("oaT" + s)

            for c in range(NC):
                act.wait_ge(sem("slotA_free"), NSL_A + PER_C * c + 2)
                if c:
                    wait(act, ("merged", c))
                for m in range(NM):
                    i = nc.scalar.activation(tb[:, m, :], bank(m), ACT.Tanh, scale=rstdh[:, m:m + 1])
                i.then_inc(sem("tb"), 1)
            for i in range(0, 8, 2):
                act.wait_ge(sem("mTp"), i + 1)
                nc.scalar.activation(hT[:, 2 * i:2 * i + 2, :].rearrange("p k t -> p (k t)"), bank(i), ACT.Copy,
                                     scale=0.5).then_inc(sem("mT"), 1)
            for m in range(NM):
                act.wait_ge(sem("x1"), 2 * NC)
                nc.scalar.activation(junk, x1[:, m, :], ACT.Square, accum_out=ss2[:, m:m + 1])\
                    .then_inc(sem("ss2"), 1)
                act.wait_ge(sem("ss2"), m + 1)
            wait(act, ("rstd2", 1))
            for m in range(NM):
                nc.scalar.activation(h2[:, m, :], x1[:, m, :], ACT.Copy, scale=rstd2[:, m:m + 1])\
                    .then_inc(sem("h2"), 1)
            wait(act, ("r_d", 1))
            nc.scalar.activation(rt["ed"], rt["d"], ACT.Exp).then_inc(sem("r_ed"), 1)
            wait(act, ("r_dm", 1))
            nc.scalar.activation(rt["e2"], rt["dm"], ACT.Exp).then_inc(sem("r_e2"), 1)

            wait(act, ("rounds_ready", 1))
            rounds = act.value_load(rounds_i[0:1, 0:1], min_val=1, max_val=SEQ // CAP)
            with act.Fori(0, rounds) as r:
                with act.Fori(0, PAIRS) as p:
                    n = r * PAIRS + p
                    act.wait_ge(sem("combT"), n + 2)
                    nc.scalar.activation(comb, bank(2, SEQ), ACT.Copy).then_inc(sem("comb"), 1)
                    act.wait_ge(sem("slotM_free"), n * PER_PAIR + RING_M + 4)
                    nc.scalar.activation(hth, bank(0), ACT.Tanh, scale=0.5).then_inc(sem("hth"), 1)
                    act.wait_ge(sem("actT"), n + 1)
                    nc.scalar.activation(aT, bank(3), ACT.Copy).then_inc(sem("aT"), 1)
                    for k in range(NC):
                        if k % 2 == 0:
                            act.wait_ge(sem("down"), n * 2 + k // 2 + 1)
                        else:
                            act.wait_ge(sem("slotM_free"), n * PER_PAIR + RING_M + 8 + k + 1)
                        nc.scalar.activation(Ysb[:, k * CB:(k + 1) * CB], bank(4 + k % 2), ACT.Copy)\
                            .then_inc(sem("yev"), 1)
            act.wait_ge(sem("loop_done"), 1)
            for m in range(NM):
                nc.scalar.activation(junk, x1[:, m, :], ACT.Square, accum_out=ss2[:, m:m + 1])\
                    .then_inc(sem("ss3"), 1)
                act.wait_ge(sem("ss3"), m + 1)

        @block.vector
        def _(dve):
            links = [0]

            def link(ins):
                links[0] += 1
                ins.then_inc(sem("dve_link"), 1)
                dve.wait_ge(sem("dve_link"), links[0])

            tt = nc.vector.tensor_tensor
            ts = nc.vector.tensor_scalar
            stt = nc.vector.scalar_tensor_tensor

            dve.wait_ge(sem("nmix_in"), 16)
            for i in range(8):
                dve.wait_ge(sem("xTp"), i + 1)
                tt(hT[:, 2 * i:2 * i + 2, :], bank(i).rearrange("p (k t) -> p k t", k=2),
                   nmix[:, 2 * i:2 * i + 2].unsqueeze(2).to_broadcast([P, 2, SEQ]), ALU.mult).then_inc(sem("hT"), 1)
            wait(dve, full("cw"))
            nc.vector.tensor_copy(cw, pair("cw")[:, 0:96]).then_inc(sem("cw"), 1)
            dve.wait_ge(sem("small_in"), SMALL)
            wait(dve, ("zs", 1))
            link(tt(mh(xa), zs3[:, :, A_HEADS:2 * A_HEADS], dtb.unsqueeze(1).to_broadcast([P, NM, A_HEADS]), ALU.add))
            stt(na, xa, -1.0, xa, ALU.mult, ALU.min).then_inc(sem("na"), 1)
            wait(dve, ("tbeta", 1))
            link(ts(beta, beta, 0.5, 0.5, ALU.mult, ALU.add))
            ts(bhalf, beta, 0.5, None, ALU.mult)
            wait(dve, ("lna", 1))
            link(stt(xa, xa, 0.0, na, ALU.max, ALU.add))
            link(tt(mh(xa), mh(xa), alog.unsqueeze(1).to_broadcast([P, NM, A_HEADS]), ALU.mult))
            ts(gdec, xa, -1.0, None, ALU.mult).then_inc(sem("gdec"), 1)
            wait(dve, full("gc"))
            link(nc.vector.tensor_copy(gcol, pair("gc")[:, 0:half16]))
            tt(gdif, pair("gc")[:, half16:2 * half16], gcol, ALU.subtract).then_inc(sem("gcol"), 1)
            wait(dve, ("eg", 1))
            tt(beg, beta, eg, ALU.mult).then_inc(sem("beg"), 1)
            wait(dve, full("gkT"))
            dve.wait_ge(sem("small_in"), SMALL)
            b4 = T_["bT"].rearrange("p (h t) -> p h t", h=B_HEADS)
            tt(b4, pair("gkT").rearrange("p (h t) -> p h t", h=B_HEADS),
               bgk.unsqueeze(2).to_broadcast([P, B_HEADS, SEQ]), ALU.add).then_inc(sem("gkx"), 1)
            dve.wait_ge(sem("gkx"), 1)
            stt(T_["bE"], T_["bT"], -1.0, T_["bT"], ALU.mult, ALU.min).then_inc(sem("gkn"), 1)
            wait(dve, ("gkl", 1))
            link(stt(T_["bE"], T_["bT"], 0.0, T_["bE"], ALU.min, ALU.subtract))
            for u in range(GU):
                sl = slice(u * P, (u + 1) * P)
                i = nc.vector.tensor_tensor_scan(T_["bT"][:, sl], ones, T_["bE"][:, sl], 0.0, ALU.mult, ALU.add)
            link(i)
            wait(dve, full("bkT"))
            nc.vector.tensor_copy(T_["bkT"], pair("bkT")).then_inc(sem("bkT"), 1)
            wait(dve, full("lv_eye"))
            tt(units(T_["attn"]), units(pair("lv_eye")), ident.unsqueeze(1).to_broadcast([P, GU, P]), ALU.mult)\
                .then_inc(sem("attn_tmp"), 1)
            qm, km = Z1[:, 0:1024], Z1[:, 1024:2048]
            nc.vector.memset(qm, 0.0)
            link(nc.vector.memset(km, 0.0))
            dve.wait_ge(sem("bqT"), 1)
            dve.wait_ge(sem("bkT"), 1)
            for i, b in enumerate(LEVELS):
                nb = 1024 // (2 * b)

                def halves(t):
                    v = t.rearrange("p (m s r) -> p m s r", s=2, r=b)
                    return v[:, :, 0, :], v[:, :, 1, :]

                (blo, bup), (elo, eup) = halves(T_["bT"]), halves(T_["bE"])
                ref = blo[:, :, b - 1:b].to_broadcast([P, nb, b])
                tt(elo, ref, blo, ALU.subtract)
                tt(eup, bup, ref, ALU.subtract).then_inc(sem("bdist"), 1)
                dve.wait_ge(sem("bE"), i + 1)
                if i:
                    wait(dve, full(f"lv{LEVELS[i - 1]}"))
                tt(halves(km)[0], halves(T_["bkT"])[0], elo, ALU.mult)
                tt(halves(qm)[1], halves(T_["bqT"])[1], eup, ALU.mult).then_inc(sem("qkm"), 1)
                wait(dve, full(f"lv{b}"))
                tt(units(T_["btmp"]), units(pair(f"lv{b}")), upp[b].unsqueeze(1).to_broadcast([P, GU, P]), ALU.mult)\
                    .then_inc(sem("attn_tmp"), 1)
                dve.wait_ge(sem("attn_tmp"), i + 2)
                i2 = tt(T_["attn"], T_["attn"], T_["btmp"], ALU.add)
                if b == LEVELS[-1]:
                    i2.then_inc(sem("attn"), 1)
                else:
                    link(i2)
            bu = T_["bT"].rearrange("p (h n t) -> p h n t", h=B_HEADS, n=NM)
            eu = T_["bE"].rearrange("p (h n t) -> p h n t", h=B_HEADS, n=NM)
            nc.vector.tensor_copy(eu[:, :, 1, :], bu[:, :, 1, :])
            tt(eu[:, :, 0, :], bu[:, :, 0, P - 1:P].to_broadcast([P, B_HEADS, P]), bu[:, :, 0, :], ALU.subtract)\
                .then_inc(sem("bedge"), 1)
            dve.wait_ge(sem("bE"), 8)
            tt(units(T_["kdT"], B_HEADS), T_["bkT"].rearrange("p (h n t) -> p h n t", h=B_HEADS, n=NM)[:, :, 0, :],
               eu[:, :, 0, :], ALU.mult)
            wait(dve, full("lv64"))
            q4 = qm.rearrange("p (h n t) -> p h n t", h=B_HEADS, n=NM)
            tt(q4[:, :, 1, :], T_["bqT"].rearrange("p (h n t) -> p h n t", h=B_HEADS, n=NM)[:, :, 1, :],
               eu[:, :, 1, :], ALU.mult).then_inc(sem("edge"), 1)
            dve.wait_ge(sem("bth"), 1)
            bg = Z1[:, 4 * 1024:6 * 1024]
            link(stt(T_["bth"], T_["bth"], 1.0, bg, ALU.add, ALU.mult))
            dve.wait_ge(sem("b_sq"), 1)
            nc.vector.reduce_sum(rms[:, 0:4], T_["bqT"].rearrange("p (h e) -> p h e", h=B_HEADS), axis=AX.X)
            link(nc.vector.reduce_sum(rms[:, 4:8], T_["bkT"].rearrange("p (h e) -> p h e", h=B_HEADS), axis=AX.X))
            ts(rms[:, 0:8], rms[:, 0:8], 1.0 / B_DV, EPS, ALU.mult, ALU.add).then_inc(sem("b_ms"), 1)
            wait(dve, ("b_rf", 1))
            o3 = T_["bo"].rearrange("p (u e) -> p u e", u=8)
            link(tt(o3, o3, rmf[:, 0:8].unsqueeze(2).to_broadcast([P, 8, B_DV]), ALU.mult))
            for n in range(NM):
                i = tt(T_["bo"][:, n * 1024:(n + 1) * 1024].rearrange("p (a c) -> p a c", a=2),
                       T_["bo"][:, n * 1024:(n + 1) * 1024].rearrange("p (a c) -> p a c", a=2),
                       T_["bth"].rearrange("p (a n c) -> p a n c", a=2, n=NM)[:, :, n, :], ALU.mult)
            i.then_inc(sem("b_out"), 1)
            dve.wait_ge(sem("small_in"), SMALL)
            for i in range(2):
                wait(dve, full(f"obT{i}"))
                for hf in range(2):
                    src = pair(f"obT{i}").rearrange("p (h f t) -> p h f t", h=2, f=2)[:, :, hf, :]
                    dst = obT[:, 4 * i:4 * i + 4, :].rearrange("p (h f) t -> p h f t", f=2)[:, :, hf, :]
                    j = ts(dst, src, bnorm[:, hf:hf + 1], 0.5, ALU.mult, ALU.mult)
                j.then_inc(sem("obT"), 1)

            for g in range(NG):
                s = f".{g}"
                Zb = Z0 if g == 0 else Z1
                c = [Zb[:, i * 1024:(i + 1) * 1024] for i in range(3)]
                zg = [T_[f"zT{i}"][:, 0:zpad].rearrange("p (h t) -> p h t", h=GH) for i in range(3)]
                hs_g = slice(g * GH, (g + 1) * GH)

                def per_unit(t):
                    return mh(t)[:, :, hs_g].rearrange("p n h -> p h n").unsqueeze(3).to_broadcast([P, GH, NM, P])

                def u4(t):
                    return t.rearrange("p (h n t) -> p h n t", h=GH, n=NM)

                if g:
                    wait(dve, full(f"oaT.{g - 1}"))
                for i in range(3):
                    nc.vector.memset(zg[i][:, :, 0:TAPS - 1], 0.0)
                wait(dve, full("zkT" + s))
                nc.vector.tensor_copy(zg[1][:, :, TAPS - 1:], pair("zkT" + s).rearrange("p (h t) -> p h t", h=GH))\
                    .then_inc(sem("zkT"), 1)
                wait(dve, full("gcb" + s))
                for what, op, dst in (("Dn", ALU.max, "Dm"), ("DTn", ALU.min, "DT")):
                    link(tt(u4(T_[dst]), u4(pair("gcb" + s)), per_unit(gcol), ALU.subtract))
                    i = ts(T_[dst], T_[dst], 0.0, None, op)
                    i.then_inc(sem(what), 1)
                nc.vector.memset(rms[:, 15:16], 0.0).then_inc(sem("gcb"), 1)
                cwv = cw.rearrange("p (w h k) -> p w h k", w=3, h=A_HEADS)
                for w, ev in ((0, "zqT"), (1, "zkT"), (2, "zvT")):
                    wait(dve, (ev, g + 1))
                    if w == 0:
                        wait(dve, full("zvT" + s))
                    c4 = c[w].rearrange("p (h t) -> p h t", h=GH)
                    for k in range(TAPS):
                        for h in range(GH):
                            wk = cwv[:, w, g * GH + h, k:k + 1]
                            src = zg[w][:, h, k:k + SEQ]
                            if k == 0:
                                i = ts(c4[:, h, :], src, wk, None, ALU.mult)
                            else:
                                i = stt(c4[:, h, :], src, wk, c4[:, h, :], ALU.mult, ALU.add)
                        if k < TAPS - 1:
                            link(i)
                    i.then_inc(sem("conv"), 1)
                for w in range(3):
                    dve.wait_ge(sem("tconv"), 3 * g + w + 1)
                    stt(c[w], T_[f"zT{w}"][:, 0:1024], 1.0, c[w], ALU.add, ALU.mult).then_inc(sem("silu"), 1)
                wait(dve, full("ssq" + s))
                ts(ssqk, pair("ssq" + s)[:, 0:16], 4 * EPS, None, ALU.add).then_inc(sem("ssqk"), 1)
                wait(dve, ("rqk", g + 1))
                wait(dve, full("ktok" + s))
                tt(units(T_["zT0"][:, 0:1024]), units(pair("ktok" + s)),
                   rqk[:, 8:16].unsqueeze(2).to_broadcast([P, GU, P]), ALU.mult).then_inc(sem("ktok"), 1)
                wait(dve, full("vtok" + s))
                tt(u4(T_["zT2"][:, 0:1024]), u4(pair("vtok" + s)), per_unit(bhalf), ALU.mult)\
                    .then_inc(sem("vtok"), 1)
                wait(dve, full("A" + s))
                wait(dve, ("DA", g + 1))
                tt(T_["Dm"], pair("A" + s), T_["Dm"], ALU.mult).then_inc(sem("A"), 1)
                wait(dve, full("PT" + s))
                wait(dve, ("DTm", g + 1))
                tt(T_["DT"], pair("PT" + s), T_["DT"], ALU.mult).then_inc(sem("PT"), 1)
                idb = ident.unsqueeze(1).to_broadcast([P, GU, P])
                wait(dve, full("Y1" + s))
                stt(units(T_["U"]), units(pair("Y1" + s)), -1.0, idb, ALU.mult, ALU.add).then_inc(sem("U"), 1)
                stt(units(T_["T"]), units(T_["gB"]), -1.0, idb, ALU.mult, ALU.add).then_inc(sem("T"), 1)
                for i, b in enumerate(LEVELS[1:]):
                    wait(dve, full(f"dU{b}" + s))
                    if b != 64:
                        wait(dve, full(f"dT{b}" + s))
                    dve.wait_ge(sem("U"), 7 * g + i + 1)
                    tt(T_["U"], T_["U"], pair(f"dU{b}" + s), ALU.subtract).then_inc(sem("U"), 1)
                    if b != 64:
                        dve.wait_ge(sem("T"), 6 * g + i + 1)
                        tt(T_["T"], T_["T"], pair(f"dT{b}" + s), ALU.subtract).then_inc(sem("T"), 1)
                wait(dve, full("oi" + s))
                tt(units(T_["inter"], GH), units(pair("oi" + s)[:, 0:512], GH),
                   mh(eg)[:, 1, hs_g].unsqueeze(2).to_broadcast([P, GH, P]), ALU.mult).then_inc(sem("inter"), 1)
                wait(dve, full("o" + s))
                nc.vector.tensor_copy(u4(T_["Y"])[:, :, 0, :], u4(pair("o" + s))[:, :, 0, :])
                dve.wait_ge(sem("inter"), g + 1)
                tt(u4(T_["Y"])[:, :, 1, :], u4(pair("o" + s))[:, :, 1, :], units(T_["inter"], GH), ALU.add)\
                    .then_inc(sem("a_o"), 1)
                dve.wait_ge(sem("tz"), g + 1)
                link(stt(T_["L1"], T_["L1"], 1.0, Zb[:, 3 * 1024:4 * 1024], ALU.add, ALU.mult))
                dve.wait_ge(sem("a_sq"), g + 1)
                nc.vector.reduce_sum(rms[:, 0:8], units(T_["zT1"][:, 0:1024]), axis=AX.X).then_inc(sem("a_ms"), 1)
                wait(dve, ("a_rf", g + 1))
                link(tt(units(T_["Y"]), units(T_["Y"]), rmf[:, 0:8].unsqueeze(2).to_broadcast([P, GU, P]), ALU.mult))
                tt(u4(T_["Y"]), u4(T_["Y"]), T_["L1"].rearrange("p (n h t) -> p h n t", h=GH, n=NM), ALU.mult)\
                    .then_inc(sem("a_out"), 1)
                if g == 0:
                    dve.wait_ge(sem("small_in"), SMALL)
                wait(dve, full("oaT" + s))
                ts(oaT[:, g * GH:(g + 1) * GH, :], pair("oaT" + s).rearrange("p (h t) -> p h t", h=GH), anorm, 0.5,
                   ALU.mult, ALU.mult).then_inc(sem("oaT"), 1)

            for c in range(NC):
                cs = slice(c * CB, (c + 1) * CB)
                if c == 0:
                    dve.wait_ge(sem("z"), len(BLOCKS))
                dve.wait_ge(sem("slotA_free"), NSL_A + PER_C * c + 3)
                for m in range(NM):
                    i = stt(gateA[:, m, cs], gateA[:, m, cs], 1.0, bank(2 + m), ALU.add, ALU.mult)
                i.then_inc(sem("gya"), 1)
                dve.wait_ge(sem("slotA_free"), NSL_A + PER_C * c + 4)
                dve.wait_ge(sem("tb"), c + 1)
                for m in range(NM):
                    i = stt(tyb[:, m, :], tb[:, m, :], 1.0, bank(4 + m), ALU.add, ALU.mult)
                i.then_inc(sem("gyb"), 1)
                dve.wait_ge(sem("gyb"), c + 1)
                dve.wait_ge(sem("gya"), c + 1)
                tt(gateA[:, :, cs], gateA[:, :, cs], tyb, ALU.add).then_inc(sem("merged"), 1)
                dve.wait_ge(sem("merged"), c + 1)
            for i in range(1, 8, 2):
                dve.wait_ge(sem("mTp"), i + 1)
                ts(hT[:, 2 * i:2 * i + 2, :].rearrange("p k t -> p (k t)"), bank(i), 0.5, None, ALU.mult)\
                    .then_inc(sem("mT"), 1)
            for c in range(NC):
                cs = slice(c * CB, (c + 1) * CB)
                dve.wait_ge(sem("slotA_free"), NSL_MERGE + 2 * (c + 1))
                for m in range(NM):
                    if c == 0 and m == 0:
                        dve.wait_ge(sem("x_back"), 16 * NM)
                    tt(x1[:, m, cs], bank(2 * (c % 2) + m), x1[:, m, cs], ALU.add).then_inc(sem("x1"), 1)
            dve.wait_ge(sem("small_in"), SMALL)
            for i in range(8):
                dve.wait_ge(sem("h2Tp"), i + 1)
                tt(hT[:, 2 * i:2 * i + 2, :], bank(i).rearrange("p (k t) -> p k t", k=2),
                   nffn[:, 2 * i:2 * i + 2].unsqueeze(2).to_broadcast([P, 2, SEQ]), ALU.mult).then_inc(sem("h2T"), 1)
            dve.wait_ge(sem("small_in"), SMALL)
            dve.wait_ge(sem("logits"), 1)
            R = GROUPS + NE
            lp = bank(0, NM * R).rearrange("p (m c) -> p m c", m=NM)

            def m_(t):
                return t.rearrange("p (m c) -> p m c", m=NM)

            def spread(t, n):
                return t.unsqueeze(2).to_broadcast([P, NM, n])

            def first(eq, cum, out, n):
                for m in range(NM):
                    i = nc.vector.tensor_tensor_scan(cum[:, m * n:(m + 1) * n], ones[:, 0:n], eq[:, m * n:(m + 1) * n],
                                                     0.0, ALU.mult, ALU.add)
                link(i)
                link(stt(out, cum, 1.0, eq, ALU.is_le, ALU.mult))

            tt(m_(rt["lg"]), lp[:, :, 0:GROUPS], brg.unsqueeze(1).to_broadcast([P, NM, GROUPS]), ALU.add)
            link(tt(m_(rt["le"]), lp[:, :, GROUPS:R], bre.unsqueeze(1).to_broadcast([P, NM, NE]), ALU.add))
            link(nc.vector.reduce_max(rt["gm"], m_(rt["lg"]), axis=AX.X))
            tt(m_(rt["d"]), m_(rt["lg"]), spread(rt["gm"], GROUPS), ALU.subtract).then_inc(sem("r_d"), 1)
            dve.wait_ge(sem("r_d"), 1)
            link(ts(rt["eq"][:, 0:8], rt["d"], 0.0, None, ALU.is_equal))
            first(rt["eq"][:, 0:8], rt["cum"][:, 0:8], rt["fg"], GROUPS)
            fg4 = m_(rt["fg"]).unsqueeze(3).to_broadcast([P, NM, GROUPS, EPG])

            def mge(t):
                return t.rearrange("p (m g e) -> p m g e", m=NM, g=GROUPS)

            link(tt(mge(rt["pr"]), mge(rt["le"]), fg4, ALU.mult))
            link(nc.vector.tensor_reduce(m_(rt["ls"]), rt["pr"].rearrange("p (m g e) -> p m e g", m=NM, g=GROUPS),
                                         AX.X, ALU.add))
            link(nc.vector.reduce_max(rt["m1"], m_(rt["ls"]), axis=AX.X))
            link(tt(m_(rt["d1"]), m_(rt["ls"]), spread(rt["m1"], EPG), ALU.subtract))
            link(ts(rt["eq"], rt["d1"], 0.0, None, ALU.is_equal))
            first(rt["eq"], rt["cum"], rt["f1"], EPG)
            link(stt(rt["ls2"], rt["f1"], NEG, rt["ls"], ALU.mult, ALU.add))
            link(nc.vector.reduce_max(rt["m2"], m_(rt["ls2"]), axis=AX.X))
            tt(rt["dm"], rt["m2"], rt["m1"], ALU.subtract).then_inc(sem("r_dm"), 1)
            link(tt(m_(rt["d2"]), m_(rt["ls2"]), spread(rt["m2"], EPG), ALU.subtract))
            link(ts(rt["eq"], rt["d2"], 0.0, None, ALU.is_equal))
            first(rt["eq"], rt["cum"], rt["f2"], EPG)
            link(tt(rt["fs"], rt["f1"], rt["f2"], ALU.add))
            tt(mge(Mt), m_(rt["fs"]).unsqueeze(2).to_broadcast([P, NM, GROUPS, EPG]), fg4, ALU.mult)\
                .then_inc(sem("Mt"), 1)
            dve.wait_ge(sem("r_ed"), 1)
            link(nc.vector.reduce_sum(rt["den"], m_(rt["ed"]), axis=AX.X))
            dve.wait_ge(sem("r_e2"), 1)
            link(ts(rt["s2"], rt["e2"], 1.0, None, ALU.add))
            link(tt(rt["s2"], rt["s2"], rt["den"], ALU.mult))
            link(nc.vector.reciprocal(rt["r2"], rt["s2"]))
            link(ts(rt["w1"], rt["r2"], 0.5, None, ALU.mult))
            link(tt(rt["w2"], rt["w1"], rt["e2"], ALU.mult))
            tt(m_(rt["ws"]), m_(rt["f1"]), spread(rt["w1"], EPG), ALU.mult)
            link(tt(m_(rt["wa"]), m_(rt["f2"]), spread(rt["w2"], EPG), ALU.mult))
            link(tt(rt["ws"], rt["ws"], rt["wa"], ALU.add))
            tt(mge(Wt), m_(rt["ws"]).unsqueeze(2).to_broadcast([P, NM, GROUPS, EPG]), fg4, ALU.mult)
            dve.wait_ge(sem("ranks"), 1)
            dve.wait_ge(sem("Mt"), 1)
            link(tt(pos, bank(1, NM * NE), Mt, ALU.mult))
            link(ts(pos, pos, 1.0, None, ALU.subtract))
            link(nc.vector.reduce_max(rt["mx"], bank(2, NE), axis=AX.X))
            ts(rt["c1"], rt["mx"], float(CAP), None, ALU.is_gt)
            ts(rt["c2"], rt["mx"], float(2 * CAP), None, ALU.is_gt)
            link(ts(rt["c3"], rt["mx"], float(3 * CAP), 1.0, ALU.is_gt, ALU.add))
            link(tt(rt["c1"], rt["c1"], rt["c2"], ALU.add))
            tt(rounds_i[:, :], rt["c1"], rt["c3"], ALU.add).then_inc(sem("rounds_ready"), 1)
            dve.wait_ge(sem("rounds_ready"), 1)

            rounds = dve.value_load(rounds_i[0:1, 0:1], min_val=1, max_val=SEQ // CAP)
            with dve.Fori(0, rounds) as r:
                with dve.Fori(0, PAIRS) as p:
                    n = r * PAIRS + p
                    for b in range(4):
                        dve.wait_ge(sem("gath"), n * 4 + b + 1)
                        tt(xeT[:, 4 * b:4 * b + 4, :], bank(2 + b % 2).rearrange("p (k s) -> p k s", k=4),
                           nffn[:, 4 * b:4 * b + 4].unsqueeze(2).to_broadcast([P, 4, P]), ALU.mult)\
                            .then_inc(sem("xe"), 1)
                    dve.wait_ge(sem("hth"), n + 1)
                    stt(hs, hth, 1.0, bank(0), ALU.add, ALU.mult).then_inc(sem("hs"), 1)
                    dve.wait_ge(sem("hs"), n + 1)
                    dve.wait_ge(sem("slotM_free"), n * PER_PAIR + RING_M + 8)
                    tt(hid, hs, bank(1), ALU.mult).then_inc(sem("hid"), 1)
                    for k in range(NC):
                        for m in range(NM):
                            dve.wait_ge(sem("cmb"), n * 8 + 2 * k + m + 1)
                            tt(x1[:, m, k * CB:(k + 1) * CB], x1[:, m, k * CB:(k + 1) * CB], bank(6 + m),
                               ALU.add).then_inc(sem("xadd"), 1)
            dve.wait_ge(sem("xadd"), rounds * (8 * PAIRS) + 2)
            nc.vector.memset(rt["c1"], 0.0).then_inc(sem("loop_done"), 1)
            dve.wait_ge(sem("nfin_in"), 16)
            wait(dve, ("rstd3", 1))
            for m in range(NM):
                stt(x1[:, m, :], x1[:, m, :], rstd2[:, m:m + 1], nfin, ALU.mult, ALU.mult).then_inc(sem("y_ready"), 1)

        @block.tensor
        def _(pe):
            mm, tr = nc.tensor.matmul, nc.tensor.transpose

            def done(step, ins):
                ins.then_inc(sem(full(step)[0]), 1)

            def open_pair(step):
                i = STEPS.index(step)
                if i >= 2:
                    wait(pe, drained(STEPS[i - 2]))

            def quarter(q):
                b, part = divmod(q, QUARTERS)
                h, m = divmod(part, NM)
                s = 2 * b + h
                if part == 0 and b >= 2:
                    pe.wait_ge(sem("z"), b - 1)
                if m == 0:
                    pe.wait_ge(sem(f"slotA{s % RING_A}"), 16 * (s // RING_A + 1))
                for k in range(HT):
                    i = mm(bank(2 * (b % 2) + m), hT[:, h * HT + k, m * P:(m + 1) * P], ringA[:, s % RING_A, k, :],
                           start=(h == 0 and k == 0), stop=(h == 1 and k == HT - 1))
                if m == NM - 1:
                    i.then_inc(sem("slotA_free"), 1)

            def fill(step):
                for q in FILL[step]:
                    quarter(q)

            pe.wait_ge(sem("ident"), 1)
            for m in range(NM):
                pe.wait_ge(sem(f"x_in{m}"), 16)
            for i in range(8):
                for k in range(2):
                    for m in range(NM):
                        j = tr(bank(i)[:, (k * NM + m) * P:(k * NM + m + 1) * P], xs0[:, m, 2 * i + k::KT], ident)
                j.then_inc(sem("xTp"), 1)
            wait(pe, ("hT", 8))
            for q in range(FIRST_BLOCKS * QUARTERS):
                quarter(q)
            pe.wait_ge(sem("small_in"), SMALL)
            ws3 = wsm[:, 0:KT * NSM].rearrange("p (k c) -> p k c", k=KT)
            for m in range(NM):
                for k in range(KT):
                    i = mm(pair("small")[:, m * NSM:(m + 1) * NSM], hT[:, k, m * P:(m + 1) * P], ws3[:, k, :],
                           start=(k == 0), stop=(k == KT - 1))
            done("small", i)
            fill("small")
            pe.wait_ge(sem("small_in"), SMALL)
            for j in range(3 * A_HEADS):
                i = tr(pair("cw")[:, j * TAPS:(j + 1) * TAPS], convw[:, j * P:(j + 1) * P], ident[0:TAPS, 0:TAPS])
            done("cw", i)
            fill("cw")
            open_pair("blrT")
            for m in range(NM):
                i = tr(pair("blrT")[0:RANK, m * P:(m + 1) * P], zs3[:, m, 2 * A_HEADS:NSM], ident)
            done("blrT", i)
            fill("blrT")
            open_pair("gc")
            pe.wait_ge(sem("consts"), 1)
            wait(pe, ("gdec", 1))
            mm(pair("gc")[:, 0:half16], upT, gdec, start=True, stop=True)
            done("gc", mm(pair("gc")[:, half16:2 * half16], ones, gdec, start=True, stop=True))
            fill("gc")
            open_pair("gkT")
            pe.wait_ge(sem("small_in"), SMALL)
            wait(pe, ("blrT", 1))
            for h in range(B_HEADS):
                i = mm(pair("gkT")[:, h * SEQ:(h + 1) * SEQ], T_["wgk2"][0:RANK, h * P:(h + 1) * P],
                       T_["blrT"][0:RANK, :], start=True, stop=True)
            done("gkT", i)
            fill("gkT")
            for name, blk in (("bqT", 0), ("bkT", 1)):
                open_pair(name)
                pe.wait_ge(sem("z"), blk + 1)
                for h in range(B_HEADS):
                    for n in range(NM):
                        i = tr(pair(name)[:, (h * NM + n) * P:(h * NM + n + 1) * P],
                               zsl("gla", blk)[:, n, h * P:(h + 1) * P], ident)
                done(name, i)
                fill(name)
            open_pair("lv_eye")
            wait(pe, ("bqT", 1))
            wait(pe, ("bkT", 1))
            for u in range(GU):
                sl = slice(u * P, (u + 1) * P)
                i = mm(pair("lv_eye")[:, sl], T_["bkT"][:, sl], T_["bqT"][:, sl], start=True, stop=True)
            done("lv_eye", i)
            fill("lv_eye")
            qm, km = Z1[:, 0:1024], Z1[:, 1024:2048]
            for j, b in enumerate(LEVELS):
                st = f"lv{b}"
                open_pair(st)
                pe.wait_ge(sem("qkm"), j + 1)
                for u in range(GU):
                    sl = slice(u * P, (u + 1) * P)
                    i = mm(pair(st)[:, sl], km[:, sl], qm[:, sl], start=True, stop=True)
                done(st, i)
                fill(st)
            open_pair("kd")
            wait(pe, ("edge", 1))
            for h in range(B_HEADS):
                i = tr(pair("kd")[:, h * P:(h + 1) * P], T_["kdT"][:, h * P:(h + 1) * P], ident)
            done("kd", i)
            fill("kd")

            def vrow(n, h):
                return zsl("gla", 2 + h // 2)[:, n, (h % 2) * B_DV:(h % 2 + 1) * B_DV]

            open_pair("bS")
            wait(pe, ("kdtok", 1))
            pe.wait_ge(sem("z"), 4)
            for h in range(B_HEADS):
                i = mm(pair("bS")[:, h * B_DV:(h + 1) * B_DV], T_["kdtok"][:, h * P:(h + 1) * P], vrow(0, h),
                       start=True, stop=True)
            done("bS", i)
            fill("bS")
            wait(pe, ("attn", 1))
            for n in range(NM):
                st = f"bo{n}"
                open_pair(st)
                if n:
                    wait(pe, ("bS", 1))
                for h in range(B_HEADS):
                    u = h * NM + n
                    sl = slice(u * P, (u + 1) * P)
                    o = pair(st)[:, h * B_DV:(h + 1) * B_DV]
                    i = mm(o, T_["attn"][:, sl], vrow(n, h), start=True, stop=(n == 0))
                    if n:
                        i = mm(o, qm[:, sl], T_["bS"][:, h * B_DV:(h + 1) * B_DV], start=False, stop=True)
                done(st, i)
                fill(st)
            wait(pe, ("b_out", 1))
            for j in range(2):
                st = f"obT{j}"
                open_pair(st)
                for h in range(2):
                    for f in range(2):
                        for n in range(NM):
                            src = T_["bo"][:, n * 1024 + (2 * j + h) * B_DV + f * P:][:, 0:P]
                            i = tr(pair(st)[:, ((h * 2 + f) * NM + n) * P:((h * 2 + f) * NM + n + 1) * P], src, ident)
                done(st, i)
                fill(st)

            for g in range(NG):
                s = f".{g}"
                which = f"gdn{g}"
                first_block = FIRST_BLOCKS + 4 * g
                Zb = Z0 if g == 0 else Z1
                c = [Zb[:, i * 1024:(i + 1) * 1024] for i in range(3)]

                def per_u(step, f, us=range(GU)):
                    for u in us:
                        i = f(u, slice(u * P, (u + 1) * P))
                    done(step + s, i)
                    fill(step + s)

                def lvl(step, f):
                    open_pair(step + s)
                    o = pair(step + s)
                    per_u(step, lambda u, sl: f(o, u, sl))

                for j, w in enumerate(("zqT", "zkT", "zvT")):
                    open_pair(w + s)
                    pe.wait_ge(sem("z"), first_block + j + 1)
                    o = pair(w + s)
                    per_u(w, lambda u, sl: tr(o[:, sl], zsl(which, j)[:, u % NM, (u // NM) * P:(u // NM + 1) * P],
                                              ident))
                wait(pe, ("gB", g + 1))
                lvl("gcb", lambda o, u, sl: mm(o[:, sl], T_["gB"][:, sl], upT, start=True, stop=True))
                open_pair("ssq" + s)
                pe.wait_ge(sem("sq"), 2 * g + 2)
                o = pair("ssq" + s)
                for j in range(2):
                    for u in range(GU):
                        i = mm(o[:, 8 * j + u:8 * j + u + 1], T_[f"zT{j}"][:, u * P:(u + 1) * P], ones[:, 0:1],
                               start=True, stop=True)
                done("ssq" + s, i)
                fill("ssq" + s)
                lvl("ktok", lambda o, u, sl: tr(o[:, sl], c[1][:, sl], ident))
                pe.wait_ge(sem("silu"), 3 * g + 3)
                lvl("vtok", lambda o, u, sl: tr(o[:, sl], c[2][:, sl], ident))
                lvl("khT", lambda o, u, sl: tr(o[:, sl], T_["zT0"][:, sl], ident))
                wait(pe, ("khT", g + 1))
                kh = T_["zT1"]
                lvl("A", lambda o, u, sl: mm(o[:, sl], kh[:, sl], kh[:, sl], start=True, stop=True))
                lvl("PT", lambda o, u, sl: mm(o[:, sl], kh[:, sl], c[0][:, sl], start=True, stop=True))
                pe.wait_ge(sem("L"), 7 * g + 1)
                lvl("Y1", lambda o, u, sl: mm(o[:, sl], T_["gB"][:, sl], ident, start=True, stop=True))
                for j, b in enumerate(LEVELS[1:]):
                    L = T_["gB"] if (j + 1) % 2 == 0 else T_["L1"]
                    pe.wait_ge(sem("L"), 7 * g + j + 2)
                    pe.wait_ge(sem("U"), 7 * g + j + 1)
                    lvl(f"Y{b}", lambda o, u, sl: mm(o[:, sl], L[:, sl], T_["U"][:, sl], start=True, stop=True))
                    pe.wait_ge(sem("Y"), 6 * g + j + 1)
                    pe.wait_ge(sem("T"), 6 * g + j + 1)
                    lvl(f"dU{b}", lambda o, u, sl: mm(o[:, sl], T_["T"][:, sl], T_["Y"][:, sl], start=True,
                                                      stop=True))
                    if b != 64:
                        lvl(f"dT{b}", lambda o, u, sl: mm(o[:, sl], T_["Y"][:, sl], T_["T"][:, sl], start=True,
                                                          stop=True))
                pe.wait_ge(sem("U"), 7 * g + 7)
                pe.wait_ge(sem("kbg"), g + 1)
                pe.wait_ge(sem("kdec"), g + 1)
                kb = T_["kbg"]

                def per_head(step, f):
                    open_pair(step + s)
                    o = pair(step + s)
                    for h in range(GH):
                        i = f(o[:, h * P:(h + 1) * P], slice(h * P, (h + 1) * P), slice((2 * h) * P, (2 * h + 1) * P),
                              slice((2 * h + 1) * P, (2 * h + 2) * P))
                    done(step + s, i)
                    fill(step + s)

                v = T_["zT2"]
                per_head("wT", lambda o, hh, u0, u1: mm(o, kb[:, u1], T_["U"][:, u1], start=True, stop=True))
                per_head("u0", lambda o, hh, u0, u1: mm(o, T_["U"][:, u0], v[:, u0], start=True, stop=True))
                wait(pe, ("u0", g + 1))
                per_head("S", lambda o, hh, u0, u1: mm(o, T_["kdec"][:, hh], T_["T"][:, hh], start=True, stop=True))
                wait(pe, ("a_S", g + 1))
                wait(pe, ("wT", g + 1))

                def v1(o, hh, u0, u1):
                    mm(o, T_["U"][:, u1], v[:, u1], start=True, stop=False)
                    return mm(o, T_["nwT"][:, hh], T_["aS"][:, hh], start=False, stop=True)

                per_head("v1", v1)
                per_head("oi", lambda o, hh, u0, u1: mm(o, c[0][:, u1], T_["aS"][:, hh], start=True, stop=True))
                wait(pe, ("v1", g + 1))
                wait(pe, ("PT", g + 1))
                lvl("o", lambda o, u, sl: mm(o[:, sl], T_["DT"][:, sl],
                                             T_["T"][:, (u % NM) * 512 + (u // NM) * P:][:, 0:P], start=True,
                                             stop=True))
                wait(pe, ("a_out", g + 1))
                lvl("oaT", lambda o, u, sl: tr(o[:, sl], T_["Y"][:, sl], ident))

            s0 = NSL_A
            wait(pe, ("oaT", NG))
            pe.wait_ge(sem("z"), len(BLOCKS))
            for c in range(NC):
                for h in range(2):
                    s = s0 + h
                    pe.wait_ge(sem(f"slotA{s % RING_A}"), 16 * (s // RING_A + 1))
                    if c and h == 0:
                        pe.wait_ge(sem("tb"), c)
                    for m in range(NM):
                        for k in range(HT):
                            i = mm(bank(m), hT[:, h * HT + k, m * P:(m + 1) * P], ringA[:, s % RING_A, k, :],
                                   start=(h == 0 and k == 0), stop=(h == 1 and k == HT - 1))
                    i.then_inc(sem("slotA_free"), 1)
                for w, (src, got) in enumerate(((oaT, "gya"), (obT, "gyb"))):
                    s = s0 + 2 + w
                    pe.wait_ge(sem(f"slotA{s % RING_A}"), 16 * (s // RING_A + 1))
                    if c:
                        pe.wait_ge(sem(got), c)
                    for m in range(NM):
                        for k in range(A_HEADS):
                            i = mm(bank(2 + 2 * w + m), src[:, k, m * P:(m + 1) * P], ringA[:, s % RING_A, k, :],
                                   start=(k == 0), stop=(k == A_HEADS - 1))
                    i.then_inc(sem("slotA_free"), 1)
                s0 += PER_C
            wait(pe, ("merged", NC))
            for i in range(8):
                for k in range(2):
                    for m in range(NM):
                        j = tr(bank(i)[:, (k * NM + m) * P:(k * NM + m + 1) * P], gateA[:, m, 2 * i + k::KT], ident)
                j.then_inc(sem("mTp"), 1)
            wait(pe, ("mT", 8))
            for c in range(NC):
                if c >= 2:
                    pe.wait_ge(sem("x1"), 2 * (c - 1))
                for h in range(2):
                    s = s0 + h
                    pe.wait_ge(sem(f"slotA{s % RING_A}"), 16 * (s // RING_A + 1))
                    for m in range(NM):
                        for k in range(HT):
                            i = mm(bank(2 * (c % 2) + m), hT[:, h * HT + k, m * P:(m + 1) * P],
                                   ringA[:, s % RING_A, k, :], start=(h == 0 and k == 0), stop=(h == 1 and k == HT - 1))
                    i.then_inc(sem("slotA_free"), 1)
                s0 += 2
            wait(pe, ("h2", 2))
            for i in range(8):
                for k in range(2):
                    for m in range(NM):
                        j = tr(bank(i)[:, (k * NM + m) * P:(k * NM + m + 1) * P], h2[:, m, 2 * i + k::KT], ident)
                j.then_inc(sem("h2Tp"), 1)
            wait(pe, ("h2T", 8))
            pe.wait_ge(sem("wr_in"), 32)
            R = GROUPS + NE
            wr = wsm.rearrange("p (k c) -> p k c", k=KT)
            for m in range(NM):
                for k in range(KT):
                    i = mm(bank(0, NM * R)[:, m * R:(m + 1) * R], hT[:, k, m * P:(m + 1) * P], wr[:, k, :],
                           start=(k == 0), stop=(k == KT - 1))
            i.then_inc(sem("logits"), 1)
            wait(pe, ("Mt", 1))
            mm(bank(1)[:, 0:NE], upT, Mt[:, 0:NE], start=True, stop=True)
            mm(bank(1)[:, NE:2 * NE], upT, Mt[:, NE:2 * NE], start=True, stop=False)
            mm(bank(1)[:, NE:2 * NE], ones, Mt[:, 0:NE], start=False, stop=True)
            mm(bank(2, NE), ones, Mt[:, 0:NE], start=True, stop=False)
            mm(bank(2, NE), ones, Mt[:, NE:2 * NE], start=False, stop=True).then_inc(sem("ranks"), 1)
            wait(pe, ("rounds_ready", 1))
            pe.sem_inc(sem("xadd"), 2)
            pe.sem_inc(sem("yev"), 2)
            pe.sem_inc(sem("combT"), 1)
            rounds = pe.value_load(rounds_i[0:1, 0:1], min_val=1, max_val=SEQ // CAP)
            with pe.Fori(0, rounds) as r:
                with pe.Fori(0, PAIRS) as p:
                    n = r * PAIRS + p
                    pe.wait_ge(sem("sel"), n + 1)
                    for b in range(4):
                        if b >= 2:
                            pe.wait_ge(sem("xe"), n * 4 + b - 1)
                        for k in range(4):
                            for m in range(NM):
                                i = mm(bank(2 + b % 2)[:, k * P:(k + 1) * P], h2[:, m, 4 * b + k::KT],
                                       sel[:, m * P:(m + 1) * P], start=(m == 0), stop=(m == NM - 1))
                        i.then_inc(sem("gath"), 1)
                    pe.wait_ge(sem("selg"), n + 1)
                    pe.wait_ge(sem("xe"), n * 4 + 3)
                    for m in range(NM):
                        i = tr(bank(2)[:, m * P:(m + 1) * P], selg[:, m * P:(m + 1) * P], ident)
                    i.then_inc(sem("combT"), 1)
                    pe.wait_ge(sem("xe"), n * 4 + 4)
                    j = 0
                    for w in range(2):
                        for h in range(2):
                            for e in range(2):
                                pe.wait_ge(sem(f"slotM{(j + e) % RING_M}"), n * 32 + 16 * ((j + e) // RING_M + 1))
                            for k in range(HT):
                                for e in range(2):
                                    i = mm(bank(w)[e * CAP:(e + 1) * CAP, :],
                                           xeT[:, h * HT + k, e * CAP:(e + 1) * CAP],
                                           ringM[:, (j + e) % RING_M, k * CB:(k + 1) * CB],
                                           start=(h == 0 and k == 0), stop=(h == 1 and k == HT - 1))
                            i.then_inc(sem("slotM_free"), 2)
                            j += 2
                    pe.wait_ge(sem("hid"), n + 1)
                    for t in range(FT):
                        i = tr(bank(3)[:, t * P:(t + 1) * P], hid[:, t::FT], ident)
                    i.then_inc(sem("actT"), 1)
                    pe.wait_ge(sem("aT"), n + 1)
                    pe.wait_ge(sem("comb"), n + 1)

                    def combine(k):
                        pe.wait_ge(sem("yev"), n * NC + k + 3)
                        for m in range(NM):
                            pe.wait_ge(sem("xadd"), n * 8 + 2 * k + m + 1)
                            mm(bank(6 + m), comb[:, m * P:(m + 1) * P], Ysb[:, k * CB:(k + 1) * CB], start=True,
                               stop=True).then_inc(sem("cmb"), 1)

                    for k in range(NC):
                        if k % 2 == 0:
                            for e in range(2):
                                pe.wait_ge(sem(f"slotM{(j + e) % RING_M}"), n * 32 + 16 * ((j + e) // RING_M + 1))
                        pe.wait_ge(sem("yev"), n * NC + k + 1)
                        for t in range(FT):
                            for e in range(2):
                                src = ringM[:, (j + e) % RING_M, :].rearrange("p (t n) -> p t n", t=FT)
                                i = mm(bank(4 + k % 2)[e * CAP:(e + 1) * CAP, :],
                                       aT[:, t * P + e * CAP:t * P + (e + 1) * CAP],
                                       src[:, t, (k % 2) * CB:(k % 2 + 1) * CB], start=(t == 0), stop=(t == FT - 1))
                        if k % 2 == 0:
                            i.then_inc(sem("down"), 1)
                        else:
                            i.then_inc(sem("slotM_free"), 2)
                            j += 2
                        if k:
                            combine(k - 1)
                    combine(NC - 1)


_INS = ["x", "norm_mix", "w_in", "conv_a", "a_log", "dt_bias", "a_norm", "w_gk2", "b_gk", "b_norm", "w_oa", "w_ob",
        "w_out", "norm_ffn", "w_rg", "b_rg", "w_re", "b_re", "w1", "w3", "w2", "norm_final"]


def kernel(**inputs):
    import numpy as _np
    import concourse.bacc as _bacc
    from concourse import mybir as _mybir
    from concourse.bass_utils import run_bass_kernel_spmd as _run

    nc = _bacc.Bacc("TRN2", target_bir_lowering=False, num_devices=1)
    arrays, args = {}, []
    for name in _INS:
        a = _np.ascontiguousarray(inputs[name])
        arrays[f"in_{name}"] = a
        args.append(nc.dram_tensor(f"in_{name}", a.shape, _mybir.dt.from_np(a.dtype), kind="ExternalInput").ap())
    args.append(nc.dram_tensor("out_y", (1, SEQ, D), _mybir.dt.float32, kind="ExternalOutput").ap())
    build(nc, *args)
    r = _run(nc, [arrays], core_ids=[0])
    return r.results[0]["out_y"]
```

```python
from contextlib import ExitStack

import concourse.bass as bass
from concourse import mybir

F32 = mybir.dt.float32
F32R = mybir.dt.float32r
I32 = mybir.dt.int32
ALU = mybir.AluOpType
ACT = mybir.ActivationFunctionType
AX = mybir.AxisListType

P = 128
D = 2048
SEQ = 256
NM = SEQ // P
KT = D // P
CB = 512
NC = D // CB
HT = KT // 2
SLOT = HT * CB
CT = 4
CHUNK = CT * CB
BCH = KT // CT
EPS = 1e-6
A_HEADS, A_D, TAPS = 8, 128, 4
B_HEADS, B_DK, B_DV, RANK = 4, 128, 256, 16
GATE_NORM = 16.0
GH = 4
NG = A_HEADS // GH
GU = GH * NM
QSCALE = float(A_D) ** -0.5
AQ = A_HEADS * A_D
BQK, BV = B_HEADS * B_DK, B_HEADS * B_DV
C_AQ, C_AK, C_AV, C_AZ = 0, AQ, 2 * AQ, 3 * AQ
C_BETA = 4 * AQ
C_BQ = C_BETA + 2 * A_HEADS
C_BK = C_BQ + BQK
C_BV = C_BK + BQK
C_BG = C_BV + BV
C_LR = C_BG + BV
C_MA = C_LR + RANK
C_MB = C_MA + D
NSM = 2 * A_HEADS + RANK
LEVELS = [1 << i for i in range(7)]
GROUPS, EPG = 4, 8
NE = GROUPS * EPG
FF = 512
FT = FF // P
CAP = 64
PAIRS = NE // 2
NEG = -3.0e38
SMALL = 16 * 12

BLOCKS = ([("gla", i, C_BQ + CB * i) for i in range(6)]
          + [("gdn0", i, c) for i, c in enumerate((C_AQ, C_AK, C_AV, C_AZ))]
          + [("gdn1", i, c + CB) for i, c in enumerate((C_AQ, C_AK, C_AV, C_AZ))]
          + [("gate", i, C_MA + CB * i) for i in range(NC)])
RING_A = 3
NSPLIT = 2
RING_M = 6
PER_PAIR = 12

GLA_STEPS = (["small", "cw", "blrT", "gc", "gkT", "bqT", "bkT", "lv_eye"]
             + [f"lv{b}" for b in LEVELS] + ["kd", "bS", "bo0", "bo1", "obT0", "obT1"])
GDN_STEPS = (["zqT", "zkT", "zvT", "gcb", "ssq", "ktok", "vtok", "khT", "A", "PT", "Y1"]
             + [f"{w}{b}" for b in LEVELS[1:-1] for w in ("Y", "dU", "dT")]
             + ["Y64", "dU64", "wT", "u0", "S", "v1", "oi", "o", "oaT"])
STEPS = GLA_STEPS + [f"{s}.{g}" for g in range(NG) for s in GDN_STEPS]
FIRST_BLOCKS = 6
SPANS = [
    {"gc": 1, "gkT": 2, "bqT": 0, "bkT": 1, "lv_eye": 1, "lv1": 1, "lv2": 1, "lv4": 1, "lv8": 1, "lv16": 1,
     "lv32": 1, "lv64": 1, "kd": 1, "bS": 0, "bo0": 0, "bo1": 2, "obT0": 0, "obT1": 1},
] + [
    {f"{k}.{g}": v for k, v in
     {"gcb": 5, "ssq": 1, "vtok": 1, "khT": 1, "PT": 1, "dT2": 1, "dT4": 1, "dT8": 1, "dT16": 1, "dT32": 1,
      "wT": 1, "o": 1}.items()} for g in range(NG)
]


def fillers():
    out = {s: [] for s in STEPS}
    q = FIRST_BLOCKS * BCH
    for span in SPANS:
        assert sum(span.values()) == 4 * BCH, span
        for s in STEPS:
            n = span.get(s, 0)
            out[s] = out[s] + list(range(q, q + n))
            q += n
    assert q == len(BLOCKS) * BCH
    return out


FILL = fillers()


def build(nc, x, norm_mix, w_in, conv_a, a_log, dt_bias, a_norm, w_gk2, b_gk, b_norm, w_oa, w_ob, w_out,
          norm_ffn, w_rg, b_rg, w_re, b_re, w1, w3, w2, norm_final, y):
    x_v = x[0].rearrange("(m p) d -> p m d", p=P)
    y_v = y[0].rearrange("(m p) d -> p m d", p=P)
    win_v = w_in[0].rearrange("(p k) n -> p k n", k=KT)
    wout_v = w_out[0].rearrange("(p k) n -> p k n", k=KT)
    woa_v = w_oa[0].rearrange("(k p) n -> p k n", p=P)
    wob_v = w_ob[0].rearrange("(k p) n -> p k n", p=P)
    w1_v = w1[0].rearrange("e (p k) f -> e p (k f)", k=KT)
    w3_v = w3[0].rearrange("e (p k) f -> e p (k f)", k=KT)
    w2_v = w2[0].rearrange("e (p t) n -> e p t n", t=FT)

    with ExitStack() as ctx:
        block_of = {}

        def sem(name):
            if name not in block_of:
                block_of[name] = ctx.enter_context(nc.semaphore(name))
            return block_of[name]

        FREE = 53200
        ARENA = nc.sbuf_base + (-nc.sbuf_base) % 32
        arena = ctx.enter_context(nc.sbuf_tensor("arena", [P, FREE], F32))
        rounds_i = ctx.enter_context(nc.sbuf_tensor("rounds_i", [P, 1], I32))

        def cut(at, size):
            return arena[:, at:at + size], at + size

        def split_tensor(name, at, size):
            t = nc.alloc_sbuf_tensor_at(name, [P, size], F32R, offset=ARENA + 4 * at)
            return t[:, :]

        H0 = 0
        h2T = arena[:, H0:H0 + KT * SEQ].rearrange("p (k t) -> p k t", k=KT)
        hTh = split_tensor("hT_hi", H0, KT * SEQ).rearrange("p (k t) -> p k t", k=KT)
        H1 = H0 + KT * SEQ
        hTl = split_tensor("hT_lo", H1, KT * SEQ).rearrange("p (k t) -> p k t", k=KT)
        OAB = H1 + KT * SEQ
        oaT_f, at = cut(OAB, A_HEADS * SEQ)
        obT_f, at = cut(at, A_HEADS * SEQ)
        oaT = oaT_f.rearrange("p (k t) -> p k t", k=A_HEADS)
        obT = obT_f.rearrange("p (k t) -> p k t", k=A_HEADS)
        RM = at
        MIX = 6 * NM * CB + 12840 + 4 * NM * CB
        RA = RM + MIX
        ringA, at = cut(RA, RING_A * CHUNK)
        ringA = ringA.rearrange("p (s n) -> p s n", s=RING_A)
        w_hi, w_lo = [], []
        for i in range(NSPLIT):
            w_hi.append(split_tensor(f"w_hi{i}", at, CHUNK))
            w_lo.append(split_tensor(f"w_lo{i}", at + CHUNK, CHUNK))
            at += 2 * CHUNK
        ringM = arena[:, RM:RM + RING_M * SLOT].rearrange("p (s n) -> p s n", s=RING_M)
        consts = at
        x1 = arena[:, OAB:OAB + NM * D].rearrange("p (m d) -> p m d", m=NM)

        at = consts
        ident, at = cut(at, P)
        upT, at = cut(at, P)
        ones, at = cut(at, P)
        iota, at = cut(at, CAP)
        mask = {}
        for b in LEVELS:
            mask[b], at = cut(at, P)
        wsm, at = cut(at, KT * (GROUPS + NE))
        cw, at = cut(at, 3 * A_HEADS * TAPS)
        zs, at = cut(at, NM * NSM)
        nmix, at = cut(at, KT)
        nffn, at = cut(at, KT)
        anorm, at = cut(at, 1)
        bnorm, at = cut(at, 2)
        bgk, at = cut(at, B_HEADS)
        alog, at = cut(at, A_HEADS)
        dtb, at = cut(at, A_HEADS)
        half16 = NM * A_HEADS
        beta, at = cut(at, half16)
        gdec, at = cut(at, half16)
        xa, at = cut(at, half16)
        na, at = cut(at, half16)
        gcol, at = cut(at, half16)
        gdif, at = cut(at, half16)
        eg, at = cut(at, half16)
        ekd, at = cut(at, half16)
        bhalf, at = cut(at, half16)
        beg, at = cut(at, half16)
        ss1, at = cut(at, NM)
        rstd, at = cut(at, NM)
        rstdh, at = cut(at, NM)
        ssqk, at = cut(at, 16)
        rqk, at = cut(at, 16)
        rms, at = cut(at, 16)
        rmf, at = cut(at, 16)
        pw, at = cut(at, 16)
        ss2, at = cut(at, NM)
        rstd2, at = cut(at, NM)
        brg, at = cut(at, GROUPS)
        bre, at = cut(at, NE)
        assert at <= FREE, at
        zs3 = zs.rearrange("p (m c) -> p m c", m=NM)

        def mh(t):
            return t.rearrange("p (m h) -> p m h", m=NM)

        at = RM
        Z1_AT = at
        Z1, at = cut(at, 6 * NM * CB)
        TEMPS = at
        LAST = RM + MIX - 4 * NM * CB
        Z0, _ = cut(LAST, 4 * NM * CB)
        xs0 = Z0.rearrange("p (m d) -> p m d", m=NM)
        gateA = xs0
        names = {}

        def temps(base, sizes):
            at = base
            for n, s in sizes:
                names[n], at = cut(at, s)
            assert at <= LAST, (at, LAST)

        temps(TEMPS, [("bqT", 1024), ("bkT", 1024), ("bT", 1024), ("bE", 1024), ("attn", 1024), ("btmp", 1024),
                      ("bS", 1024), ("bo", 2048), ("bth", 2048), ("wgk2", 512),
                      ("blrT", 256)])
        names["kdT"], names["kdtok"] = names["btmp"][:, 0:512], names["btmp"][:, 512:1024]
        zpad = GH * (SEQ + TAPS - 1)
        temps(TEMPS, [("zT0", zpad), ("zT1", zpad), ("zT2", zpad), ("kbg", 1024), ("kdec", 512), ("nwT", 512),
                      ("aS", 512), ("gB", 1024), ("Dm", 1024), ("DT", 1024), ("L1", 1024), ("U", 1024), ("T", 1024),
                      ("Y", 1024)])
        names["inter"] = names["nwT"]
        convw = arena[0:TAPS, TEMPS:TEMPS + 3 * AQ]
        T_ = names

        def zsl(which, i):
            base = {"gla": Z1, "gdn0": Z0, "gdn1": Z1, "gate": Z0}[which]
            if which == "gate":
                return gateA[:, :, i * CB:(i + 1) * CB]
            return base[:, i * NM * CB:(i + 1) * NM * CB].rearrange("p (m n) -> p m n", m=NM)

        h2, _ = cut(H1, NM * D)
        at = RM + RING_M * SLOT
        h2 = h2.rearrange("p (m d) -> p m d", m=NM)
        xeT, at = cut(at, KT * P)
        xeT = xeT.rearrange("p (k s) -> p k s", k=KT)
        Ysb, at = cut(at, D)
        aT, at = cut(at, FT * P)
        hid, at = cut(at, FF)
        hth, at = cut(at, FF)
        hs, at = cut(at, FF)
        comb, at = cut(at, SEQ)
        sel, at = cut(at, NM * P)
        selg, at = cut(at, NM * P)
        nfin, at = cut(at, D)
        junk, at = cut(at, D)
        pos, at = cut(at, NM * NE)
        Wt, at = cut(at, NM * NE)
        Mt, at = cut(at, NM * NE)
        rt = {}
        for n, s in [("lg", 8), ("le", 64), ("gm", 2), ("d", 8), ("ed", 8), ("den", 2), ("pt", 2), ("eq", 16),
                     ("cum", 16), ("fg", 8), ("pr", 64), ("ls", 16), ("m1", 2), ("d1", 16), ("f1", 16), ("ls2", 16),
                     ("m2", 2), ("d2", 16), ("f2", 16), ("dm", 2), ("e2", 2), ("s2", 2), ("r2", 2), ("w1", 2),
                     ("w2", 2), ("fs", 16), ("ws", 16), ("wa", 16), ("mx", 1), ("c1", 1), ("c2", 1), ("c3", 1),
                     ("rf", 1)]:
            rt[n], at = cut(at, s)
        assert at <= consts, (at, consts)
        o_hi = [split_tensor(f"o{b}_hi", Z1_AT + 4096 * i, 2048) for i, b in enumerate("ab")]
        o_lo = [split_tensor(f"o{b}_lo", Z1_AT + 4096 * i + 2048, 2048) for i, b in enumerate("ab")]
        MRG = Z1_AT + 8192
        tb = arena[:, MRG:MRG + NM * CB].rearrange("p (m n) -> p m n", m=NM)
        tyb = arena[:, MRG + 1024:MRG + 2048].rearrange("p (m n) -> p m n", m=NM)

        psum = ctx.enter_context(nc.psum_tensor("psum", [P, 8 * CB], F32))

        def bank(i, n=CB):
            return psum[:, i * CB:i * CB + n]

        def pair(step):
            return psum[:, (4 + 2 * (STEPS.index(step) % 2)) * CB:(4 + 2 * (STEPS.index(step) % 2)) * CB + 2 * CB]

        def drained(step):
            base, _, g = step.partition(".")
            g = int(g or 0)
            if base[0] == "Y" and base != "Y1":
                return "Y", g * 6 + LEVELS.index(int(base[1:]))
            if base in ("Y1",) or base[:2] == "dU":
                return "U", g * 7 + (1 if base == "Y1" else LEVELS.index(int(base[2:])) + 1)
            if base[:2] == "dT":
                return "T", g * 6 + LEVELS.index(int(base[2:])) + 1
            if base[:2] == "lv":
                return "attn_tmp", (1 if base == "lv_eye" else LEVELS.index(int(base[2:])) + 2)
            alias = {"small": "zs", "o": "a_o", "bo0": "b_o", "bo1": "b_o", "obT0": "obT", "obT1": "obT",
                     "ssq": "ssqk", "S": "a_S", "kd": "kdtok", "gc": "gcol", "oi": "inter", "gkT": "gkx"}
            n = {"bo1": 2, "obT1": 2}.get(base, 1)
            return alias.get(base, base), g + n

        def full(step):
            i = STEPS.index(step)
            return f"pair{i % 2}_full", i // 2 + 1

        def wait(eng, what):
            eng.wait_ge(sem(what[0]), what[1])

        U3 = "p (u t) -> p u t"

        def units(t, u=GU):
            return t.rearrange(U3, u=u)

        block = ctx.enter_context(nc.Block())
        CH_MIX = BCH * len(BLOCKS)
        PER_C = BCH + 2 * (A_HEADS // CT)
        CH_MERGE = CH_MIX + PER_C * NC
        CHUNKS = CH_MERGE + BCH * NC
        after_step = {x: s for s in STEPS for x in FILL[s]}

        class Splitter:

            def __init__(self, split, evacuate):
                self.x, self.split, self.evacuate = 0, split, evacuate
                for i in range(NSPLIT):
                    split(i)

            def follow(self, end):
                while self.x < end:
                    if self.x + NSPLIT < CHUNKS:
                        self.split(self.x + NSPLIT)
                    self.x += 1
                    if self.x % BCH == 0 and self.x <= CH_MIX:
                        self.evacuate(self.x // BCH - 1)

            def before(self, step, most=CHUNKS):
                i, n = STEPS.index(step), 0
                while (self.x < CH_MIX and n < most
                       and (self.x not in after_step or STEPS.index(after_step[self.x]) < i)):
                    self.follow(self.x + 1)
                    n += 1

        @block.sync
        def _(sp):
            sp.dma_start(xs0[:, 0, :], x_v[:, 0, :]).then_inc(sem("x_in0"), 16)
            sp.dma_start(xs0[:, 1, :], x_v[:, 1, :]).then_inc(sem("x_in1"), 16)

            def load(x, src):
                if x >= RING_A:
                    sp.wait_ge(sem("w_lo"), x - RING_A + 1)
                sp.dma_start(ringA[:, x % RING_A, :].rearrange("p (k n) -> p k n", k=CT), src)\
                    .then_inc(sem(f"raw{x % RING_A}"), 16)

            x = 0
            for _, _, c in BLOCKS:
                for h in range(BCH):
                    load(x, win_v[:, h * CT:(h + 1) * CT, c:c + CB])
                    x += 1
            for c in range(NC):
                for h in range(BCH):
                    load(x, win_v[:, h * CT:(h + 1) * CT, C_MB + c * CB:C_MB + (c + 1) * CB])
                    x += 1
                for v in (woa_v, wob_v):
                    for h in range(A_HEADS // CT):
                        load(x, v[:, h * CT:(h + 1) * CT, c * CB:(c + 1) * CB])
                        x += 1
            for c in range(NC):
                if c == 1:
                    wait(sp, ("o_lo", 2))
                    for m in range(NM):
                        sp.dma_start(x1[:, m, :], x_v[:, m, :]).then_inc(sem("x_back"), 16)
                for h in range(BCH):
                    load(x, wout_v[:, h * CT:(h + 1) * CT, c * CB:(c + 1) * CB])
                    x += 1
            assert x == CHUNKS
            wait(sp, ("mT", 8))
            sp.sem_inc(sem("slotM_free"), RING_M - 1)
            wait(sp, ("rounds_ready", 1))
            rounds = sp.value_load(rounds_i[0:1, 0:1], min_val=1, max_val=SEQ // CAP)
            with sp.Fori(0, rounds) as r:
                with sp.Fori(0, PAIRS) as p:
                    n = r * PAIRS + p
                    j = 0
                    for v in (w1_v, w3_v):
                        for h in range(2):
                            for e in range(2):
                                sp.wait_ge(sem("slotM_free"), n * PER_PAIR + j + 1)
                                sp.dma_start(ringM[:, j % RING_M, :],
                                             v[bass.ds(p * 2 + e, 1), :, h * SLOT:(h + 1) * SLOT]
                                             .rearrange("a p n -> (a p) n")).then_inc(sem(f"slotM{j % RING_M}"), 16)
                                j += 1
                    for h in range(2):
                        for e in range(2):
                            sp.wait_ge(sem("slotM_free"), n * PER_PAIR + j + 1)
                            sp.dma_start(ringM[:, j % RING_M, :].rearrange("p (t n) -> p t n", t=FT),
                                         w2_v[bass.ds(p * 2 + e, 1), :, :, h * (D // 2):(h + 1) * (D // 2)]
                                         .rearrange("a p t n -> (a p) t n")).then_inc(sem(f"slotM{j % RING_M}"), 16)
                            j += 1
            wait(sp, ("y_ready", 2))
            sp.dma_start(y_v, x1[:, :, :]).then_inc(sem("y_out"), 16)
            sp.wait_ge(sem("y_out"), 16)

        @block.gpsimd
        def _(pool):
            def small(dst, src, name):
                pool.dma_start(dst, src, allow_slow_non_contiguous=True).then_inc(sem(name), 16)

            small(nmix, norm_mix[0].rearrange("(p k) -> p k", k=KT), "nmix_in")
            w3d = wsm[:, 0:KT * NSM].rearrange("p (k c) -> p k c", k=KT)
            small(w3d[:, :, 0:2 * A_HEADS], win_v[:, :, C_BETA:C_BETA + 2 * A_HEADS], "small_in")
            small(w3d[:, :, 2 * A_HEADS:NSM], win_v[:, :, C_LR:C_LR + RANK], "small_in")
            small(convw, conv_a[0], "small_in")
            small(T_["wgk2"][0:RANK, :], w_gk2[0], "small_in")
            small(dtb, dt_bias[0].partition_broadcast(P), "small_in")
            small(alog, a_log[0].partition_broadcast(P), "small_in")
            small(bgk, b_gk[0].rearrange("(h p) -> p h", p=P), "small_in")
            small(anorm, a_norm[0].rearrange("(p a) -> p a", a=1), "small_in")
            small(bnorm, b_norm[0].rearrange("(h p) -> p h", p=P), "small_in")
            small(nffn, norm_ffn[0].rearrange("(p k) -> p k", k=KT), "small_in")
            small(brg, b_rg[0].partition_broadcast(P), "small_in")
            small(bre, b_re[0].rearrange("g e -> (g e)").partition_broadcast(P), "small_in")

            links = [0]

            def link(ins):
                links[0] += 1
                ins.then_inc(sem("pool_link"), 1)
                pool.wait_ge(sem("pool_link"), links[0])

            nc.gpsimd.memset(ident, 0.0)
            nc.gpsimd.memset(ones, 1.0)
            nc.gpsimd.memset(pw, -0.5)
            link(nc.gpsimd.memset(upT, 1.0))
            nc.gpsimd.affine_select(out=ident, in_=ident, compare_op=ALU.not_equal, fill=1.0, base=0,
                                    pattern=[[-1, P]], channel_multiplier=1).then_inc(sem("ident"), 1)
            link(nc.gpsimd.affine_select(out=upT, in_=upT, compare_op=ALU.is_ge, fill=0.0, base=0,
                                         pattern=[[1, P]], channel_multiplier=-1))
            def masks(upper):
                for b in LEVELS:
                    i = nc.gpsimd.memset(mask[b], 1.0)
                link(i)
                for part in range(2):
                    for b in LEVELS:
                        mb = P // (2 * b)
                        if upper:
                            base, st = ((-1000, [[-2 * b, mb], [1000, 2], [0, b]]) if part == 0
                                        else (b - 1, [[2 * b, mb], [0, 2], [0, b]]))
                        else:
                            base, st = ((-b, [[-2 * b, mb], [-1000, 2], [0, b]]) if part == 0
                                        else (2 * b - 1, [[2 * b, mb], [0, 2], [0, b]]))
                        v = mask[b].rearrange("p (m s r) -> p m s r", s=2, r=b)
                        i = nc.gpsimd.affine_select(out=v, in_=v, compare_op=ALU.is_ge, fill=0.0, base=base,
                                                    pattern=st, channel_multiplier=1 - 2 * part)
                    link(i)

            masks(upper=True)
            nc.gpsimd.iota(iota, pattern=[[1, CAP]], base=0, channel_multiplier=0,
                           allow_small_or_imprecise_dtypes=True).then_inc(sem("consts"), 1)

            wait(pool, ("ss1", 2))
            link(nc.gpsimd.tensor_scalar(ss1, ss1, 1.0 / D, EPS, ALU.mult, ALU.add))
            link(nc.gpsimd.tensor_tensor(rstd, ss1, pw[:, 0:NM], ALU.pow))
            nc.gpsimd.tensor_scalar(rstdh, rstd, 0.5, None, ALU.mult).then_inc(sem("rstd"), 1)

            wait(pool, ("b_ms", 1))
            nc.gpsimd.tensor_tensor(rmf[:, 0:8], rms[:, 0:8], pw[:, 0:8], ALU.pow).then_inc(sem("b_rf"), 1)

            wait(pool, ("attn", len(LEVELS)))
            masks(upper=False)
            for g in range(NG):
                if g == 0:
                    wait(pool, ("obT", 2))
                    wait(pool, ("gdec", 1))
                else:
                    wait(pool, ("oaT", g))
                for h in range(GH):
                    for n in range(NM):
                        u = h * NM + n
                        i = nc.gpsimd.tensor_scalar(T_["gB"][:, u * P:(u + 1) * P], ones,
                                                    mh(gdec)[:, n, g * GH + h:g * GH + h + 1], None, ALU.mult)
                i.then_inc(sem("gB"), 1)
                wait(pool, ("expD", g + 1))
                Dm = units(T_["Dm"])
                bv = mh(beta)[:, :, g * GH:(g + 1) * GH].rearrange("p n h -> p h n").unsqueeze(3)\
                    .to_broadcast([P, GH, NM, P])
                nc.gpsimd.tensor_tensor(T_["Dm"].rearrange("p (h n t) -> p h n t", h=GH, n=NM),
                                        T_["Dm"].rearrange("p (h n t) -> p h n t", h=GH, n=NM), bv,
                                        ALU.mult).then_inc(sem("DA"), 1)
                wait(pool, ("expDT", g + 1))
                nc.gpsimd.tensor_tensor(units(T_["DT"]), units(T_["DT"]),
                                        upT.unsqueeze(1).to_broadcast([P, GU, P]), ALU.mult)\
                    .then_inc(sem("DTm"), 1)
                wait(pool, ("ssqk", g + 1))
                nc.gpsimd.tensor_tensor(rqk, ssqk, pw, ALU.pow).then_inc(sem("rqk"), 1)
                wait(pool, ("ktok", g + 1))
                k4 = T_["zT0"][:, 0:1024].rearrange("p (h n t) -> p h n t", h=GH, n=NM)
                nc.gpsimd.tensor_tensor(T_["kbg"].rearrange("p (h n t) -> p h n t", h=GH, n=NM), k4,
                                        mh(beg)[:, :, g * GH:(g + 1) * GH].rearrange("p n h -> p h n")
                                        .unsqueeze(3).to_broadcast([P, GH, NM, P]), ALU.mult).then_inc(sem("kbg"), 1)
                nc.gpsimd.tensor_tensor(units(T_["kdec"], GH), k4[:, :, 0, :],
                                        mh(ekd)[:, 0, g * GH:(g + 1) * GH].unsqueeze(2).to_broadcast([P, GH, P]),
                                        ALU.mult).then_inc(sem("kdec"), 1)
                wait(pool, ("A", g + 1))
                wait(pool, full(f"gcb.{g}"))
                for i, b in enumerate(LEVELS):
                    if i >= 2:
                        wait(pool, full(f"Y{LEVELS[i - 2]}.{g}"))
                        if i == 2:
                            wait(pool, ("T", g * 6 + 1))
                    dst = T_["gB"] if i % 2 == 0 else T_["L1"]
                    nc.gpsimd.tensor_tensor(units(dst), units(T_["Dm"]),
                                            mask[b].unsqueeze(1).to_broadcast([P, GU, P]), ALU.mult)\
                        .then_inc(sem("L"), 1)
                wait(pool, ("a_ms", g + 1))
                link(nc.gpsimd.tensor_scalar(rqk[:, 0:8], rqk[:, 0:8], QSCALE, None, ALU.mult))
                link(nc.gpsimd.tensor_tensor(rms[:, 0:8], rms[:, 0:8], rqk[:, 0:8], ALU.mult))
                link(nc.gpsimd.tensor_tensor(rms[:, 0:8], rms[:, 0:8], rqk[:, 0:8], ALU.mult))
                link(nc.gpsimd.tensor_scalar(rms[:, 0:8], rms[:, 0:8], 1.0 / A_D, EPS, ALU.mult, ALU.add))
                link(nc.gpsimd.tensor_tensor(rmf[:, 0:8], rms[:, 0:8], pw[:, 0:8], ALU.pow))
                nc.gpsimd.tensor_tensor(rmf[:, 0:8], rmf[:, 0:8], rqk[:, 0:8], ALU.mult).then_inc(sem("a_rf"), 1)

            wait(pool, ("zs", 1))
            wr = wsm.rearrange("p (k c) -> p k c", k=KT)
            small(wr[:, :, 0:GROUPS], w_rg[0].rearrange("(p k) g -> p k g", k=KT), "wr_in")
            small(wr[:, :, GROUPS:GROUPS + NE], w_re[0].rearrange("(p k) g e -> p k (g e)", k=KT), "wr_in")
            wait(pool, ("x1", 2 * NC))
            small(nfin, norm_final.partition_broadcast(P), "nfin_in")
            wait(pool, ("ss2", 2))
            link(nc.gpsimd.tensor_scalar(ss2, ss2, 1.0 / D, EPS, ALU.mult, ALU.add))
            nc.gpsimd.tensor_tensor(rstd2, ss2, pw[:, 0:NM], ALU.pow).then_inc(sem("rstd2"), 1)

            wait(pool, ("rounds_ready", 1))
            rounds = pool.value_load(rounds_i[0:1, 0:1], min_val=1, max_val=SEQ // CAP)
            s4 = sel.rearrange("p (m e s) -> p m e s", m=NM, e=2)
            g4 = selg.rearrange("p (m e s) -> p m e s", m=NM, e=2)
            io = iota.unsqueeze(1).to_broadcast([P, 2, CAP])
            with pool.Fori(0, rounds) as r:
                with pool.Fori(0, PAIRS) as p:
                    n = r * PAIRS + p
                    pool.wait_ge(sem("combT"), n + 1)
                    for m in range(NM):
                        i = nc.gpsimd.tensor_tensor(
                            s4[:, m], io, pos[:, bass.ds(m * NE + 2 * p, 2)].unsqueeze(2).to_broadcast([P, 2, CAP]),
                            ALU.subtract)
                    pool.drain()
                    nc.gpsimd.tensor_scalar(sel, sel, 0.0, None, ALU.is_equal).then_inc(sem("sel"), 1)
                    pool.wait_ge(sem("sel"), n + 1)
                    for m in range(NM):
                        i = nc.gpsimd.tensor_tensor(
                            g4[:, m], s4[:, m],
                            Wt[:, bass.ds(m * NE + 2 * p, 2)].unsqueeze(2).to_broadcast([P, 2, CAP]), ALU.mult)
                    i.then_inc(sem("selg"), 1)
                pool.drain()
                nc.gpsimd.tensor_scalar(pos, pos, float(-CAP), None, ALU.add)
                pool.drain()
            wait(pool, ("ss3", 2))
            link(nc.gpsimd.tensor_scalar(ss2, ss2, 1.0 / D, EPS, ALU.mult, ALU.add))
            nc.gpsimd.tensor_tensor(rstd2, ss2, pw[:, 0:NM], ALU.pow).then_inc(sem("rstd3"), 1)

        @block.scalar
        def _(act):
            def high(x):
                act.wait_ge(sem(f"raw{x % RING_A}"), 16 * (x // RING_A + 1))
                if x >= NSPLIT:
                    act.wait_ge(sem("chunk"), x - NSPLIT + 1)
                nc.scalar.activation(w_hi[x % NSPLIT], ringA[:, x % RING_A, :], ACT.Copy).then_inc(sem("w_hi"), 1)

            def evac(b):
                which, i, _ = BLOCKS[b]
                act.wait_ge(sem("chunk"), BCH * (b + 1))
                if b == 0:
                    wait(act, ("rstd", 1))
                if which == "gdn1" and i == 0:
                    wait(act, ("obT", 2))
                if which == "gate" and i == 0:
                    wait(act, ("oaT", 1))
                dst = zsl(which, i)
                for m in range(NM):
                    if which == "gate":
                        j = nc.scalar.activation(dst[:, m, :], bank(2 * (b % 2) + m), ACT.Tanh,
                                                 scale=rstdh[:, m:m + 1])
                    else:
                        j = nc.scalar.activation(dst[:, m, :], bank(2 * (b % 2) + m), ACT.Copy,
                                                 scale=rstd[:, m:m + 1])
                j.then_inc(sem("z"), 1)

            def result(step):
                sp_.before(step)
                wait(act, full(step))

            for m in range(NM):
                act.wait_ge(sem(f"x_in{m}"), 16)
                nc.scalar.activation(Z1[:, m * D:(m + 1) * D], xs0[:, m, :], ACT.Square,
                                     accum_out=ss1[:, m:m + 1]).then_inc(sem("ss1"), 1)
            act.wait_ge(sem("nmix_in"), 16)
            for i in range(8):
                act.wait_ge(sem("xTp"), i + 1)
                for k in range(2):
                    j = nc.scalar.activation(hTh[:, 2 * i + k, :], bank(i)[:, k * SEQ:(k + 1) * SEQ], ACT.Copy,
                                             scale=nmix[:, 2 * i + k:2 * i + k + 1])
                j.then_inc(sem("hTh"), 1)
            sp_ = Splitter(high, evac)
            act.wait_ge(sem("small_in"), SMALL)
            sp_.follow(FIRST_BLOCKS * BCH)
            result("small")
            zp = pair("small")[:, 0:NM * NSM].rearrange("p (m c) -> p m c", m=NM)
            for m in range(NM):
                i = nc.scalar.activation(zs3[:, m, :], zp[:, m, :], ACT.Copy, scale=rstd[:, m:m + 1])
            i.then_inc(sem("zs"), 1)
            act.wait_ge(sem("zs"), 1)
            nc.scalar.activation(mh(beta), zs3[:, :, 0:A_HEADS], ACT.Tanh, scale=0.5).then_inc(sem("tbeta"), 1)
            result("blrT")
            nc.scalar.activation(T_["blrT"][0:RANK, :], pair("blrT")[0:RANK, 0:SEQ], ACT.Copy)\
                .then_inc(sem("blrT"), 1)
            wait(act, ("na", 1))
            nc.scalar.activation(na, na, ACT.Exp).then_inc(sem("ena"), 1)
            nc.scalar.activation(alog, alog, ACT.Exp).then_inc(sem("ealog"), 1)
            act.wait_ge(sem("ena"), 1)
            nc.scalar.activation(na, na, ACT.Ln, bias=1.0).then_inc(sem("lna"), 1)
            sp_.before("gc")
            wait(act, ("gcol", 1))
            nc.scalar.activation(eg, gcol, ACT.Exp).then_inc(sem("eg"), 1)
            nc.scalar.activation(ekd, gdif, ACT.Exp).then_inc(sem("ekd"), 1)
            sp_.before("gkT")
            wait(act, ("gkn", 1))
            nc.scalar.activation(T_["bE"], T_["bE"], ACT.Exp).then_inc(sem("gke"), 1)
            act.wait_ge(sem("gke"), 1)
            nc.scalar.activation(T_["bE"], T_["bE"], ACT.Ln, bias=1.0).then_inc(sem("gkl"), 1)
            result("bqT")
            nc.scalar.activation(T_["bqT"], pair("bqT"), ACT.Copy, scale=QSCALE).then_inc(sem("bqT"), 1)
            for i, b in enumerate(LEVELS):
                sp_.before("lv_eye" if i < 2 else f"lv{LEVELS[i - 2]}")
                wait(act, ("bdist", i + 1))
                nc.scalar.activation(T_["bE"], T_["bE"], ACT.Exp, scale=1.0 / GATE_NORM).then_inc(sem("bE"), 1)
            sp_.before("lv64")
            wait(act, ("bedge", 1))
            nc.scalar.activation(T_["bE"], T_["bE"], ACT.Exp, scale=1.0 / GATE_NORM).then_inc(sem("bE"), 1)
            result("kd")
            nc.scalar.activation(T_["kdtok"], pair("kd")[:, 0:512], ACT.Copy).then_inc(sem("kdtok"), 1)
            result("bS")
            nc.scalar.activation(T_["bS"], pair("bS"), ACT.Copy).then_inc(sem("bS"), 1)
            bg = Z1[:, 4 * 1024:6 * 1024]
            nc.scalar.activation(T_["bth"], bg, ACT.Tanh, scale=0.5).then_inc(sem("bth"), 1)
            for i in range(2):
                result(f"bo{i}")
                nc.scalar.activation(T_["bo"][:, i * 1024:(i + 1) * 1024], pair(f"bo{i}"), ACT.Copy)\
                    .then_inc(sem("b_o"), 1)
            act.wait_ge(sem("b_o"), 2)
            wait(act, ("edge", 1))
            nc.scalar.activation(T_["bqT"], T_["bo"][:, 0:1024], ACT.Square)
            nc.scalar.activation(T_["bkT"], T_["bo"][:, 1024:2048], ACT.Square).then_inc(sem("b_sq"), 1)

            for g in range(NG):
                s = f".{g}"
                zg = [T_[f"zT{i}"][:, 0:zpad].rearrange("p (h t) -> p h t", h=GH) for i in range(3)]
                Zb = Z0 if g == 0 else Z1
                c = [Zb[:, i * 1024:(i + 1) * 1024] for i in range(3)]
                for i, w in ((0, "zqT"), (2, "zvT")):
                    result(w + s)
                    nc.scalar.activation(zg[i][:, :, TAPS - 1:], pair(w + s).rearrange("p (h t) -> p h t", h=GH),
                                         ACT.Copy).then_inc(sem(w), 1)
                for i in range(3):
                    sp_.before("ssq" + s, most=2)
                    act.wait_ge(sem("conv"), 3 * g + i + 1)
                    nc.scalar.activation(T_[f"zT{i}"][:, 0:1024], c[i], ACT.Tanh, scale=0.5).then_inc(sem("tconv"), 1)
                wait(act, ("Dn", g + 1))
                nc.scalar.activation(T_["Dm"], T_["Dm"], ACT.Exp, scale=-1.0).then_inc(sem("expD"), 1)
                wait(act, ("DTn", g + 1))
                nc.scalar.activation(T_["DT"], T_["DT"], ACT.Exp).then_inc(sem("expDT"), 1)
                for i in range(2):
                    act.wait_ge(sem("silu"), 3 * g + i + 1)
                    nc.scalar.activation(T_[f"zT{i}"][:, 0:1024], c[i], ACT.Square).then_inc(sem("sq"), 1)
                result("khT" + s)
                nc.scalar.activation(T_["zT1"][:, 0:1024], pair("khT" + s), ACT.Copy).then_inc(sem("khT"), 1)
                for i, b in enumerate(LEVELS[1:]):
                    result(f"Y{b}" + s)
                    nc.scalar.activation(T_["Y"], pair(f"Y{b}" + s), ACT.Copy).then_inc(sem("Y"), 1)
                result("wT" + s)
                nc.scalar.activation(T_["nwT"], pair("wT" + s)[:, 0:512], ACT.Copy, scale=-1.0)\
                    .then_inc(sem("wT"), 1)
                result("u0" + s)
                vn = units(T_["T"])
                nc.scalar.activation(T_["T"][:, 0:512], pair("u0" + s)[:, 0:512], ACT.Copy).then_inc(sem("u0"), 1)
                result("S" + s)
                nc.scalar.activation(T_["aS"], pair("S" + s)[:, 0:512], ACT.Copy).then_inc(sem("a_S"), 1)
                result("v1" + s)
                nc.scalar.activation(T_["T"][:, 512:1024], pair("v1" + s)[:, 0:512], ACT.Copy).then_inc(sem("v1"), 1)
                nc.scalar.activation(T_["L1"], Zb[:, 3 * 1024:4 * 1024], ACT.Tanh, scale=0.5).then_inc(sem("tz"), 1)
                sp_.before("o" + s)
                wait(act, ("a_o", g + 1))
                nc.scalar.activation(T_["zT1"][:, 0:1024], T_["Y"], ACT.Square).then_inc(sem("a_sq"), 1)

            sp_.before(STEPS[-1])
            sp_.follow(CH_MIX)
            wait(act, ("oaT", NG))
            for i, o in enumerate((oaT_f, obT_f)):
                nc.scalar.activation(o_hi[i], o, ACT.Copy).then_inc(sem("o_hi"), 1)
            for c in range(NC):
                sp_.follow(CH_MIX + PER_C * c + BCH)
                act.wait_ge(sem("chunk"), CH_MIX + PER_C * c + BCH)
                if c:
                    wait(act, ("merged", c))
                for m in range(NM):
                    i = nc.scalar.activation(tb[:, m, :], bank(m), ACT.Tanh, scale=rstdh[:, m:m + 1])
                i.then_inc(sem("tb"), 1)
                sp_.follow(CH_MIX + PER_C * (c + 1))
            for i in range(8):
                act.wait_ge(sem("mTp"), i + 1)
                nc.scalar.activation(hTh[:, 2 * i:2 * i + 2, :].rearrange("p k t -> p (k t)"), bank(i), ACT.Copy,
                                     scale=0.5).then_inc(sem("mTh"), 1)
            sp_.follow(CHUNKS)
            for m in range(NM):
                act.wait_ge(sem("x1"), 2 * NC)
                nc.scalar.activation(junk, x1[:, m, :], ACT.Square, accum_out=ss2[:, m:m + 1])\
                    .then_inc(sem("ss2"), 1)
                act.wait_ge(sem("ss2"), m + 1)
            wait(act, ("rstd2", 1))
            for m in range(NM):
                nc.scalar.activation(h2[:, m, :], x1[:, m, :], ACT.Copy, scale=rstd2[:, m:m + 1])\
                    .then_inc(sem("h2"), 1)
            wait(act, ("r_d", 1))
            nc.scalar.activation(rt["ed"], rt["d"], ACT.Exp).then_inc(sem("r_ed"), 1)
            wait(act, ("r_dm", 1))
            nc.scalar.activation(rt["e2"], rt["dm"], ACT.Exp).then_inc(sem("r_e2"), 1)

            wait(act, ("rounds_ready", 1))
            rounds = act.value_load(rounds_i[0:1, 0:1], min_val=1, max_val=SEQ // CAP)
            with act.Fori(0, rounds) as r:
                with act.Fori(0, PAIRS) as p:
                    n = r * PAIRS + p
                    act.wait_ge(sem("combT"), n + 2)
                    nc.scalar.activation(comb, bank(2, SEQ), ACT.Copy).then_inc(sem("comb"), 1)
                    act.wait_ge(sem("slotM_free"), n * PER_PAIR + RING_M + 4)
                    nc.scalar.activation(hth, bank(0), ACT.Tanh, scale=0.5).then_inc(sem("hth"), 1)
                    act.wait_ge(sem("actT"), n + 1)
                    nc.scalar.activation(aT, bank(3), ACT.Copy).then_inc(sem("aT"), 1)
                    for k in range(NC):
                        if k % 2 == 0:
                            act.wait_ge(sem("down"), n * 2 + k // 2 + 1)
                        else:
                            act.wait_ge(sem("slotM_free"), n * PER_PAIR + RING_M + 8 + k + 1)
                        nc.scalar.activation(Ysb[:, k * CB:(k + 1) * CB], bank(4 + k % 2), ACT.Copy)\
                            .then_inc(sem("yev"), 1)
            act.wait_ge(sem("loop_done"), 1)
            for m in range(NM):
                nc.scalar.activation(junk, x1[:, m, :], ACT.Square, accum_out=ss2[:, m:m + 1])\
                    .then_inc(sem("ss3"), 1)
                act.wait_ge(sem("ss3"), m + 1)

        @block.vector
        def _(dve):
            links = [0]

            def link(ins):
                links[0] += 1
                ins.then_inc(sem("dve_link"), 1)
                dve.wait_ge(sem("dve_link"), links[0])

            tt = nc.vector.tensor_tensor
            ts = nc.vector.tensor_scalar
            stt = nc.vector.scalar_tensor_tensor

            def low(x):
                dve.wait_ge(sem("w_hi"), x + 1)
                tt(w_lo[x % NSPLIT], ringA[:, x % RING_A, :], w_hi[x % NSPLIT].bitcast(F32), ALU.subtract)\
                    .then_inc(sem("w_lo"), 1)

            def result(step):
                sp_.before(step)
                wait(dve, full(step))

            dve.wait_ge(sem("nmix_in"), 16)
            for i in range(8):
                dve.wait_ge(sem("hTh"), i + 1)
                for k in range(2):
                    j = stt(hTl[:, 2 * i + k, :], bank(i)[:, k * SEQ:(k + 1) * SEQ], nmix[:, 2 * i + k:2 * i + k + 1],
                            hTh[:, 2 * i + k, :].bitcast(F32), ALU.mult, ALU.subtract)
                j.then_inc(sem("hTl"), 1)
            sp_ = Splitter(low, lambda b: None)
            sp_.follow(FIRST_BLOCKS * BCH)
            result("cw")
            nc.vector.tensor_copy(cw, pair("cw")[:, 0:96]).then_inc(sem("cw"), 1)
            dve.wait_ge(sem("small_in"), SMALL)
            wait(dve, ("zs", 1))
            link(tt(mh(xa), zs3[:, :, A_HEADS:2 * A_HEADS], dtb.unsqueeze(1).to_broadcast([P, NM, A_HEADS]), ALU.add))
            stt(na, xa, -1.0, xa, ALU.mult, ALU.min).then_inc(sem("na"), 1)
            wait(dve, ("tbeta", 1))
            link(ts(beta, beta, 0.5, 0.5, ALU.mult, ALU.add))
            ts(bhalf, beta, 0.5, None, ALU.mult)
            wait(dve, ("lna", 1))
            link(stt(xa, xa, 0.0, na, ALU.max, ALU.add))
            link(tt(mh(xa), mh(xa), alog.unsqueeze(1).to_broadcast([P, NM, A_HEADS]), ALU.mult))
            ts(gdec, xa, -1.0, None, ALU.mult).then_inc(sem("gdec"), 1)
            result("gc")
            link(nc.vector.tensor_copy(gcol, pair("gc")[:, 0:half16]))
            tt(gdif, pair("gc")[:, half16:2 * half16], gcol, ALU.subtract).then_inc(sem("gcol"), 1)
            wait(dve, ("eg", 1))
            tt(beg, beta, eg, ALU.mult).then_inc(sem("beg"), 1)
            result("gkT")
            dve.wait_ge(sem("small_in"), SMALL)
            b4 = T_["bT"].rearrange("p (h t) -> p h t", h=B_HEADS)
            tt(b4, pair("gkT").rearrange("p (h t) -> p h t", h=B_HEADS),
               bgk.unsqueeze(2).to_broadcast([P, B_HEADS, SEQ]), ALU.add).then_inc(sem("gkx"), 1)
            dve.wait_ge(sem("gkx"), 1)
            stt(T_["bE"], T_["bT"], -1.0, T_["bT"], ALU.mult, ALU.min).then_inc(sem("gkn"), 1)
            wait(dve, ("gkl", 1))
            link(stt(T_["bE"], T_["bT"], 0.0, T_["bE"], ALU.min, ALU.subtract))
            for u in range(GU):
                sl = slice(u * P, (u + 1) * P)
                i = nc.vector.tensor_tensor_scan(T_["bT"][:, sl], ones, T_["bE"][:, sl], 0.0, ALU.mult, ALU.add)
            link(i)
            result("bkT")
            nc.vector.tensor_copy(T_["bkT"], pair("bkT")).then_inc(sem("bkT"), 1)
            result("lv_eye")
            tt(units(T_["attn"]), units(pair("lv_eye")), ident.unsqueeze(1).to_broadcast([P, GU, P]), ALU.mult)\
                .then_inc(sem("attn_tmp"), 1)
            qm, km = Z1[:, 0:1024], Z1[:, 1024:2048]
            nc.vector.memset(qm, 0.0)
            link(nc.vector.memset(km, 0.0))
            dve.wait_ge(sem("bqT"), 1)
            dve.wait_ge(sem("bkT"), 1)

            def add_level(i):
                b = LEVELS[i]
                result(f"lv{b}")
                tt(units(T_["btmp"]), units(pair(f"lv{b}")), mask[b].unsqueeze(1).to_broadcast([P, GU, P]), ALU.mult)\
                    .then_inc(sem("attn_tmp"), 1)
                dve.wait_ge(sem("attn_tmp"), i + 2)
                tt(T_["attn"], T_["attn"], T_["btmp"], ALU.add).then_inc(sem("attn"), 1)
                dve.wait_ge(sem("attn"), i + 1)

            for i, b in enumerate(LEVELS):
                nb = 1024 // (2 * b)

                def halves(t):
                    v = t.rearrange("p (m s r) -> p m s r", s=2, r=b)
                    return v[:, :, 0, :], v[:, :, 1, :]

                (blo, bup), (elo, eup) = halves(T_["bT"]), halves(T_["bE"])
                ref = blo[:, :, b - 1:b].to_broadcast([P, nb, b])
                if i:
                    dve.wait_ge(sem("qkm"), i)
                tt(elo, ref, blo, ALU.subtract)
                tt(eup, bup, ref, ALU.subtract).then_inc(sem("bdist"), 1)
                dve.wait_ge(sem("bE"), i + 1)
                if i:
                    wait(dve, full(f"lv{LEVELS[i - 1]}"))
                tt(halves(km)[0], halves(T_["bkT"])[0], elo, ALU.mult)
                tt(halves(qm)[1], halves(T_["bqT"])[1], eup, ALU.mult).then_inc(sem("qkm"), 1)
                if i:
                    add_level(i - 1)
            add_level(len(LEVELS) - 1)
            bu = T_["bT"].rearrange("p (h n t) -> p h n t", h=B_HEADS, n=NM)
            eu = T_["bE"].rearrange("p (h n t) -> p h n t", h=B_HEADS, n=NM)
            dve.wait_ge(sem("qkm"), len(LEVELS))
            nc.vector.tensor_copy(eu[:, :, 1, :], bu[:, :, 1, :])
            tt(eu[:, :, 0, :], bu[:, :, 0, P - 1:P].to_broadcast([P, B_HEADS, P]), bu[:, :, 0, :], ALU.subtract)\
                .then_inc(sem("bedge"), 1)
            dve.wait_ge(sem("bE"), 8)
            tt(units(T_["kdT"], B_HEADS), T_["bkT"].rearrange("p (h n t) -> p h n t", h=B_HEADS, n=NM)[:, :, 0, :],
               eu[:, :, 0, :], ALU.mult)
            result("lv64")
            q4 = qm.rearrange("p (h n t) -> p h n t", h=B_HEADS, n=NM)
            tt(q4[:, :, 1, :], T_["bqT"].rearrange("p (h n t) -> p h n t", h=B_HEADS, n=NM)[:, :, 1, :],
               eu[:, :, 1, :], ALU.mult).then_inc(sem("edge"), 1)
            sp_.before("bS")
            dve.wait_ge(sem("bth"), 1)
            bg = Z1[:, 4 * 1024:6 * 1024]
            link(stt(T_["bth"], T_["bth"], 1.0, bg, ALU.add, ALU.mult))
            sp_.before("bo1")
            dve.wait_ge(sem("b_sq"), 1)
            nc.vector.reduce_sum(rms[:, 0:4], T_["bqT"].rearrange("p (h e) -> p h e", h=B_HEADS), axis=AX.X)
            link(nc.vector.reduce_sum(rms[:, 4:8], T_["bkT"].rearrange("p (h e) -> p h e", h=B_HEADS), axis=AX.X))
            ts(rms[:, 0:8], rms[:, 0:8], 1.0 / B_DV, EPS, ALU.mult, ALU.add).then_inc(sem("b_ms"), 1)
            wait(dve, ("b_rf", 1))
            o3 = T_["bo"].rearrange("p (u e) -> p u e", u=8)
            link(tt(o3, o3, rmf[:, 0:8].unsqueeze(2).to_broadcast([P, 8, B_DV]), ALU.mult))
            for n in range(NM):
                i = tt(T_["bo"][:, n * 1024:(n + 1) * 1024].rearrange("p (a c) -> p a c", a=2),
                       T_["bo"][:, n * 1024:(n + 1) * 1024].rearrange("p (a c) -> p a c", a=2),
                       T_["bth"].rearrange("p (a n c) -> p a n c", a=2, n=NM)[:, :, n, :], ALU.mult)
            i.then_inc(sem("b_out"), 1)
            dve.wait_ge(sem("small_in"), SMALL)
            for i in range(2):
                result(f"obT{i}")
                for hf in range(2):
                    src = pair(f"obT{i}").rearrange("p (h f t) -> p h f t", h=2, f=2)[:, :, hf, :]
                    dst = obT[:, 4 * i:4 * i + 4, :].rearrange("p (h f) t -> p h f t", f=2)[:, :, hf, :]
                    j = ts(dst, src, bnorm[:, hf:hf + 1], 0.5, ALU.mult, ALU.mult)
                j.then_inc(sem("obT"), 1)

            for g in range(NG):
                s = f".{g}"
                Zb = Z0 if g == 0 else Z1
                c = [Zb[:, i * 1024:(i + 1) * 1024] for i in range(3)]
                zg = [T_[f"zT{i}"][:, 0:zpad].rearrange("p (h t) -> p h t", h=GH) for i in range(3)]
                hs_g = slice(g * GH, (g + 1) * GH)

                def per_unit(t):
                    return mh(t)[:, :, hs_g].rearrange("p n h -> p h n").unsqueeze(3).to_broadcast([P, GH, NM, P])

                def u4(t):
                    return t.rearrange("p (h n t) -> p h n t", h=GH, n=NM)

                if g:
                    result(f"oaT.{g - 1}")
                for i in range(3):
                    nc.vector.memset(zg[i][:, :, 0:TAPS - 1], 0.0)
                result("zkT" + s)
                nc.vector.tensor_copy(zg[1][:, :, TAPS - 1:], pair("zkT" + s).rearrange("p (h t) -> p h t", h=GH))\
                    .then_inc(sem("zkT"), 1)
                result("gcb" + s)
                for what, op, dst in (("Dn", ALU.max, "Dm"), ("DTn", ALU.min, "DT")):
                    link(tt(u4(T_[dst]), u4(pair("gcb" + s)), per_unit(gcol), ALU.subtract))
                    i = ts(T_[dst], T_[dst], 0.0, None, op)
                    i.then_inc(sem(what), 1)
                nc.vector.memset(rms[:, 15:16], 0.0).then_inc(sem("gcb"), 1)
                cwv = cw.rearrange("p (w h k) -> p w h k", w=3, h=A_HEADS)
                for w, ev in ((0, "zqT"), (1, "zkT"), (2, "zvT")):
                    sp_.before("ssq" + s, most=2)
                    wait(dve, (ev, g + 1))
                    if w == 0:
                        result("zvT" + s)
                    c4 = c[w].rearrange("p (h t) -> p h t", h=GH)
                    for k in range(TAPS):
                        for h in range(GH):
                            wk = cwv[:, w, g * GH + h, k:k + 1]
                            src = zg[w][:, h, k:k + SEQ]
                            if k == 0:
                                i = ts(c4[:, h, :], src, wk, None, ALU.mult)
                            else:
                                i = stt(c4[:, h, :], src, wk, c4[:, h, :], ALU.mult, ALU.add)
                        if k < TAPS - 1:
                            link(i)
                    i.then_inc(sem("conv"), 1)
                for w in range(3):
                    dve.wait_ge(sem("tconv"), 3 * g + w + 1)
                    stt(c[w], T_[f"zT{w}"][:, 0:1024], 1.0, c[w], ALU.add, ALU.mult).then_inc(sem("silu"), 1)
                result("ssq" + s)
                ts(ssqk, pair("ssq" + s)[:, 0:16], 4 * EPS, None, ALU.add).then_inc(sem("ssqk"), 1)
                wait(dve, ("rqk", g + 1))
                result("ktok" + s)
                tt(units(T_["zT0"][:, 0:1024]), units(pair("ktok" + s)),
                   rqk[:, 8:16].unsqueeze(2).to_broadcast([P, GU, P]), ALU.mult).then_inc(sem("ktok"), 1)
                result("vtok" + s)
                tt(u4(T_["zT2"][:, 0:1024]), u4(pair("vtok" + s)), per_unit(bhalf), ALU.mult)\
                    .then_inc(sem("vtok"), 1)
                result("A" + s)
                wait(dve, ("DA", g + 1))
                tt(T_["Dm"], pair("A" + s), T_["Dm"], ALU.mult).then_inc(sem("A"), 1)
                result("PT" + s)
                wait(dve, ("DTm", g + 1))
                tt(T_["DT"], pair("PT" + s), T_["DT"], ALU.mult).then_inc(sem("PT"), 1)
                idb = ident.unsqueeze(1).to_broadcast([P, GU, P])
                result("Y1" + s)
                stt(units(T_["U"]), units(pair("Y1" + s)), -1.0, idb, ALU.mult, ALU.add).then_inc(sem("U"), 1)
                stt(units(T_["T"]), units(T_["gB"]), -1.0, idb, ALU.mult, ALU.add).then_inc(sem("T"), 1)
                for i, b in enumerate(LEVELS[1:]):
                    result(f"dU{b}" + s)
                    if b != 64:
                        result(f"dT{b}" + s)
                    dve.wait_ge(sem("U"), 7 * g + i + 1)
                    tt(T_["U"], T_["U"], pair(f"dU{b}" + s), ALU.subtract).then_inc(sem("U"), 1)
                    if b != 64:
                        dve.wait_ge(sem("T"), 6 * g + i + 1)
                        tt(T_["T"], T_["T"], pair(f"dT{b}" + s), ALU.subtract).then_inc(sem("T"), 1)
                result("oi" + s)
                tt(units(T_["inter"], GH), units(pair("oi" + s)[:, 0:512], GH),
                   mh(eg)[:, 1, hs_g].unsqueeze(2).to_broadcast([P, GH, P]), ALU.mult).then_inc(sem("inter"), 1)
                result("o" + s)
                nc.vector.tensor_copy(u4(T_["Y"])[:, :, 0, :], u4(pair("o" + s))[:, :, 0, :])
                dve.wait_ge(sem("inter"), g + 1)
                tt(u4(T_["Y"])[:, :, 1, :], u4(pair("o" + s))[:, :, 1, :], units(T_["inter"], GH), ALU.add)\
                    .then_inc(sem("a_o"), 1)
                dve.wait_ge(sem("tz"), g + 1)
                link(stt(T_["L1"], T_["L1"], 1.0, Zb[:, 3 * 1024:4 * 1024], ALU.add, ALU.mult))
                dve.wait_ge(sem("a_sq"), g + 1)
                nc.vector.reduce_sum(rms[:, 0:8], units(T_["zT1"][:, 0:1024]), axis=AX.X).then_inc(sem("a_ms"), 1)
                wait(dve, ("a_rf", g + 1))
                link(tt(units(T_["Y"]), units(T_["Y"]), rmf[:, 0:8].unsqueeze(2).to_broadcast([P, GU, P]), ALU.mult))
                tt(u4(T_["Y"]), u4(T_["Y"]), T_["L1"].rearrange("p (n h t) -> p h n t", h=GH, n=NM), ALU.mult)\
                    .then_inc(sem("a_out"), 1)
                if g == 0:
                    dve.wait_ge(sem("small_in"), SMALL)
                result("oaT" + s)
                ts(oaT[:, g * GH:(g + 1) * GH, :], pair("oaT" + s).rearrange("p (h t) -> p h t", h=GH), anorm, 0.5,
                   ALU.mult, ALU.mult).then_inc(sem("oaT"), 1)

            sp_.before(STEPS[-1])
            sp_.follow(CH_MIX)
            for i, o in enumerate((oaT_f, obT_f)):
                dve.wait_ge(sem("o_hi"), i + 1)
                tt(o_lo[i], o, o_hi[i].bitcast(F32), ALU.subtract).then_inc(sem("o_lo"), 1)
            for c in range(NC):
                cs = slice(c * CB, (c + 1) * CB)
                if c == 0:
                    dve.wait_ge(sem("z"), len(BLOCKS))
                sp_.follow(CH_MIX + PER_C * c + BCH + 2)
                dve.wait_ge(sem("chunk"), CH_MIX + PER_C * c + BCH + 2)
                for m in range(NM):
                    i = stt(gateA[:, m, cs], gateA[:, m, cs], 1.0, bank(2 + m), ALU.add, ALU.mult)
                i.then_inc(sem("gya"), 1)
                sp_.follow(CH_MIX + PER_C * (c + 1))
                dve.wait_ge(sem("chunk"), CH_MIX + PER_C * (c + 1))
                dve.wait_ge(sem("tb"), c + 1)
                for m in range(NM):
                    i = stt(tyb[:, m, :], tb[:, m, :], 1.0, bank(4 + m), ALU.add, ALU.mult)
                i.then_inc(sem("gyb"), 1)
                dve.wait_ge(sem("gyb"), c + 1)
                dve.wait_ge(sem("gya"), c + 1)
                tt(gateA[:, :, cs], gateA[:, :, cs], tyb, ALU.add).then_inc(sem("merged"), 1)
                dve.wait_ge(sem("merged"), c + 1)
            for i in range(8):
                dve.wait_ge(sem("mTh"), i + 1)
                stt(hTl[:, 2 * i:2 * i + 2, :].rearrange("p k t -> p (k t)"), bank(i), 0.5,
                    hTh[:, 2 * i:2 * i + 2, :].rearrange("p k t -> p (k t)").bitcast(F32), ALU.mult, ALU.subtract)\
                    .then_inc(sem("mT"), 1)
            for c in range(NC):
                cs = slice(c * CB, (c + 1) * CB)
                sp_.follow(CH_MERGE + BCH * (c + 1))
                dve.wait_ge(sem("chunk"), CH_MERGE + BCH * (c + 1))
                for m in range(NM):
                    if c == 0 and m == 0:
                        dve.wait_ge(sem("x_back"), 16 * NM)
                    tt(x1[:, m, cs], bank(2 * (c % 2) + m), x1[:, m, cs], ALU.add).then_inc(sem("x1"), 1)
            dve.wait_ge(sem("small_in"), SMALL)
            for i in range(8):
                dve.wait_ge(sem("h2Tp"), i + 1)
                tt(h2T[:, 2 * i:2 * i + 2, :], bank(i).rearrange("p (k t) -> p k t", k=2),
                   nffn[:, 2 * i:2 * i + 2].unsqueeze(2).to_broadcast([P, 2, SEQ]), ALU.mult).then_inc(sem("h2T"), 1)
            dve.wait_ge(sem("small_in"), SMALL)
            dve.wait_ge(sem("logits"), 1)
            R = GROUPS + NE
            lp = bank(0, NM * R).rearrange("p (m c) -> p m c", m=NM)

            def m_(t):
                return t.rearrange("p (m c) -> p m c", m=NM)

            def spread(t, n):
                return t.unsqueeze(2).to_broadcast([P, NM, n])

            def first(eq, cum, out, n):
                for m in range(NM):
                    i = nc.vector.tensor_tensor_scan(cum[:, m * n:(m + 1) * n], ones[:, 0:n], eq[:, m * n:(m + 1) * n],
                                                     0.0, ALU.mult, ALU.add)
                link(i)
                link(stt(out, cum, 1.0, eq, ALU.is_le, ALU.mult))

            tt(m_(rt["lg"]), lp[:, :, 0:GROUPS], brg.unsqueeze(1).to_broadcast([P, NM, GROUPS]), ALU.add)
            link(tt(m_(rt["le"]), lp[:, :, GROUPS:R], bre.unsqueeze(1).to_broadcast([P, NM, NE]), ALU.add))
            link(nc.vector.reduce_max(rt["gm"], m_(rt["lg"]), axis=AX.X))
            tt(m_(rt["d"]), m_(rt["lg"]), spread(rt["gm"], GROUPS), ALU.subtract).then_inc(sem("r_d"), 1)
            dve.wait_ge(sem("r_d"), 1)
            link(ts(rt["eq"][:, 0:8], rt["d"], 0.0, None, ALU.is_equal))
            first(rt["eq"][:, 0:8], rt["cum"][:, 0:8], rt["fg"], GROUPS)
            fg4 = m_(rt["fg"]).unsqueeze(3).to_broadcast([P, NM, GROUPS, EPG])

            def mge(t):
                return t.rearrange("p (m g e) -> p m g e", m=NM, g=GROUPS)

            link(tt(mge(rt["pr"]), mge(rt["le"]), fg4, ALU.mult))
            link(nc.vector.tensor_reduce(m_(rt["ls"]), rt["pr"].rearrange("p (m g e) -> p m e g", m=NM, g=GROUPS),
                                         AX.X, ALU.add))
            link(nc.vector.reduce_max(rt["m1"], m_(rt["ls"]), axis=AX.X))
            link(tt(m_(rt["d1"]), m_(rt["ls"]), spread(rt["m1"], EPG), ALU.subtract))
            link(ts(rt["eq"], rt["d1"], 0.0, None, ALU.is_equal))
            first(rt["eq"], rt["cum"], rt["f1"], EPG)
            link(stt(rt["ls2"], rt["f1"], NEG, rt["ls"], ALU.mult, ALU.add))
            link(nc.vector.reduce_max(rt["m2"], m_(rt["ls2"]), axis=AX.X))
            tt(rt["dm"], rt["m2"], rt["m1"], ALU.subtract).then_inc(sem("r_dm"), 1)
            link(tt(m_(rt["d2"]), m_(rt["ls2"]), spread(rt["m2"], EPG), ALU.subtract))
            link(ts(rt["eq"], rt["d2"], 0.0, None, ALU.is_equal))
            first(rt["eq"], rt["cum"], rt["f2"], EPG)
            link(tt(rt["fs"], rt["f1"], rt["f2"], ALU.add))
            tt(mge(Mt), m_(rt["fs"]).unsqueeze(2).to_broadcast([P, NM, GROUPS, EPG]), fg4, ALU.mult)\
                .then_inc(sem("Mt"), 1)
            dve.wait_ge(sem("r_ed"), 1)
            link(nc.vector.reduce_sum(rt["den"], m_(rt["ed"]), axis=AX.X))
            dve.wait_ge(sem("r_e2"), 1)
            link(ts(rt["s2"], rt["e2"], 1.0, None, ALU.add))
            link(tt(rt["s2"], rt["s2"], rt["den"], ALU.mult))
            link(nc.vector.reciprocal(rt["r2"], rt["s2"]))
            link(ts(rt["w1"], rt["r2"], 0.5, None, ALU.mult))
            link(tt(rt["w2"], rt["w1"], rt["e2"], ALU.mult))
            tt(m_(rt["ws"]), m_(rt["f1"]), spread(rt["w1"], EPG), ALU.mult)
            link(tt(m_(rt["wa"]), m_(rt["f2"]), spread(rt["w2"], EPG), ALU.mult))
            link(tt(rt["ws"], rt["ws"], rt["wa"], ALU.add))
            tt(mge(Wt), m_(rt["ws"]).unsqueeze(2).to_broadcast([P, NM, GROUPS, EPG]), fg4, ALU.mult)
            dve.wait_ge(sem("ranks"), 1)
            dve.wait_ge(sem("Mt"), 1)
            link(tt(pos, bank(1, NM * NE), Mt, ALU.mult))
            link(ts(pos, pos, 1.0, None, ALU.subtract))
            link(nc.vector.reduce_max(rt["mx"], bank(2, NE), axis=AX.X))
            ts(rt["c1"], rt["mx"], float(CAP), None, ALU.is_gt)
            ts(rt["c2"], rt["mx"], float(2 * CAP), None, ALU.is_gt)
            link(ts(rt["c3"], rt["mx"], float(3 * CAP), 1.0, ALU.is_gt, ALU.add))
            link(tt(rt["c1"], rt["c1"], rt["c2"], ALU.add))
            tt(rounds_i[:, :], rt["c1"], rt["c3"], ALU.add).then_inc(sem("rounds_ready"), 1)
            dve.wait_ge(sem("rounds_ready"), 1)

            rounds = dve.value_load(rounds_i[0:1, 0:1], min_val=1, max_val=SEQ // CAP)
            with dve.Fori(0, rounds) as r:
                with dve.Fori(0, PAIRS) as p:
                    n = r * PAIRS + p
                    for b in range(4):
                        dve.wait_ge(sem("gath"), n * 4 + b + 1)
                        tt(xeT[:, 4 * b:4 * b + 4, :], bank(2 + b % 2).rearrange("p (k s) -> p k s", k=4),
                           nffn[:, 4 * b:4 * b + 4].unsqueeze(2).to_broadcast([P, 4, P]), ALU.mult)\
                            .then_inc(sem("xe"), 1)
                    dve.wait_ge(sem("hth"), n + 1)
                    stt(hs, hth, 1.0, bank(0), ALU.add, ALU.mult).then_inc(sem("hs"), 1)
                    dve.wait_ge(sem("hs"), n + 1)
                    dve.wait_ge(sem("slotM_free"), n * PER_PAIR + RING_M + 8)
                    tt(hid, hs, bank(1), ALU.mult).then_inc(sem("hid"), 1)
                    for k in range(NC):
                        for m in range(NM):
                            dve.wait_ge(sem("cmb"), n * 8 + 2 * k + m + 1)
                            tt(x1[:, m, k * CB:(k + 1) * CB], x1[:, m, k * CB:(k + 1) * CB], bank(6 + m),
                               ALU.add).then_inc(sem("xadd"), 1)
            dve.wait_ge(sem("xadd"), rounds * (8 * PAIRS) + 2)
            nc.vector.memset(rt["c1"], 0.0).then_inc(sem("loop_done"), 1)
            dve.wait_ge(sem("nfin_in"), 16)
            wait(dve, ("rstd3", 1))
            for m in range(NM):
                stt(x1[:, m, :], x1[:, m, :], rstd2[:, m:m + 1], nfin, ALU.mult, ALU.mult).then_inc(sem("y_ready"), 1)

        @block.tensor
        def _(pe):
            mm, tr = nc.tensor.matmul, nc.tensor.transpose

            def done(step, ins):
                ins.then_inc(sem(full(step)[0]), 1)

            def open_pair(step):
                i = STEPS.index(step)
                if i >= 2:
                    wait(pe, drained(STEPS[i - 2]))

            def chunk(x, m_banks, lhs, k0, start, stop):
                pe.wait_ge(sem("w_lo"), x + 1)
                wh, wl = w_hi[x % NSPLIT], w_lo[x % NSPLIT]
                for m in range(NM):
                    for k in range(CT):
                        cs, ms = slice(k * CB, (k + 1) * CB), slice(m * P, (m + 1) * P)
                        mm(m_banks[m], lhs[0][:, k0 + k, ms], wh[:, cs], start=(start and k == 0), stop=False)
                        mm(m_banks[m], lhs[0][:, k0 + k, ms], wl[:, cs], start=False, stop=False)
                        i = mm(m_banks[m], lhs[1][:, k0 + k, ms], wh[:, cs], start=False,
                               stop=(stop and k == CT - 1))
                i.then_inc(sem("chunk"), 1)

            def project(x):
                b, h = divmod(x, BCH)
                if h == 0 and b >= 2:
                    pe.wait_ge(sem("z"), b - 1)
                chunk(x, (bank(2 * (b % 2)), bank(2 * (b % 2) + 1)), (hTh, hTl), h * CT, h == 0, h == BCH - 1)

            def fill(step):
                for x in FILL[step]:
                    project(x)

            pe.wait_ge(sem("ident"), 1)
            for m in range(NM):
                pe.wait_ge(sem(f"x_in{m}"), 16)
            for i in range(8):
                for k in range(2):
                    for m in range(NM):
                        j = tr(bank(i)[:, (k * NM + m) * P:(k * NM + m + 1) * P], xs0[:, m, 2 * i + k::KT], ident)
                j.then_inc(sem("xTp"), 1)
            wait(pe, ("hTl", 8))
            for x in range(FIRST_BLOCKS * BCH):
                project(x)
            pe.wait_ge(sem("small_in"), SMALL)
            ws3 = wsm[:, 0:KT * NSM].rearrange("p (k c) -> p k c", k=KT)
            for m in range(NM):
                for k in range(KT):
                    for part in (hTh, hTl):
                        i = mm(pair("small")[:, m * NSM:(m + 1) * NSM],
                               part[:, k, m * P:(m + 1) * P].bitcast(F32), ws3[:, k, :],
                               start=(k == 0 and part is hTh), stop=(k == KT - 1 and part is hTl))
            done("small", i)
            fill("small")
            pe.wait_ge(sem("small_in"), SMALL)
            for j in range(3 * A_HEADS):
                i = tr(pair("cw")[:, j * TAPS:(j + 1) * TAPS], convw[:, j * P:(j + 1) * P], ident[0:TAPS, 0:TAPS])
            done("cw", i)
            fill("cw")
            open_pair("blrT")
            for m in range(NM):
                i = tr(pair("blrT")[0:RANK, m * P:(m + 1) * P], zs3[:, m, 2 * A_HEADS:NSM], ident)
            done("blrT", i)
            fill("blrT")
            open_pair("gc")
            pe.wait_ge(sem("consts"), 1)
            wait(pe, ("gdec", 1))
            mm(pair("gc")[:, 0:half16], upT, gdec, start=True, stop=True)
            done("gc", mm(pair("gc")[:, half16:2 * half16], ones, gdec, start=True, stop=True))
            fill("gc")
            open_pair("gkT")
            pe.wait_ge(sem("small_in"), SMALL)
            wait(pe, ("blrT", 1))
            for h in range(B_HEADS):
                i = mm(pair("gkT")[:, h * SEQ:(h + 1) * SEQ], T_["wgk2"][0:RANK, h * P:(h + 1) * P],
                       T_["blrT"][0:RANK, :], start=True, stop=True)
            done("gkT", i)
            fill("gkT")
            for name, blk in (("bqT", 0), ("bkT", 1)):
                open_pair(name)
                pe.wait_ge(sem("z"), blk + 1)
                for h in range(B_HEADS):
                    for n in range(NM):
                        i = tr(pair(name)[:, (h * NM + n) * P:(h * NM + n + 1) * P],
                               zsl("gla", blk)[:, n, h * P:(h + 1) * P], ident)
                done(name, i)
                fill(name)
            open_pair("lv_eye")
            wait(pe, ("bqT", 1))
            wait(pe, ("bkT", 1))
            for u in range(GU):
                sl = slice(u * P, (u + 1) * P)
                i = mm(pair("lv_eye")[:, sl], T_["bkT"][:, sl], T_["bqT"][:, sl], start=True, stop=True)
            done("lv_eye", i)
            fill("lv_eye")
            qm, km = Z1[:, 0:1024], Z1[:, 1024:2048]
            for j, b in enumerate(LEVELS):
                st = f"lv{b}"
                open_pair(st)
                pe.wait_ge(sem("qkm"), j + 1)
                for u in range(GU):
                    sl = slice(u * P, (u + 1) * P)
                    i = mm(pair(st)[:, sl], km[:, sl], qm[:, sl], start=True, stop=True)
                done(st, i)
                fill(st)
            open_pair("kd")
            wait(pe, ("edge", 1))
            for h in range(B_HEADS):
                i = tr(pair("kd")[:, h * P:(h + 1) * P], T_["kdT"][:, h * P:(h + 1) * P], ident)
            done("kd", i)
            fill("kd")

            def vrow(n, h):
                return zsl("gla", 2 + h // 2)[:, n, (h % 2) * B_DV:(h % 2 + 1) * B_DV]

            open_pair("bS")
            wait(pe, ("kdtok", 1))
            pe.wait_ge(sem("z"), 4)
            for h in range(B_HEADS):
                i = mm(pair("bS")[:, h * B_DV:(h + 1) * B_DV], T_["kdtok"][:, h * P:(h + 1) * P], vrow(0, h),
                       start=True, stop=True)
            done("bS", i)
            fill("bS")
            wait(pe, ("attn", len(LEVELS)))
            for n in range(NM):
                st = f"bo{n}"
                open_pair(st)
                if n:
                    wait(pe, ("bS", 1))
                for h in range(B_HEADS):
                    u = h * NM + n
                    sl = slice(u * P, (u + 1) * P)
                    o = pair(st)[:, h * B_DV:(h + 1) * B_DV]
                    i = mm(o, T_["attn"][:, sl], vrow(n, h), start=True, stop=(n == 0))
                    if n:
                        i = mm(o, qm[:, sl], T_["bS"][:, h * B_DV:(h + 1) * B_DV], start=False, stop=True)
                done(st, i)
                fill(st)
            wait(pe, ("b_out", 1))
            for j in range(2):
                st = f"obT{j}"
                open_pair(st)
                for h in range(2):
                    for f in range(2):
                        for n in range(NM):
                            src = T_["bo"][:, n * 1024 + (2 * j + h) * B_DV + f * P:][:, 0:P]
                            i = tr(pair(st)[:, ((h * 2 + f) * NM + n) * P:((h * 2 + f) * NM + n + 1) * P], src, ident)
                done(st, i)
                fill(st)

            for g in range(NG):
                s = f".{g}"
                which = f"gdn{g}"
                first_block = FIRST_BLOCKS + 4 * g
                Zb = Z0 if g == 0 else Z1
                c = [Zb[:, i * 1024:(i + 1) * 1024] for i in range(3)]

                def per_u(step, f, us=range(GU)):
                    for u in us:
                        i = f(u, slice(u * P, (u + 1) * P))
                    done(step + s, i)
                    fill(step + s)

                def lvl(step, f):
                    open_pair(step + s)
                    o = pair(step + s)
                    per_u(step, lambda u, sl: f(o, u, sl))

                for j, w in enumerate(("zqT", "zkT", "zvT")):
                    open_pair(w + s)
                    pe.wait_ge(sem("z"), first_block + j + 1)
                    o = pair(w + s)
                    per_u(w, lambda u, sl: tr(o[:, sl], zsl(which, j)[:, u % NM, (u // NM) * P:(u // NM + 1) * P],
                                              ident))
                wait(pe, ("gB", g + 1))
                lvl("gcb", lambda o, u, sl: mm(o[:, sl], T_["gB"][:, sl], upT, start=True, stop=True))
                open_pair("ssq" + s)
                pe.wait_ge(sem("sq"), 2 * g + 2)
                o = pair("ssq" + s)
                for j in range(2):
                    for u in range(GU):
                        i = mm(o[:, 8 * j + u:8 * j + u + 1], T_[f"zT{j}"][:, u * P:(u + 1) * P], ones[:, 0:1],
                               start=True, stop=True)
                done("ssq" + s, i)
                fill("ssq" + s)
                lvl("ktok", lambda o, u, sl: tr(o[:, sl], c[1][:, sl], ident))
                pe.wait_ge(sem("silu"), 3 * g + 3)
                lvl("vtok", lambda o, u, sl: tr(o[:, sl], c[2][:, sl], ident))
                lvl("khT", lambda o, u, sl: tr(o[:, sl], T_["zT0"][:, sl], ident))
                wait(pe, ("khT", g + 1))
                kh = T_["zT1"]
                lvl("A", lambda o, u, sl: mm(o[:, sl], kh[:, sl], kh[:, sl], start=True, stop=True))
                lvl("PT", lambda o, u, sl: mm(o[:, sl], kh[:, sl], c[0][:, sl], start=True, stop=True))
                pe.wait_ge(sem("L"), 7 * g + 1)
                lvl("Y1", lambda o, u, sl: mm(o[:, sl], T_["gB"][:, sl], ident, start=True, stop=True))
                for j, b in enumerate(LEVELS[1:]):
                    L = T_["gB"] if (j + 1) % 2 == 0 else T_["L1"]
                    pe.wait_ge(sem("L"), 7 * g + j + 2)
                    pe.wait_ge(sem("U"), 7 * g + j + 1)
                    lvl(f"Y{b}", lambda o, u, sl: mm(o[:, sl], L[:, sl], T_["U"][:, sl], start=True, stop=True))
                    pe.wait_ge(sem("Y"), 6 * g + j + 1)
                    pe.wait_ge(sem("T"), 6 * g + j + 1)
                    lvl(f"dU{b}", lambda o, u, sl: mm(o[:, sl], T_["T"][:, sl], T_["Y"][:, sl], start=True,
                                                      stop=True))
                    if b != 64:
                        lvl(f"dT{b}", lambda o, u, sl: mm(o[:, sl], T_["Y"][:, sl], T_["T"][:, sl], start=True,
                                                          stop=True))
                pe.wait_ge(sem("U"), 7 * g + 7)
                pe.wait_ge(sem("kbg"), g + 1)
                pe.wait_ge(sem("kdec"), g + 1)
                kb = T_["kbg"]

                def per_head(step, f):
                    open_pair(step + s)
                    o = pair(step + s)
                    for h in range(GH):
                        i = f(o[:, h * P:(h + 1) * P], slice(h * P, (h + 1) * P), slice((2 * h) * P, (2 * h + 1) * P),
                              slice((2 * h + 1) * P, (2 * h + 2) * P))
                    done(step + s, i)
                    fill(step + s)

                v = T_["zT2"]
                per_head("wT", lambda o, hh, u0, u1: mm(o, kb[:, u1], T_["U"][:, u1], start=True, stop=True))
                per_head("u0", lambda o, hh, u0, u1: mm(o, T_["U"][:, u0], v[:, u0], start=True, stop=True))
                wait(pe, ("u0", g + 1))
                per_head("S", lambda o, hh, u0, u1: mm(o, T_["kdec"][:, hh], T_["T"][:, hh], start=True, stop=True))
                wait(pe, ("a_S", g + 1))
                wait(pe, ("wT", g + 1))

                def v1(o, hh, u0, u1):
                    mm(o, T_["U"][:, u1], v[:, u1], start=True, stop=False)
                    return mm(o, T_["nwT"][:, hh], T_["aS"][:, hh], start=False, stop=True)

                per_head("v1", v1)
                per_head("oi", lambda o, hh, u0, u1: mm(o, c[0][:, u1], T_["aS"][:, hh], start=True, stop=True))
                wait(pe, ("v1", g + 1))
                wait(pe, ("PT", g + 1))
                lvl("o", lambda o, u, sl: mm(o[:, sl], T_["DT"][:, sl],
                                             T_["T"][:, (u % NM) * 512 + (u // NM) * P:][:, 0:P], start=True,
                                             stop=True))
                wait(pe, ("a_out", g + 1))
                lvl("oaT", lambda o, u, sl: tr(o[:, sl], T_["Y"][:, sl], ident))

            x = CH_MIX
            wait(pe, ("oaT", NG))
            pe.wait_ge(sem("z"), len(BLOCKS))
            oh = [t.rearrange("p (k t) -> p k t", k=A_HEADS) for t in o_hi]
            ol = [t.rearrange("p (k t) -> p k t", k=A_HEADS) for t in o_lo]
            for c in range(NC):
                if c:
                    pe.wait_ge(sem("tb"), c)
                for h in range(BCH):
                    chunk(x, (bank(0), bank(1)), (hTh, hTl), h * CT, h == 0, h == BCH - 1)
                    x += 1
                for w, got in enumerate(("gya", "gyb")):
                    if c:
                        pe.wait_ge(sem(got), c)
                    else:
                        pe.wait_ge(sem("o_lo"), w + 1)
                    for h in range(A_HEADS // CT):
                        chunk(x, (bank(2 + 2 * w), bank(3 + 2 * w)), (oh[w], ol[w]), h * CT, h == 0,
                              h == A_HEADS // CT - 1)
                        x += 1
            wait(pe, ("merged", NC))
            for i in range(8):
                for k in range(2):
                    for m in range(NM):
                        j = tr(bank(i)[:, (k * NM + m) * P:(k * NM + m + 1) * P], gateA[:, m, 2 * i + k::KT], ident)
                j.then_inc(sem("mTp"), 1)
            wait(pe, ("mT", 8))
            for c in range(NC):
                if c >= 2:
                    pe.wait_ge(sem("x1"), 2 * (c - 1))
                for h in range(BCH):
                    chunk(x, (bank(2 * (c % 2)), bank(2 * (c % 2) + 1)), (hTh, hTl), h * CT, h == 0, h == BCH - 1)
                    x += 1
            assert x == CHUNKS
            pe.sem_inc(sem("slotM_free"), 1)
            wait(pe, ("h2", 2))
            for i in range(8):
                for k in range(2):
                    for m in range(NM):
                        j = tr(bank(i)[:, (k * NM + m) * P:(k * NM + m + 1) * P], h2[:, m, 2 * i + k::KT], ident)
                j.then_inc(sem("h2Tp"), 1)
            wait(pe, ("h2T", 8))
            pe.wait_ge(sem("wr_in"), 32)
            R = GROUPS + NE
            wr = wsm.rearrange("p (k c) -> p k c", k=KT)
            for m in range(NM):
                for k in range(KT):
                    i = mm(bank(0, NM * R)[:, m * R:(m + 1) * R], h2T[:, k, m * P:(m + 1) * P], wr[:, k, :],
                           start=(k == 0), stop=(k == KT - 1))
            i.then_inc(sem("logits"), 1)
            wait(pe, ("Mt", 1))
            mm(bank(1)[:, 0:NE], upT, Mt[:, 0:NE], start=True, stop=True)
            mm(bank(1)[:, NE:2 * NE], upT, Mt[:, NE:2 * NE], start=True, stop=False)
            mm(bank(1)[:, NE:2 * NE], ones, Mt[:, 0:NE], start=False, stop=True)
            mm(bank(2, NE), ones, Mt[:, 0:NE], start=True, stop=False)
            mm(bank(2, NE), ones, Mt[:, NE:2 * NE], start=False, stop=True).then_inc(sem("ranks"), 1)
            wait(pe, ("rounds_ready", 1))
            pe.sem_inc(sem("xadd"), 2)
            pe.sem_inc(sem("yev"), 2)
            pe.sem_inc(sem("combT"), 1)
            rounds = pe.value_load(rounds_i[0:1, 0:1], min_val=1, max_val=SEQ // CAP)
            with pe.Fori(0, rounds) as r:
                with pe.Fori(0, PAIRS) as p:
                    n = r * PAIRS + p
                    pe.wait_ge(sem("sel"), n + 1)
                    for b in range(4):
                        if b >= 2:
                            pe.wait_ge(sem("xe"), n * 4 + b - 1)
                        for k in range(4):
                            for m in range(NM):
                                i = mm(bank(2 + b % 2)[:, k * P:(k + 1) * P], h2[:, m, 4 * b + k::KT],
                                       sel[:, m * P:(m + 1) * P], start=(m == 0), stop=(m == NM - 1))
                        i.then_inc(sem("gath"), 1)
                    pe.wait_ge(sem("selg"), n + 1)
                    pe.wait_ge(sem("xe"), n * 4 + 3)
                    for m in range(NM):
                        i = tr(bank(2)[:, m * P:(m + 1) * P], selg[:, m * P:(m + 1) * P], ident)
                    i.then_inc(sem("combT"), 1)
                    pe.wait_ge(sem("xe"), n * 4 + 4)
                    j = 0
                    for w in range(2):
                        for h in range(2):
                            for e in range(2):
                                pe.wait_ge(sem(f"slotM{(j + e) % RING_M}"), n * 32 + 16 * ((j + e) // RING_M + 1))
                            for k in range(HT):
                                for e in range(2):
                                    i = mm(bank(w)[e * CAP:(e + 1) * CAP, :],
                                           xeT[:, h * HT + k, e * CAP:(e + 1) * CAP],
                                           ringM[:, (j + e) % RING_M, k * CB:(k + 1) * CB],
                                           start=(h == 0 and k == 0), stop=(h == 1 and k == HT - 1))
                            i.then_inc(sem("slotM_free"), 2)
                            j += 2
                    pe.wait_ge(sem("hid"), n + 1)
                    for t in range(FT):
                        i = tr(bank(3)[:, t * P:(t + 1) * P], hid[:, t::FT], ident)
                    i.then_inc(sem("actT"), 1)
                    pe.wait_ge(sem("aT"), n + 1)
                    pe.wait_ge(sem("comb"), n + 1)

                    def combine(k):
                        pe.wait_ge(sem("yev"), n * NC + k + 3)
                        for m in range(NM):
                            pe.wait_ge(sem("xadd"), n * 8 + 2 * k + m + 1)
                            mm(bank(6 + m), comb[:, m * P:(m + 1) * P], Ysb[:, k * CB:(k + 1) * CB], start=True,
                               stop=True).then_inc(sem("cmb"), 1)

                    for k in range(NC):
                        if k % 2 == 0:
                            for e in range(2):
                                pe.wait_ge(sem(f"slotM{(j + e) % RING_M}"), n * 32 + 16 * ((j + e) // RING_M + 1))
                        pe.wait_ge(sem("yev"), n * NC + k + 1)
                        for t in range(FT):
                            for e in range(2):
                                src = ringM[:, (j + e) % RING_M, :].rearrange("p (t n) -> p t n", t=FT)
                                i = mm(bank(4 + k % 2)[e * CAP:(e + 1) * CAP, :],
                                       aT[:, t * P + e * CAP:t * P + (e + 1) * CAP],
                                       src[:, t, (k % 2) * CB:(k % 2 + 1) * CB], start=(t == 0), stop=(t == FT - 1))
                        if k % 2 == 0:
                            i.then_inc(sem("down"), 1)
                        else:
                            i.then_inc(sem("slotM_free"), 2)
                            j += 2
                        if k:
                            combine(k - 1)
                    combine(NC - 1)


_INS = ["x", "norm_mix", "w_in", "conv_a", "a_log", "dt_bias", "a_norm", "w_gk2", "b_gk", "b_norm", "w_oa", "w_ob",
        "w_out", "norm_ffn", "w_rg", "b_rg", "w_re", "b_re", "w1", "w3", "w2", "norm_final"]


def kernel(**inputs):
    import numpy as _np
    import concourse.bacc as _bacc
    from concourse import mybir as _mybir
    from concourse.bass_utils import run_bass_kernel_spmd as _run

    nc = _bacc.Bacc("TRN2", target_bir_lowering=False, num_devices=1)
    arrays, args = {}, []
    for name in _INS:
        a = _np.ascontiguousarray(inputs[name])
        arrays[f"in_{name}"] = a
        args.append(nc.dram_tensor(f"in_{name}", a.shape, _mybir.dt.from_np(a.dtype), kind="ExternalInput").ap())
    args.append(nc.dram_tensor("out_y", (1, SEQ, D), _mybir.dt.float32, kind="ExternalOutput").ap())
    build(nc, *args)
    r = _run(nc, [arrays], core_ids=[0])
    return r.results[0]["out_y"]
```

```python
from contextlib import ExitStack

import concourse.bass as bass
from concourse import mybir

F32 = mybir.dt.float32
F32R = mybir.dt.float32r
I32 = mybir.dt.int32
ALU = mybir.AluOpType
ACT = mybir.ActivationFunctionType
AX = mybir.AxisListType

P = 128
D = 2048
SEQ = 256
NM = SEQ // P
KT = D // P
CB = 512
NC = D // CB
HT = KT // 2
SLOT = HT * CB
CT = 4
CHUNK = CT * CB
BCH = KT // CT
EPS = 1e-6
A_HEADS, A_D, TAPS = 8, 128, 4
B_HEADS, B_DK, B_DV, RANK = 4, 128, 256, 16
GATE_NORM = 16.0
GH = 4
NG = A_HEADS // GH
GU = GH * NM
QSCALE = float(A_D) ** -0.5
AQ = A_HEADS * A_D
BQK, BV = B_HEADS * B_DK, B_HEADS * B_DV
C_AQ, C_AK, C_AV, C_AZ = 0, AQ, 2 * AQ, 3 * AQ
C_BETA = 4 * AQ
C_BQ = C_BETA + 2 * A_HEADS
C_BK = C_BQ + BQK
C_BV = C_BK + BQK
C_BG = C_BV + BV
C_LR = C_BG + BV
C_MA = C_LR + RANK
C_MB = C_MA + D
NSM = 2 * A_HEADS + RANK
LEVELS = [1 << i for i in range(7)]
GROUPS, EPG = 4, 8
NE = GROUPS * EPG
FF = 512
FT = FF // P
CAP = 64
PAIRS = NE // 2
NEG = -3.0e38
SMALL = 16 * 12

PRE = 2
BLOCKS = ([("gla", i, C_BQ + CB * i) for i in range(6)]
          + [("gdn0", i, c) for i, c in enumerate((C_AQ, C_AK, C_AV, C_AZ))]
          + [("gdn1", i, c + CB) for i, c in enumerate((C_AQ, C_AK, C_AV))]
          + [("gateB", i, C_MB + CB * i) for i in range(PRE)]
          + [("gdn1", 3, C_AZ + CB)]
          + [("gateA", i, C_MA + CB * i) for i in range(NC)])
RING_A = 3
NSPLIT = 2
RING_M = 6
PER_PAIR = 12

GLA_STEPS = (["small", "cw", "smallT", "blrT", "gc", "gkT", "bqT", "bkT", "lv_eye"]
             + [f"lv{b}" for b in LEVELS] + ["kd", "bS", "bo0", "bo1", "obT0", "obT1"])
GDN_STEPS = (["zqT", "zkT", "zvT", "gcb", "ssq", "ktok", "vtok", "khT", "A", "PT", "Y1"]
             + [f"{w}{b}" for b in LEVELS[1:-1] for w in ("Y", "dU", "dT")]
             + ["Y64", "dU64", "wT", "u0", "S", "v1", "oi", "o", "oaT"])
STEPS = GLA_STEPS + [f"{s}.{g}" for g in range(NG) for s in GDN_STEPS]
FIRST_BLOCKS = 2
SPAN_BLOCKS = [7, 4 + PRE, 1 + NC]
SPANS = [
    {"small": 1, "smallT": 0, "cw": 1, "blrT": 2, "gc": 1, "gkT": 4, "bkT": 2, "lv_eye": 2, "lv1": 2, "lv2": 1,
     "lv4": 2, "lv8": 1, "lv16": 2, "lv32": 1, "lv64": 2, "kd": 1, "bo1": 3},
] + [
    {f"{k}.0": v for k, v in
     {"gcb": 9, "ssq": 2, "vtok": 1, "khT": 1, "PT": 1, "dT2": 1, "dT4": 1, "dT8": 1, "dT16": 1, "dT32": 1,
      "dU64": 1, "wT": 1, "o": 3}.items()},
    {f"{k}.1": v for k, v in
     {"gcb": 7, "ssq": 2, "vtok": 1, "khT": 1, "PT": 1, "dT2": 1, "dT4": 1, "dT8": 1, "dT16": 1, "dT32": 1,
      "wT": 1, "o": 2}.items()},
]


def fillers():
    out = {s: [] for s in STEPS}
    q = FIRST_BLOCKS * BCH
    for span, blocks in zip(SPANS, SPAN_BLOCKS):
        assert sum(span.values()) == blocks * BCH, span
        for s in STEPS:
            n = span.get(s, 0)
            out[s] = out[s] + list(range(q, q + n))
            q += n
    assert q == len(BLOCKS) * BCH
    return out


FILL = fillers()


def build(nc, x, norm_mix, w_in, conv_a, a_log, dt_bias, a_norm, w_gk2, b_gk, b_norm, w_oa, w_ob, w_out,
          norm_ffn, w_rg, b_rg, w_re, b_re, w1, w3, w2, norm_final, y):
    x_v = x[0].rearrange("(m p) d -> p m d", p=P)
    y_v = y[0].rearrange("(m p) d -> p m d", p=P)
    win_v = w_in[0].rearrange("(p k) n -> p k n", k=KT)
    wout_v = w_out[0].rearrange("(p k) n -> p k n", k=KT)
    woa_v = w_oa[0].rearrange("(k p) n -> p k n", p=P)
    wob_v = w_ob[0].rearrange("(k p) n -> p k n", p=P)
    w1_v = w1[0].rearrange("e (p k) f -> e p (k f)", k=KT)
    w3_v = w3[0].rearrange("e (p k) f -> e p (k f)", k=KT)
    w2_v = w2[0].rearrange("e (p t) n -> e p (t n)", t=FT)

    with ExitStack() as ctx:
        block_of = {}

        def sem(name):
            if name not in block_of:
                block_of[name] = ctx.enter_context(nc.semaphore(name))
            return block_of[name]

        FREE = 53200
        ARENA = nc.sbuf_base + (-nc.sbuf_base) % 32
        arena = ctx.enter_context(nc.sbuf_tensor("arena", [P, FREE], F32))
        rounds_i = ctx.enter_context(nc.sbuf_tensor("rounds_i", [P, 2], I32))

        def cut(at, size):
            return arena[:, at:at + size], at + size

        def split_tensor(name, at, size):
            t = nc.alloc_sbuf_tensor_at(name, [P, size], F32R, offset=ARENA + 4 * at)
            return t[:, :]

        H0 = 0
        hTh = split_tensor("hT_hi", H0, KT * SEQ).rearrange("p (k t) -> p k t", k=KT)
        H1 = H0 + KT * SEQ
        hTl = split_tensor("hT_lo", H1, KT * SEQ).rearrange("p (k t) -> p k t", k=KT)
        OAB = H1 + KT * SEQ
        oaT_f, at = cut(OAB, A_HEADS * SEQ)
        obT_f, at = cut(at, A_HEADS * SEQ)
        oaT = oaT_f.rearrange("p (k t) -> p k t", k=A_HEADS)
        obT = obT_f.rearrange("p (k t) -> p k t", k=A_HEADS)
        RM = at
        MIX = 6 * NM * CB + 12840 + 4 * NM * CB
        RA = RM + MIX
        ringA, at = cut(RA, RING_A * CHUNK)
        ringA = ringA.rearrange("p (s n) -> p s n", s=RING_A)
        w_hi, w_lo = [], []
        for i in range(NSPLIT):
            w_hi.append(split_tensor(f"w_hi{i}", at, CHUNK))
            w_lo.append(split_tensor(f"w_lo{i}", at + CHUNK, CHUNK))
            at += 2 * CHUNK
        ringM = arena[:, RM:RM + RING_M * SLOT].rearrange("p (s n) -> p s n", s=RING_M)
        consts = at
        x1 = arena[:, OAB:OAB + NM * D].rearrange("p (m d) -> p m d", m=NM)

        at = consts
        ident, at = cut(at, P)
        upT, at = cut(at, P)
        ones, at = cut(at, P)
        iota, at = cut(at, CAP)
        mask = {}
        for b in LEVELS:
            mask[b], at = cut(at, P)
        wsm, at = cut(at, KT * (GROUPS + NE))
        cw, at = cut(at, 3 * A_HEADS * TAPS)
        zs, at = cut(at, NM * NSM)
        nmix, at = cut(at, KT)
        nffn, at = cut(at, KT)
        anorm, at = cut(at, 1)
        bnorm, at = cut(at, 2)
        bgk, at = cut(at, B_HEADS)
        alog, at = cut(at, A_HEADS)
        dtb, at = cut(at, A_HEADS)
        half16 = NM * A_HEADS
        beta, at = cut(at, half16)
        gdec, at = cut(at, half16)
        xa, at = cut(at, half16)
        na, at = cut(at, half16)
        gcol, at = cut(at, half16)
        gdif, at = cut(at, half16)
        eg, at = cut(at, half16)
        ekd, at = cut(at, half16)
        bhalf, at = cut(at, half16)
        beg, at = cut(at, half16)
        ss1, at = cut(at, NM)
        rstd, at = cut(at, NM)
        rstdh, at = cut(at, NM)
        ssqk, at = cut(at, 16)
        rqk, at = cut(at, 16)
        rms, at = cut(at, 16)
        rmf, at = cut(at, 16)
        pw, at = cut(at, 16)
        ss2, at = cut(at, NM)
        rstd2, at = cut(at, NM)
        nfft, at = cut(at, KT)
        ssp, at = cut(at, NM * NC)
        brg, at = cut(at, GROUPS)
        bre, at = cut(at, NE)
        assert at <= FREE, at
        zs3 = zs.rearrange("p (m c) -> p m c", m=NM)

        def mh(t):
            return t.rearrange("p (m h) -> p m h", m=NM)

        at = RM
        Z1_AT = at
        Z1, at = cut(at, 6 * NM * CB)
        TEMPS = at
        LAST = RM + MIX - 4 * NM * CB
        Z0, _ = cut(LAST, 4 * NM * CB)
        xs0 = Z0.rearrange("p (m d) -> p m d", m=NM)
        gateA = xs0
        names = {}

        def temps(base, sizes):
            at = base
            for n, s in sizes:
                names[n], at = cut(at, s)
            assert at <= LAST, (at, LAST)

        temps(TEMPS, [("bqT", 1024), ("bkT", 1024), ("bT", 1024), ("bE", 1024), ("attn", 1024), ("btmp", 1024),
                      ("bS", 1024), ("bo", 2048), ("bth", 2048), ("wgk2", 512),
                      ("blrT", 256)])
        names["kdT"], names["kdtok"] = names["btmp"][:, 0:512], names["btmp"][:, 512:1024]
        zpad = GH * (SEQ + TAPS - 1)
        temps(TEMPS, [("zT0", zpad), ("zT1", zpad), ("zT2", zpad), ("kbg", 1024), ("kdec", 512), ("nwT", 512),
                      ("aS", 512), ("gB", 1024), ("Dm", 1024), ("DT", 1024), ("L1", 1024), ("U", 1024), ("T", 1024),
                      ("Y", 1024)])
        names["inter"] = names["nwT"]
        convw = arena[0:TAPS, TEMPS:TEMPS + 3 * AQ]
        T_ = names

        def zsl(which, i):
            if which == "gateA":
                return gateA[:, :, i * CB:(i + 1) * CB]
            if which == "gateB":
                which, i = "gla", 4 + i
            base = {"gla": Z1, "gdn0": Z0, "gdn1": Z1}[which]
            return base[:, i * NM * CB:(i + 1) * NM * CB].rearrange("p (m n) -> p m n", m=NM)

        at = RM + (RING_M - 1) * SLOT
        x1c = []
        for i in range(2):
            t, at = cut(at, CT * SEQ)
            x1c.append(t.rearrange("p (k t) -> p k t", k=CT))
        sqs, at = cut(at, CB)
        assert at <= RA, (at, RA)

        h2, _ = cut(H1, NM * D)
        at = RM + RING_M * SLOT
        h2 = h2.rearrange("p (m d) -> p m d", m=NM)
        xeT, at = cut(at, KT * P)
        xeT = xeT.rearrange("p (k s) -> p k s", k=KT)
        Ysb, at = cut(at, D)
        aT, at = cut(at, FT * P)
        hid, at = cut(at, FF)
        hth, at = cut(at, FF)
        hs, at = cut(at, FF)
        comb, at = cut(at, SEQ)
        sel, at = cut(at, NM * P)
        selg, at = cut(at, NM * P)
        nfin, at = cut(at, D)
        junk, at = cut(at, D)
        pos, at = cut(at, NM * NE)
        Wt, at = cut(at, NM * NE)
        Mt, at = cut(at, NM * NE)
        rt = {}
        for n, s in [("lg", 8), ("le", 64), ("gm", 2), ("d", 8), ("ed", 8), ("den", 2), ("pt", 2), ("eq", 16),
                     ("cum", 16), ("fg", 8), ("pr", 64), ("ls", 16), ("m1", 2), ("d1", 16), ("f1", 16), ("ls2", 16),
                     ("m2", 2), ("d2", 16), ("f2", 16), ("dm", 2), ("e2", 2), ("s2", 2), ("r2", 2), ("w1", 2),
                     ("w2", 2), ("fs", 16), ("ws", 16), ("wa", 16), ("mx", 1), ("c1", 1), ("c2", 1), ("c3", 1),
                     ("rf", 1)]:
            rt[n], at = cut(at, s)
        assert at <= consts, (at, consts)
        o_hi = [split_tensor(f"o{b}_hi", TEMPS + 4096 * i, 2048) for i, b in enumerate("ab")]
        o_lo = [split_tensor(f"o{b}_lo", TEMPS + 4096 * i + 2048, 2048) for i, b in enumerate("ab")]
        MRG = TEMPS + 8192
        tb = arena[:, MRG:MRG + NM * CB].rearrange("p (m n) -> p m n", m=NM)
        tyb = arena[:, MRG + 1024:MRG + 2048].rearrange("p (m n) -> p m n", m=NM)

        psum = ctx.enter_context(nc.psum_tensor("psum", [P, 8 * CB], F32))

        def bank(i, n=CB):
            return psum[:, i * CB:i * CB + n]

        def pair(step):
            return psum[:, (4 + 2 * (STEPS.index(step) % 2)) * CB:(4 + 2 * (STEPS.index(step) % 2)) * CB + 2 * CB]

        def drained(step):
            base, _, g = step.partition(".")
            g = int(g or 0)
            if base[0] == "Y" and base != "Y1":
                return "Y", g * 6 + LEVELS.index(int(base[1:]))
            if base in ("Y1",) or base[:2] == "dU":
                return "U", g * 7 + (1 if base == "Y1" else LEVELS.index(int(base[2:])) + 1)
            if base[:2] == "dT":
                return "T", g * 6 + LEVELS.index(int(base[2:])) + 1
            if base[:2] == "lv":
                return "attn_tmp", (1 if base == "lv_eye" else LEVELS.index(int(base[2:])) + 2)
            alias = {"small": "small_t", "smallT": "zs", "o": "a_o", "bo0": "b_o", "bo1": "b_o", "obT0": "obT", "obT1": "obT",
                     "ssq": "ssqk", "S": "a_S", "kd": "kdtok", "gc": "gcol", "oi": "inter", "gkT": "gkx"}
            n = {"bo1": 2, "obT1": 2}.get(base, 1)
            return alias.get(base, base), g + n

        def full(step):
            i = STEPS.index(step)
            return f"pair{i % 2}_full", i // 2 + 1

        def wait(eng, what):
            eng.wait_ge(sem(what[0]), what[1])

        U3 = "p (u t) -> p u t"

        def units(t, u=GU):
            return t.rearrange(U3, u=u)

        block = ctx.enter_context(nc.Block())
        CH_MIX = BCH * len(BLOCKS)
        MERGE, at_chunk = [], CH_MIX
        for c in list(range(PRE, NC)) + list(range(PRE)):
            a_at = at_chunk + (BCH if c >= PRE else 0)
            b_at = a_at + A_HEADS // CT
            at_chunk = b_at + A_HEADS // CT
            MERGE.append((c, a_at, b_at, at_chunk))
        CH_MERGE = at_chunk
        CHUNKS = CH_MERGE + BCH * NC

        def chunks_before(i):
            return FIRST_BLOCKS * BCH + sum(len(FILL[s]) for s in STEPS[:i])

        class Splitter:

            def __init__(self, split, evacuate):
                self.x, self.blocks, self.split, self.evacuate = 0, 0, split, evacuate
                for i in range(NSPLIT):
                    split(i)

            def follow(self, end):
                while self.x < end:
                    if self.x + NSPLIT < CHUNKS:
                        self.split(self.x + NSPLIT)
                    self.x += 1
                    self.evacuate_to(self.x)

            def evacuate_to(self, end):
                while self.blocks < min(end, CH_MIX) // BCH:
                    self.evacuate(self.blocks)
                    self.blocks += 1

            def before(self, step, most=CHUNKS):
                i = STEPS.index(step)
                end, last = chunks_before(i), chunks_before(i - 1) if i else 0
                self.seen = end
                self.follow(min(end - min(1, end - last), self.x + most))
                if most == CHUNKS:
                    self.evacuate_to(end)

            def rest(self):
                self.follow(self.seen)

        @block.sync
        def _(sp):
            sp.dma_start(xs0[:, 0, :], x_v[:, 0, :]).then_inc(sem("x_in0"), 16)
            sp.dma_start(xs0[:, 1, :], x_v[:, 1, :]).then_inc(sem("x_in1"), 16)

            def load(x, src):
                if x >= RING_A:
                    sp.wait_ge(sem("w_lo"), x - RING_A + 1)
                sp.dma_start(ringA[:, x % RING_A, :].rearrange("p (k n) -> p k n", k=CT), src)\
                    .then_inc(sem(f"raw{x % RING_A}"), 16)

            x = 0
            for _, _, c in BLOCKS:
                for h in range(BCH):
                    load(x, win_v[:, h * CT:(h + 1) * CT, c:c + CB])
                    x += 1
            for c, *_ in MERGE:
                if c >= PRE:
                    for h in range(BCH):
                        load(x, win_v[:, h * CT:(h + 1) * CT, C_MB + c * CB:C_MB + (c + 1) * CB])
                        x += 1
                for v in (woa_v, wob_v):
                    for h in range(A_HEADS // CT):
                        load(x, v[:, h * CT:(h + 1) * CT, c * CB:(c + 1) * CB])
                        x += 1
            for c in range(NC):
                if c == 1:
                    wait(sp, ("o_lo", 2))
                    for m in range(NM):
                        sp.dma_start(x1[:, m, :], x_v[:, m, :]).then_inc(sem("x_back"), 16)
                for h in range(BCH):
                    load(x, wout_v[:, h * CT:(h + 1) * CT, c * CB:(c + 1) * CB])
                    x += 1
            assert x == CHUNKS
            def load_up(pair, n, first=False):
                j = 0
                for v, h in ((w1_v, 0), (w1_v, 1), (w3_v, 0)):
                    for e in range(2):
                        if first and j == RING_M - 1:
                            wait(sp, ("ss2", 1))
                            wait(sp, ("logits", NC))
                        sp.wait_ge(sem("slotM_free"), n * PER_PAIR + j + 1)
                        sp.dma_start(ringM[:, j, :], v[bass.ds(pair * 2 + e, 1), :, h * SLOT:(h + 1) * SLOT]
                                     .rearrange("a p n -> (a p) n")).then_inc(sem(f"slotM{j}"), 16)
                        j += 1

            def load_rest(pair, n):
                for e in range(2):
                    sp.wait_ge(sem("slotM_free"), n * PER_PAIR + RING_M + e + 1)
                    sp.dma_start(ringM[:, e, :], w3_v[bass.ds(pair * 2 + e, 1), :, SLOT:2 * SLOT]
                                 .rearrange("a p n -> (a p) n")).then_inc(sem(f"slotM{e}"), 16)
                j = 2
                for h in range(2):
                    for e in range(2):
                        sp.wait_ge(sem("slotM_free"), n * PER_PAIR + RING_M + j + 1)
                        sp.sem_inc(sem("w2_turn"), 1)
                        sp.dma_start(ringM[:, j, :].rearrange("p (t n) -> p t n", t=FT),
                                     w2_v[bass.ds(pair * 2 + e, 1), :, :]
                                     .rearrange("a p (t n) -> (a p) t n", t=FT)[:, :, h * (D // 2):(h + 1) * (D // 2)]).then_inc(sem(f"slotM{j}"), 16)
                        j += 1

            wait(sp, ("mT", 8))
            sp.sem_inc(sem("slotM_free"), RING_M - 1)
            load_up(0, 0, first=True)
            wait(sp, ("rounds_ready", 1))
            more = sp.value_load(rounds_i[0:1, 1:2], min_val=0, max_val=SEQ // CAP - 1)
            last = more * PAIRS + (PAIRS - 1)
            with sp.Fori(0, last) as n:
                with sp.Fori(n & (PAIRS - 1), (n & (PAIRS - 1)) + 1) as p:
                    load_rest(p, n)
                with sp.Fori((n + 1) & (PAIRS - 1), ((n + 1) & (PAIRS - 1)) + 1) as p:
                    load_up(p, n + 1)
            load_rest(PAIRS - 1, last)
            wait(sp, ("y_ready", 2))
            sp.dma_start(y_v, x1[:, :, :]).then_inc(sem("y_out"), 16)
            sp.wait_ge(sem("y_out"), 16)

        @block.gpsimd
        def _(pool):
            def small(dst, src, name):
                pool.dma_start(dst, src, allow_slow_non_contiguous=True).then_inc(sem(name), 16)

            small(nmix, norm_mix[0].rearrange("(p k) -> p k", k=KT), "nmix_in")
            w3d = wsm[:, 0:KT * NSM].rearrange("p (k c) -> p k c", k=KT)
            small(w3d[:, :, 0:2 * A_HEADS], win_v[:, :, C_BETA:C_BETA + 2 * A_HEADS], "small_in")
            small(w3d[:, :, 2 * A_HEADS:NSM], win_v[:, :, C_LR:C_LR + RANK], "small_in")
            small(convw, conv_a[0], "small_in")
            small(T_["wgk2"][0:RANK, :], w_gk2[0], "small_in")
            small(dtb, dt_bias[0].partition_broadcast(P), "small_in")
            small(alog, a_log[0].partition_broadcast(P), "small_in")
            small(bgk, b_gk[0].rearrange("(h p) -> p h", p=P), "small_in")
            small(anorm, a_norm[0].rearrange("(p a) -> p a", a=1), "small_in")
            small(bnorm, b_norm[0].rearrange("(h p) -> p h", p=P), "small_in")
            small(nffn, norm_ffn[0].rearrange("(p k) -> p k", k=KT), "small_in")
            small(brg, b_rg[0].partition_broadcast(P), "small_in")
            small(bre, b_re[0].rearrange("g e -> (g e)").partition_broadcast(P), "small_in")

            links = [0]

            def link(ins):
                links[0] += 1
                ins.then_inc(sem("pool_link"), 1)
                pool.wait_ge(sem("pool_link"), links[0])

            nc.gpsimd.memset(ident, 0.0)
            nc.gpsimd.memset(ones, 1.0)
            nc.gpsimd.memset(pw, -0.5)
            link(nc.gpsimd.memset(upT, 1.0))
            nc.gpsimd.affine_select(out=ident, in_=ident, compare_op=ALU.not_equal, fill=1.0, base=0,
                                    pattern=[[-1, P]], channel_multiplier=1).then_inc(sem("ident"), 1)
            link(nc.gpsimd.affine_select(out=upT, in_=upT, compare_op=ALU.is_ge, fill=0.0, base=0,
                                         pattern=[[1, P]], channel_multiplier=-1))
            def masks(upper):
                for b in LEVELS:
                    i = nc.gpsimd.memset(mask[b], 1.0)
                link(i)
                for part in range(2):
                    for b in LEVELS:
                        mb = P // (2 * b)
                        if upper:
                            base, st = ((-1000, [[-2 * b, mb], [1000, 2], [0, b]]) if part == 0
                                        else (b - 1, [[2 * b, mb], [0, 2], [0, b]]))
                        else:
                            base, st = ((-b, [[-2 * b, mb], [-1000, 2], [0, b]]) if part == 0
                                        else (2 * b - 1, [[2 * b, mb], [0, 2], [0, b]]))
                        v = mask[b].rearrange("p (m s r) -> p m s r", s=2, r=b)
                        i = nc.gpsimd.affine_select(out=v, in_=v, compare_op=ALU.is_ge, fill=0.0, base=base,
                                                    pattern=st, channel_multiplier=1 - 2 * part)
                    link(i)

            masks(upper=True)
            nc.gpsimd.iota(iota, pattern=[[1, CAP]], base=0, channel_multiplier=0,
                           allow_small_or_imprecise_dtypes=True).then_inc(sem("consts"), 1)

            wait(pool, ("ss1", 2))
            link(nc.gpsimd.tensor_scalar(ss1, ss1, 1.0 / D, EPS, ALU.mult, ALU.add))
            link(nc.gpsimd.tensor_tensor(rstd, ss1, pw[:, 0:NM], ALU.pow))
            nc.gpsimd.tensor_scalar(rstdh, rstd, 0.5, None, ALU.mult).then_inc(sem("rstd"), 1)

            wait(pool, ("b_ms", 1))
            nc.gpsimd.tensor_tensor(rmf[:, 0:8], rms[:, 0:8], pw[:, 0:8], ALU.pow).then_inc(sem("b_rf"), 1)

            wait(pool, ("attn", len(LEVELS)))
            masks(upper=False)
            for g in range(NG):
                if g == 0:
                    wait(pool, ("obT", 2))
                    wait(pool, ("gdec", 1))
                else:
                    wait(pool, ("oaT", g))
                for h in range(GH):
                    for n in range(NM):
                        u = h * NM + n
                        i = nc.gpsimd.tensor_scalar(T_["gB"][:, u * P:(u + 1) * P], ones,
                                                    mh(gdec)[:, n, g * GH + h:g * GH + h + 1], None, ALU.mult)
                i.then_inc(sem("gB"), 1)
                wait(pool, ("expD", g + 1))
                Dm = units(T_["Dm"])
                bv = mh(beta)[:, :, g * GH:(g + 1) * GH].rearrange("p n h -> p h n").unsqueeze(3)\
                    .to_broadcast([P, GH, NM, P])
                nc.gpsimd.tensor_tensor(T_["Dm"].rearrange("p (h n t) -> p h n t", h=GH, n=NM),
                                        T_["Dm"].rearrange("p (h n t) -> p h n t", h=GH, n=NM), bv,
                                        ALU.mult).then_inc(sem("DA"), 1)
                wait(pool, ("expDT", g + 1))
                nc.gpsimd.tensor_tensor(units(T_["DT"]), units(T_["DT"]),
                                        upT.unsqueeze(1).to_broadcast([P, GU, P]), ALU.mult)\
                    .then_inc(sem("DTm"), 1)
                wait(pool, ("ssqk", g + 1))
                nc.gpsimd.tensor_tensor(rqk, ssqk, pw, ALU.pow).then_inc(sem("rqk"), 1)
                wait(pool, ("ktok", g + 1))
                k4 = T_["zT0"][:, 0:1024].rearrange("p (h n t) -> p h n t", h=GH, n=NM)
                nc.gpsimd.tensor_tensor(T_["kbg"].rearrange("p (h n t) -> p h n t", h=GH, n=NM), k4,
                                        mh(beg)[:, :, g * GH:(g + 1) * GH].rearrange("p n h -> p h n")
                                        .unsqueeze(3).to_broadcast([P, GH, NM, P]), ALU.mult).then_inc(sem("kbg"), 1)
                nc.gpsimd.tensor_tensor(units(T_["kdec"], GH), k4[:, :, 0, :],
                                        mh(ekd)[:, 0, g * GH:(g + 1) * GH].unsqueeze(2).to_broadcast([P, GH, P]),
                                        ALU.mult).then_inc(sem("kdec"), 1)
                wait(pool, ("A", g + 1))
                wait(pool, full(f"gcb.{g}"))
                for i, b in enumerate(LEVELS):
                    if i >= 2:
                        wait(pool, full(f"Y{LEVELS[i - 2]}.{g}"))
                        if i == 2:
                            wait(pool, ("T", g * 6 + 1))
                    dst = T_["gB"] if i % 2 == 0 else T_["L1"]
                    nc.gpsimd.tensor_tensor(units(dst), units(T_["Dm"]),
                                            mask[b].unsqueeze(1).to_broadcast([P, GU, P]), ALU.mult)\
                        .then_inc(sem("L"), 1)
                wait(pool, ("a_ms", g + 1))
                link(nc.gpsimd.tensor_scalar(rqk[:, 0:8], rqk[:, 0:8], QSCALE, None, ALU.mult))
                link(nc.gpsimd.tensor_tensor(rms[:, 0:8], rms[:, 0:8], rqk[:, 0:8], ALU.mult))
                link(nc.gpsimd.tensor_tensor(rms[:, 0:8], rms[:, 0:8], rqk[:, 0:8], ALU.mult))
                link(nc.gpsimd.tensor_scalar(rms[:, 0:8], rms[:, 0:8], 1.0 / A_D, EPS, ALU.mult, ALU.add))
                link(nc.gpsimd.tensor_tensor(rmf[:, 0:8], rms[:, 0:8], pw[:, 0:8], ALU.pow))
                nc.gpsimd.tensor_tensor(rmf[:, 0:8], rmf[:, 0:8], rqk[:, 0:8], ALU.mult).then_inc(sem("a_rf"), 1)

            wait(pool, ("zs", 1))
            wr = wsm.rearrange("p (k c) -> p k c", k=KT)
            small(wr[:, :, 0:GROUPS], w_rg[0].rearrange("(k p) g -> p k g", k=KT), "wr_in")
            small(wr[:, :, GROUPS:GROUPS + NE], w_re[0].rearrange("(k p) g e -> p k (g e)", k=KT), "wr_in")
            small(nfft, norm_ffn[0].rearrange("(k p) -> p k", k=KT), "wr_in")
            pool.wait_ge(sem("wr_in"), 48)
            nc.gpsimd.tensor_tensor(wr, wr, nfft.unsqueeze(2).to_broadcast([P, KT, GROUPS + NE]), ALU.mult)\
                .then_inc(sem("wr"), 1)
            wait(pool, ("ss2", 1))
            link(nc.gpsimd.tensor_scalar(ss2, ss2, 1.0 / D, EPS, ALU.mult, ALU.add))
            nc.gpsimd.tensor_tensor(rstd2, ss2, pw[:, 0:NM], ALU.pow).then_inc(sem("rstd2"), 1)
            small(nfin, norm_final.partition_broadcast(P), "nfin_in")

            wait(pool, ("rounds_ready", 1))
            rounds = pool.value_load(rounds_i[0:1, 0:1], min_val=1, max_val=SEQ // CAP)
            s4 = sel.rearrange("p (m e s) -> p m e s", m=NM, e=2)
            g4 = selg.rearrange("p (m e s) -> p m e s", m=NM, e=2)
            io = iota.unsqueeze(1).to_broadcast([P, 2, CAP])
            with pool.Fori(0, rounds) as r:
                with pool.Fori(0, PAIRS) as p:
                    n = r * PAIRS + p
                    pool.wait_ge(sem("combT"), n + 1)
                    for m in range(NM):
                        i = nc.gpsimd.tensor_tensor(
                            s4[:, m], io, pos[:, bass.ds(m * NE + 2 * p, 2)].unsqueeze(2).to_broadcast([P, 2, CAP]),
                            ALU.subtract)
                    pool.drain()
                    nc.gpsimd.tensor_scalar(sel, sel, 0.0, None, ALU.is_equal).then_inc(sem("sel"), 1)
                    pool.wait_ge(sem("sel"), n + 1)
                    for m in range(NM):
                        i = nc.gpsimd.tensor_tensor(
                            g4[:, m], s4[:, m],
                            Wt[:, bass.ds(m * NE + 2 * p, 2)].unsqueeze(2).to_broadcast([P, 2, CAP]), ALU.mult)
                    i.then_inc(sem("selg"), 1)
                pool.drain()
                nc.gpsimd.tensor_scalar(pos, pos, float(-CAP), None, ALU.add)
                pool.drain()
            wait(pool, ("ss3", 2))
            link(nc.gpsimd.tensor_scalar(ss2, ss2, 1.0 / D, EPS, ALU.mult, ALU.add))
            nc.gpsimd.tensor_tensor(rstd2, ss2, pw[:, 0:NM], ALU.pow).then_inc(sem("rstd3"), 1)

        @block.scalar
        def _(act):
            def high(x):
                act.wait_ge(sem(f"raw{x % RING_A}"), 16 * (x // RING_A + 1))
                if x >= NSPLIT:
                    act.wait_ge(sem("chunk"), x - NSPLIT + 1)
                nc.scalar.activation(w_hi[x % NSPLIT], ringA[:, x % RING_A, :], ACT.Copy).then_inc(sem("w_hi"), 1)

            def evac(b):
                which, i, _ = BLOCKS[b]
                act.wait_ge(sem("chunk"), BCH * (b + 1))
                if b == 0:
                    wait(act, ("rstd", 1))
                if which == "gdn1" and i == 0:
                    wait(act, ("obT", 2))
                if which == "gateA" and i == 0:
                    wait(act, ("oaT", 1))
                dst = zsl(which, i)
                for m in range(NM):
                    if which in ("gateA", "gateB"):
                        j = nc.scalar.activation(dst[:, m, :], bank(2 * (b % 2) + m), ACT.Tanh,
                                                 scale=rstdh[:, m:m + 1])
                    else:
                        j = nc.scalar.activation(dst[:, m, :], bank(2 * (b % 2) + m), ACT.Copy,
                                                 scale=rstd[:, m:m + 1])
                j.then_inc(sem("z"), 1)

            def result(step):
                sp_.before(step)
                wait(act, full(step))

            for m in range(NM):
                act.wait_ge(sem(f"x_in{m}"), 16)
                nc.scalar.activation(Z1[:, m * D:(m + 1) * D], xs0[:, m, :], ACT.Square,
                                     accum_out=ss1[:, m:m + 1]).then_inc(sem("ss1"), 1)
            act.wait_ge(sem("nmix_in"), 16)
            for i in range(8):
                act.wait_ge(sem("xTp"), i + 1)
                for k in range(2):
                    j = nc.scalar.activation(hTh[:, 2 * i + k, :], bank(i)[:, k * SEQ:(k + 1) * SEQ], ACT.Copy,
                                             scale=nmix[:, 2 * i + k:2 * i + k + 1])
                j.then_inc(sem("hTh"), 1)
            sp_ = Splitter(high, evac)
            act.wait_ge(sem("small_in"), SMALL)
            sp_.follow(FIRST_BLOCKS * BCH)
            result("small")
            nc.scalar.activation(T_["bo"][0:NSM, 0:SEQ], pair("small")[0:NSM, 0:SEQ], ACT.Copy)\
                .then_inc(sem("small_t"), 1)
            result("smallT")
            zp = pair("smallT")[:, 0:NM * NSM].rearrange("p (m c) -> p m c", m=NM)
            for m in range(NM):
                i = nc.scalar.activation(zs3[:, m, :], zp[:, m, :], ACT.Copy, scale=rstd[:, m:m + 1])
            i.then_inc(sem("zs"), 1)
            act.wait_ge(sem("zs"), 1)
            nc.scalar.activation(mh(beta), zs3[:, :, 0:A_HEADS], ACT.Tanh, scale=0.5).then_inc(sem("tbeta"), 1)
            result("blrT")
            nc.scalar.activation(T_["blrT"][0:RANK, :], pair("blrT")[0:RANK, 0:SEQ], ACT.Copy)\
                .then_inc(sem("blrT"), 1)
            wait(act, ("na", 1))
            nc.scalar.activation(na, na, ACT.Exp).then_inc(sem("ena"), 1)
            nc.scalar.activation(alog, alog, ACT.Exp).then_inc(sem("ealog"), 1)
            act.wait_ge(sem("ena"), 1)
            nc.scalar.activation(na, na, ACT.Ln, bias=1.0).then_inc(sem("lna"), 1)
            sp_.before("gc")
            wait(act, ("gcol", 1))
            nc.scalar.activation(eg, gcol, ACT.Exp).then_inc(sem("eg"), 1)
            nc.scalar.activation(ekd, gdif, ACT.Exp).then_inc(sem("ekd"), 1)
            sp_.before("gkT")
            wait(act, ("gkn", 1))
            nc.scalar.activation(T_["bE"], T_["bE"], ACT.Exp).then_inc(sem("gke"), 1)
            act.wait_ge(sem("gke"), 1)
            nc.scalar.activation(T_["bE"], T_["bE"], ACT.Ln, bias=1.0).then_inc(sem("gkl"), 1)
            result("bqT")
            nc.scalar.activation(T_["bqT"], pair("bqT"), ACT.Copy, scale=QSCALE).then_inc(sem("bqT"), 1)
            for i, b in enumerate(LEVELS):
                if i == 0:
                    sp_.before("lv_eye")
                else:
                    sp_.rest()
                wait(act, ("bdist", i + 1))
                nc.scalar.activation(T_["bE"], T_["bE"], ACT.Exp, scale=1.0 / GATE_NORM).then_inc(sem("bE"), 1)
                if i:
                    sp_.before(f"lv{LEVELS[i - 1]}")
            sp_.before("lv64")
            wait(act, ("bedge", 1))
            nc.scalar.activation(T_["bE"], T_["bE"], ACT.Exp, scale=1.0 / GATE_NORM).then_inc(sem("bE"), 1)
            result("kd")
            nc.scalar.activation(T_["kdtok"], pair("kd")[:, 0:512], ACT.Copy).then_inc(sem("kdtok"), 1)
            result("bS")
            nc.scalar.activation(T_["bS"], pair("bS"), ACT.Copy).then_inc(sem("bS"), 1)
            bg = Z1[:, 4 * 1024:6 * 1024]
            nc.scalar.activation(T_["bth"], bg, ACT.Tanh, scale=0.5).then_inc(sem("bth"), 1)
            for i in range(2):
                result(f"bo{i}")
                nc.scalar.activation(T_["bo"][:, i * 1024:(i + 1) * 1024], pair(f"bo{i}"), ACT.Copy)\
                    .then_inc(sem("b_o"), 1)
            act.wait_ge(sem("b_o"), 2)
            wait(act, ("edge", 1))
            nc.scalar.activation(T_["bqT"], T_["bo"][:, 0:1024], ACT.Square)
            nc.scalar.activation(T_["bkT"], T_["bo"][:, 1024:2048], ACT.Square).then_inc(sem("b_sq"), 1)

            for g in range(NG):
                s = f".{g}"
                zg = [T_[f"zT{i}"][:, 0:zpad].rearrange("p (h t) -> p h t", h=GH) for i in range(3)]
                Zb = Z0 if g == 0 else Z1
                c = [Zb[:, i * 1024:(i + 1) * 1024] for i in range(3)]
                cwv = cw.rearrange("p (w h k) -> p w h k", w=3, h=A_HEADS)
                if g == 0:
                    wait(act, ("cw", 1))
                for i, w in ((0, "zqT"), (2, "zvT")):
                    result(w + s)
                    nc.scalar.activation(zg[i][:, :, TAPS - 1:], pair(w + s).rearrange("p (h t) -> p h t", h=GH),
                                         ACT.Copy).then_inc(sem(w), 1)
                wait(act, ("zkT", g + 1))
                act.wait_ge(sem("zqT"), g + 1)
                act.wait_ge(sem("zvT"), g + 1)
                for i in range(3):
                    for h in range(GH):
                        j = nc.scalar.activation(c[i].rearrange("p (h t) -> p h t", h=GH)[:, h, :],
                                                 zg[i][:, h, 0:SEQ], ACT.Copy,
                                                 scale=cwv[:, i, g * GH + h, 0:1])
                    j.then_inc(sem("tap0"), 1)
                for i in range(3):
                    sp_.before("ssq" + s, most=2 if i else 3)
                    act.wait_ge(sem("conv"), 3 * g + i + 1)
                    nc.scalar.activation(T_[f"zT{i}"][:, 0:1024], c[i], ACT.Tanh, scale=0.5).then_inc(sem("tconv"), 1)
                wait(act, ("Dn", g + 1))
                nc.scalar.activation(T_["Dm"], T_["Dm"], ACT.Exp, scale=-1.0).then_inc(sem("expD"), 1)
                wait(act, ("DTn", g + 1))
                nc.scalar.activation(T_["DT"], T_["DT"], ACT.Exp).then_inc(sem("expDT"), 1)
                for i in range(2):
                    act.wait_ge(sem("silu"), 3 * g + i + 1)
                    nc.scalar.activation(T_[f"zT{i}"][:, 0:1024], c[i], ACT.Square).then_inc(sem("sq"), 1)
                result("khT" + s)
                nc.scalar.activation(T_["zT1"][:, 0:1024], pair("khT" + s), ACT.Copy).then_inc(sem("khT"), 1)
                for i, b in enumerate(LEVELS[1:]):
                    result(f"Y{b}" + s)
                    nc.scalar.activation(T_["Y"], pair(f"Y{b}" + s), ACT.Copy).then_inc(sem("Y"), 1)
                    sp_.rest()
                result("wT" + s)
                nc.scalar.activation(T_["nwT"], pair("wT" + s)[:, 0:512], ACT.Copy, scale=-1.0)\
                    .then_inc(sem("wT"), 1)
                result("u0" + s)
                vn = units(T_["T"])
                nc.scalar.activation(T_["T"][:, 0:512], pair("u0" + s)[:, 0:512], ACT.Copy).then_inc(sem("u0"), 1)
                result("S" + s)
                nc.scalar.activation(T_["aS"], pair("S" + s)[:, 0:512], ACT.Copy).then_inc(sem("a_S"), 1)
                result("v1" + s)
                nc.scalar.activation(T_["T"][:, 512:1024], pair("v1" + s)[:, 0:512], ACT.Copy).then_inc(sem("v1"), 1)
                nc.scalar.activation(T_["L1"], Zb[:, 3 * 1024:4 * 1024], ACT.Tanh, scale=0.5).then_inc(sem("tz"), 1)
                sp_.before("o" + s)
                wait(act, ("a_o", g + 1))
                nc.scalar.activation(T_["zT1"][:, 0:1024], T_["Y"], ACT.Square).then_inc(sem("a_sq"), 1)

            sp_.before(STEPS[-1])
            sp_.follow(CH_MIX)
            wait(act, ("oaT", NG))
            for i, o in enumerate((oaT_f, obT_f)):
                nc.scalar.activation(o_hi[i], o, ACT.Copy).then_inc(sem("o_hi"), 1)
            for j, (c, a_at, b_at, end) in enumerate(MERGE):
                if c >= PRE:
                    sp_.follow(a_at)
                    act.wait_ge(sem("chunk"), a_at)
                    if j:
                        wait(act, ("merged", j))
                    for m in range(NM):
                        i = nc.scalar.activation(tb[:, m, :], bank(m), ACT.Tanh, scale=rstdh[:, m:m + 1])
                    i.then_inc(sem("tb"), 1)
                sp_.follow(end)
            for i in range(8):
                act.wait_ge(sem("mTp"), i + 1)
                nc.scalar.activation(hTh[:, 2 * i:2 * i + 2, :].rearrange("p k t -> p (k t)"), bank(i), ACT.Copy,
                                     scale=0.5).then_inc(sem("mTh"), 1)
            for c in range(NC):
                sp_.follow(min(CH_MERGE + BCH * (c + 1) + 1, CHUNKS))
                act.wait_ge(sem("x1"), 2 * (c + 1))
                for m in range(NM):
                    if c or m:
                        act.wait_ge(sem("sq2"), NM * c + m)
                    nc.scalar.activation(sqs, x1[:, m, c * CB:(c + 1) * CB], ACT.Square,
                                         accum_out=ssp[:, m * NC + c:m * NC + c + 1]).then_inc(sem("sq2"), 1)
                wait(act, ("x1Tp", c + 1))
                nc.scalar.activation(x1c[c % 2].rearrange("p k t -> p (k t)"), psum[:, 4 * CB:6 * CB], ACT.Copy)\
                    .then_inc(sem("x1T"), 1)
            wait(act, ("rstd2", 1))
            for m in range(NM):
                nc.scalar.activation(h2[:, m, :], x1[:, m, :], ACT.Copy, scale=rstd2[:, m:m + 1])\
                    .then_inc(sem("h2"), 1)
            wait(act, ("r_d", 1))
            nc.scalar.activation(rt["ed"], rt["d"], ACT.Exp).then_inc(sem("r_ed"), 1)
            wait(act, ("r_dm", 1))
            nc.scalar.activation(rt["e2"], rt["dm"], ACT.Exp).then_inc(sem("r_e2"), 1)

            wait(act, ("rounds_ready", 1))
            rounds = act.value_load(rounds_i[0:1, 0:1], min_val=1, max_val=SEQ // CAP)
            with act.Fori(0, rounds) as r:
                with act.Fori(0, PAIRS) as p:
                    n = r * PAIRS + p
                    act.wait_ge(sem("combT"), n + 2)
                    nc.scalar.activation(comb, bank(2, SEQ), ACT.Copy).then_inc(sem("comb"), 1)
                    act.wait_ge(sem("slotM_free"), n * PER_PAIR + RING_M + 4)
                    nc.scalar.activation(hth, bank(0), ACT.Tanh, scale=0.5).then_inc(sem("hth"), 1)
                    act.wait_ge(sem("actT"), n + 1)
                    nc.scalar.activation(aT, bank(3), ACT.Copy).then_inc(sem("aT"), 1)
                    for k in range(NC):
                        if k % 2 == 0:
                            act.wait_ge(sem("down"), n * 2 + k // 2 + 1)
                        else:
                            act.wait_ge(sem("slotM_free"), n * PER_PAIR + RING_M + 8 + k + 1)
                        nc.scalar.activation(Ysb[:, k * CB:(k + 1) * CB], bank(4 + k % 2), ACT.Copy)\
                            .then_inc(sem("yev"), 1)
            act.wait_ge(sem("loop_done"), 1)
            for m in range(NM):
                nc.scalar.activation(junk, x1[:, m, :], ACT.Square, accum_out=ss2[:, m:m + 1])\
                    .then_inc(sem("ss3"), 1)
                act.wait_ge(sem("ss3"), m + 1)

        @block.vector
        def _(dve):
            links = [0]

            def link(ins):
                links[0] += 1
                ins.then_inc(sem("dve_link"), 1)
                dve.wait_ge(sem("dve_link"), links[0])

            tt = nc.vector.tensor_tensor
            ts = nc.vector.tensor_scalar
            stt = nc.vector.scalar_tensor_tensor

            def low(x):
                dve.wait_ge(sem("w_hi"), x + 1)
                tt(w_lo[x % NSPLIT], ringA[:, x % RING_A, :], w_hi[x % NSPLIT].bitcast(F32), ALU.subtract)\
                    .then_inc(sem("w_lo"), 1)

            def result(step):
                sp_.before(step)
                wait(dve, full(step))

            dve.wait_ge(sem("nmix_in"), 16)
            for i in range(8):
                dve.wait_ge(sem("hTh"), i + 1)
                for k in range(2):
                    j = stt(hTl[:, 2 * i + k, :], bank(i)[:, k * SEQ:(k + 1) * SEQ], nmix[:, 2 * i + k:2 * i + k + 1],
                            hTh[:, 2 * i + k, :].bitcast(F32), ALU.mult, ALU.subtract)
                j.then_inc(sem("hTl"), 1)
            sp_ = Splitter(low, lambda b: None)
            sp_.follow(FIRST_BLOCKS * BCH)
            result("cw")
            nc.vector.tensor_copy(cw, pair("cw")[:, 0:96]).then_inc(sem("cw"), 1)
            dve.wait_ge(sem("small_in"), SMALL)
            wait(dve, ("zs", 1))
            link(tt(mh(xa), zs3[:, :, A_HEADS:2 * A_HEADS], dtb.unsqueeze(1).to_broadcast([P, NM, A_HEADS]), ALU.add))
            stt(na, xa, -1.0, xa, ALU.mult, ALU.min).then_inc(sem("na"), 1)
            wait(dve, ("tbeta", 1))
            link(ts(beta, beta, 0.5, 0.5, ALU.mult, ALU.add))
            ts(bhalf, beta, 0.5, None, ALU.mult)
            wait(dve, ("lna", 1))
            link(stt(xa, xa, 0.0, na, ALU.max, ALU.add))
            link(tt(mh(xa), mh(xa), alog.unsqueeze(1).to_broadcast([P, NM, A_HEADS]), ALU.mult))
            ts(gdec, xa, -1.0, None, ALU.mult).then_inc(sem("gdec"), 1)
            result("gc")
            link(nc.vector.tensor_copy(gcol, pair("gc")[:, 0:half16]))
            tt(gdif, pair("gc")[:, half16:2 * half16], gcol, ALU.subtract).then_inc(sem("gcol"), 1)
            wait(dve, ("eg", 1))
            tt(beg, beta, eg, ALU.mult).then_inc(sem("beg"), 1)
            result("gkT")
            dve.wait_ge(sem("small_in"), SMALL)
            b4 = T_["bT"].rearrange("p (h t) -> p h t", h=B_HEADS)
            tt(b4, pair("gkT").rearrange("p (h t) -> p h t", h=B_HEADS),
               bgk.unsqueeze(2).to_broadcast([P, B_HEADS, SEQ]), ALU.add).then_inc(sem("gkx"), 1)
            dve.wait_ge(sem("gkx"), 1)
            stt(T_["bE"], T_["bT"], -1.0, T_["bT"], ALU.mult, ALU.min).then_inc(sem("gkn"), 1)
            wait(dve, ("gkl", 1))
            link(stt(T_["bE"], T_["bT"], 0.0, T_["bE"], ALU.min, ALU.subtract))
            for u in range(GU):
                sl = slice(u * P, (u + 1) * P)
                i = nc.vector.tensor_tensor_scan(T_["bT"][:, sl], ones, T_["bE"][:, sl], 0.0, ALU.mult, ALU.add)
            link(i)
            result("bkT")
            nc.vector.tensor_copy(T_["bkT"], pair("bkT")).then_inc(sem("bkT"), 1)
            result("lv_eye")
            tt(units(T_["attn"]), units(pair("lv_eye")), ident.unsqueeze(1).to_broadcast([P, GU, P]), ALU.mult)\
                .then_inc(sem("attn_tmp"), 1)
            qm, km = Z1[:, 0:1024], Z1[:, 1024:2048]
            nc.vector.memset(qm, 0.0)
            link(nc.vector.memset(km, 0.0))
            dve.wait_ge(sem("bqT"), 1)
            dve.wait_ge(sem("bkT"), 1)

            def add_level(i):
                b = LEVELS[i]
                result(f"lv{b}")
                tt(units(T_["btmp"]), units(pair(f"lv{b}")), mask[b].unsqueeze(1).to_broadcast([P, GU, P]), ALU.mult)\
                    .then_inc(sem("attn_tmp"), 1)
                dve.wait_ge(sem("attn_tmp"), i + 2)
                tt(T_["attn"], T_["attn"], T_["btmp"], ALU.add).then_inc(sem("attn"), 1)
                dve.wait_ge(sem("attn"), i + 1)

            for i, b in enumerate(LEVELS):
                nb = 1024 // (2 * b)

                def halves(t):
                    v = t.rearrange("p (m s r) -> p m s r", s=2, r=b)
                    return v[:, :, 0, :], v[:, :, 1, :]

                (blo, bup), (elo, eup) = halves(T_["bT"]), halves(T_["bE"])
                ref = blo[:, :, b - 1:b].to_broadcast([P, nb, b])
                if i:
                    dve.wait_ge(sem("qkm"), i)
                tt(elo, ref, blo, ALU.subtract)
                tt(eup, bup, ref, ALU.subtract).then_inc(sem("bdist"), 1)
                dve.wait_ge(sem("bE"), i + 1)
                if i:
                    result(f"lv{LEVELS[i - 1]}")
                tt(halves(km)[0], halves(T_["bkT"])[0], elo, ALU.mult)
                tt(halves(qm)[1], halves(T_["bqT"])[1], eup, ALU.mult).then_inc(sem("qkm"), 1)
                sp_.rest()
                if i:
                    add_level(i - 1)
            add_level(len(LEVELS) - 1)
            bu = T_["bT"].rearrange("p (h n t) -> p h n t", h=B_HEADS, n=NM)
            eu = T_["bE"].rearrange("p (h n t) -> p h n t", h=B_HEADS, n=NM)
            dve.wait_ge(sem("qkm"), len(LEVELS))
            nc.vector.tensor_copy(eu[:, :, 1, :], bu[:, :, 1, :])
            tt(eu[:, :, 0, :], bu[:, :, 0, P - 1:P].to_broadcast([P, B_HEADS, P]), bu[:, :, 0, :], ALU.subtract)\
                .then_inc(sem("bedge"), 1)
            dve.wait_ge(sem("bE"), 8)
            tt(units(T_["kdT"], B_HEADS), T_["bkT"].rearrange("p (h n t) -> p h n t", h=B_HEADS, n=NM)[:, :, 0, :],
               eu[:, :, 0, :], ALU.mult)
            result("lv64")
            q4 = qm.rearrange("p (h n t) -> p h n t", h=B_HEADS, n=NM)
            tt(q4[:, :, 1, :], T_["bqT"].rearrange("p (h n t) -> p h n t", h=B_HEADS, n=NM)[:, :, 1, :],
               eu[:, :, 1, :], ALU.mult).then_inc(sem("edge"), 1)
            sp_.before("bS")
            dve.wait_ge(sem("bth"), 1)
            bg = Z1[:, 4 * 1024:6 * 1024]
            link(stt(T_["bth"], T_["bth"], 1.0, bg, ALU.add, ALU.mult))
            sp_.before("bo1")
            dve.wait_ge(sem("b_sq"), 1)
            nc.vector.reduce_sum(rms[:, 0:4], T_["bqT"].rearrange("p (h e) -> p h e", h=B_HEADS), axis=AX.X)
            link(nc.vector.reduce_sum(rms[:, 4:8], T_["bkT"].rearrange("p (h e) -> p h e", h=B_HEADS), axis=AX.X))
            ts(rms[:, 0:8], rms[:, 0:8], 1.0 / B_DV, EPS, ALU.mult, ALU.add).then_inc(sem("b_ms"), 1)
            wait(dve, ("b_rf", 1))
            o3 = T_["bo"].rearrange("p (u e) -> p u e", u=8)
            link(tt(o3, o3, rmf[:, 0:8].unsqueeze(2).to_broadcast([P, 8, B_DV]), ALU.mult))
            for n in range(NM):
                i = tt(T_["bo"][:, n * 1024:(n + 1) * 1024].rearrange("p (a c) -> p a c", a=2),
                       T_["bo"][:, n * 1024:(n + 1) * 1024].rearrange("p (a c) -> p a c", a=2),
                       T_["bth"].rearrange("p (a n c) -> p a n c", a=2, n=NM)[:, :, n, :], ALU.mult)
            i.then_inc(sem("b_out"), 1)
            dve.wait_ge(sem("small_in"), SMALL)
            for i in range(2):
                result(f"obT{i}")
                for hf in range(2):
                    src = pair(f"obT{i}").rearrange("p (h f t) -> p h f t", h=2, f=2)[:, :, hf, :]
                    dst = obT[:, 4 * i:4 * i + 4, :].rearrange("p (h f) t -> p h f t", f=2)[:, :, hf, :]
                    j = ts(dst, src, bnorm[:, hf:hf + 1], 0.5, ALU.mult, ALU.mult)
                j.then_inc(sem("obT"), 1)

            for g in range(NG):
                s = f".{g}"
                Zb = Z0 if g == 0 else Z1
                c = [Zb[:, i * 1024:(i + 1) * 1024] for i in range(3)]
                zg = [T_[f"zT{i}"][:, 0:zpad].rearrange("p (h t) -> p h t", h=GH) for i in range(3)]
                hs_g = slice(g * GH, (g + 1) * GH)

                def per_unit(t):
                    return mh(t)[:, :, hs_g].rearrange("p n h -> p h n").unsqueeze(3).to_broadcast([P, GH, NM, P])

                def u4(t):
                    return t.rearrange("p (h n t) -> p h n t", h=GH, n=NM)

                if g:
                    result(f"oaT.{g - 1}")
                for i in range(3):
                    nc.vector.memset(zg[i][:, :, 0:TAPS - 1], 0.0)
                result("zkT" + s)
                nc.vector.tensor_copy(zg[1][:, :, TAPS - 1:], pair("zkT" + s).rearrange("p (h t) -> p h t", h=GH))\
                    .then_inc(sem("zkT"), 1)
                result("gcb" + s)
                for what, op, dst in (("Dn", ALU.max, "Dm"), ("DTn", ALU.min, "DT")):
                    link(tt(u4(T_[dst]), u4(pair("gcb" + s)), per_unit(gcol), ALU.subtract))
                    i = ts(T_[dst], T_[dst], 0.0, None, op)
                    i.then_inc(sem(what), 1)
                nc.vector.memset(rms[:, 15:16], 0.0).then_inc(sem("gcb"), 1)
                cwv = cw.rearrange("p (w h k) -> p w h k", w=3, h=A_HEADS)
                for w in range(3):
                    dve.wait_ge(sem("tap0"), 3 * g + w + 1)
                    c4 = c[w].rearrange("p (h t) -> p h t", h=GH)
                    for k in range(1, TAPS):
                        if k < 3:
                            sp_.before("ssq" + s, most=1)
                        for h in range(GH):
                            wk = cwv[:, w, g * GH + h, k:k + 1]
                            src = zg[w][:, h, k:k + SEQ]
                            i = stt(c4[:, h, :], src, wk, c4[:, h, :], ALU.mult, ALU.add)
                        if k < TAPS - 1:
                            link(i)
                    i.then_inc(sem("conv"), 1)
                for w in range(3):
                    dve.wait_ge(sem("tconv"), 3 * g + w + 1)
                    stt(c[w], T_[f"zT{w}"][:, 0:1024], 1.0, c[w], ALU.add, ALU.mult).then_inc(sem("silu"), 1)
                result("ssq" + s)
                ts(ssqk, pair("ssq" + s)[:, 0:16], 4 * EPS, None, ALU.add).then_inc(sem("ssqk"), 1)
                wait(dve, ("rqk", g + 1))
                result("ktok" + s)
                tt(units(T_["zT0"][:, 0:1024]), units(pair("ktok" + s)),
                   rqk[:, 8:16].unsqueeze(2).to_broadcast([P, GU, P]), ALU.mult).then_inc(sem("ktok"), 1)
                result("vtok" + s)
                tt(u4(T_["zT2"][:, 0:1024]), u4(pair("vtok" + s)), per_unit(bhalf), ALU.mult)\
                    .then_inc(sem("vtok"), 1)
                result("A" + s)
                wait(dve, ("DA", g + 1))
                tt(T_["Dm"], pair("A" + s), T_["Dm"], ALU.mult).then_inc(sem("A"), 1)
                result("PT" + s)
                wait(dve, ("DTm", g + 1))
                tt(T_["DT"], pair("PT" + s), T_["DT"], ALU.mult).then_inc(sem("PT"), 1)
                idb = ident.unsqueeze(1).to_broadcast([P, GU, P])
                result("Y1" + s)
                stt(units(T_["U"]), units(pair("Y1" + s)), -1.0, idb, ALU.mult, ALU.add).then_inc(sem("U"), 1)
                stt(units(T_["T"]), units(T_["gB"]), -1.0, idb, ALU.mult, ALU.add).then_inc(sem("T"), 1)
                for i, b in enumerate(LEVELS[1:]):
                    result(f"dU{b}" + s)
                    if b != 64:
                        result(f"dT{b}" + s)
                    dve.wait_ge(sem("U"), 7 * g + i + 1)
                    tt(T_["U"], T_["U"], pair(f"dU{b}" + s), ALU.subtract).then_inc(sem("U"), 1)
                    if b != 64:
                        dve.wait_ge(sem("T"), 6 * g + i + 1)
                        tt(T_["T"], T_["T"], pair(f"dT{b}" + s), ALU.subtract).then_inc(sem("T"), 1)
                    sp_.rest()
                result("oi" + s)
                tt(units(T_["inter"], GH), units(pair("oi" + s)[:, 0:512], GH),
                   mh(eg)[:, 1, hs_g].unsqueeze(2).to_broadcast([P, GH, P]), ALU.mult).then_inc(sem("inter"), 1)
                result("o" + s)
                nc.vector.tensor_copy(u4(T_["Y"])[:, :, 0, :], u4(pair("o" + s))[:, :, 0, :])
                dve.wait_ge(sem("inter"), g + 1)
                tt(u4(T_["Y"])[:, :, 1, :], u4(pair("o" + s))[:, :, 1, :], units(T_["inter"], GH), ALU.add)\
                    .then_inc(sem("a_o"), 1)
                dve.wait_ge(sem("tz"), g + 1)
                link(stt(T_["L1"], T_["L1"], 1.0, Zb[:, 3 * 1024:4 * 1024], ALU.add, ALU.mult))
                dve.wait_ge(sem("a_sq"), g + 1)
                nc.vector.reduce_sum(rms[:, 0:8], units(T_["zT1"][:, 0:1024]), axis=AX.X).then_inc(sem("a_ms"), 1)
                wait(dve, ("a_rf", g + 1))
                link(tt(units(T_["Y"]), units(T_["Y"]), rmf[:, 0:8].unsqueeze(2).to_broadcast([P, GU, P]), ALU.mult))
                tt(u4(T_["Y"]), u4(T_["Y"]), T_["L1"].rearrange("p (n h t) -> p h n t", h=GH, n=NM), ALU.mult)\
                    .then_inc(sem("a_out"), 1)
                if g == 0:
                    dve.wait_ge(sem("small_in"), SMALL)
                result("oaT" + s)
                ts(oaT[:, g * GH:(g + 1) * GH, :], pair("oaT" + s).rearrange("p (h t) -> p h t", h=GH), anorm, 0.5,
                   ALU.mult, ALU.mult).then_inc(sem("oaT"), 1)

            sp_.before(STEPS[-1])
            sp_.follow(CH_MIX)
            for i, o in enumerate((oaT_f, obT_f)):
                dve.wait_ge(sem("o_hi"), i + 1)
                tt(o_lo[i], o, o_hi[i].bitcast(F32), ALU.subtract).then_inc(sem("o_lo"), 1)
            for j, (c, a_at, b_at, end) in enumerate(MERGE):
                cs = slice(c * CB, (c + 1) * CB)
                if j == 0:
                    dve.wait_ge(sem("z"), len(BLOCKS))
                sp_.follow(b_at)
                dve.wait_ge(sem("chunk"), b_at)
                for m in range(NM):
                    i = stt(gateA[:, m, cs], gateA[:, m, cs], 1.0, bank(2 + m), ALU.add, ALU.mult)
                i.then_inc(sem("gya"), 1)
                sp_.follow(end)
                dve.wait_ge(sem("chunk"), end)
                if c >= PRE:
                    gate_b = tb
                    dve.wait_ge(sem("tb"), j + 1)
                else:
                    gate_b = zsl("gateB", c)
                for m in range(NM):
                    i = stt(tyb[:, m, :], gate_b[:, m, :], 1.0, bank(4 + m), ALU.add, ALU.mult)
                i.then_inc(sem("gyb"), 1)
                dve.wait_ge(sem("gyb"), j + 1)
                dve.wait_ge(sem("gya"), j + 1)
                tt(gateA[:, :, cs], gateA[:, :, cs], tyb, ALU.add).then_inc(sem("merged"), 1)
                dve.wait_ge(sem("merged"), j + 1)
            for i in range(8):
                dve.wait_ge(sem("mTh"), i + 1)
                stt(hTl[:, 2 * i:2 * i + 2, :].rearrange("p k t -> p (k t)"), bank(i), 0.5,
                    hTh[:, 2 * i:2 * i + 2, :].rearrange("p k t -> p (k t)").bitcast(F32), ALU.mult, ALU.subtract)\
                    .then_inc(sem("mT"), 1)
            for c in range(NC):
                cs = slice(c * CB, (c + 1) * CB)
                sp_.follow(CH_MERGE + BCH * (c + 1))
                dve.wait_ge(sem("chunk"), CH_MERGE + BCH * (c + 1))
                for m in range(NM):
                    if c == 0 and m == 0:
                        dve.wait_ge(sem("x_back"), 16 * NM)
                    tt(x1[:, m, cs], bank(2 * (c % 2) + m), x1[:, m, cs], ALU.add).then_inc(sem("x1"), 1)
            dve.wait_ge(sem("sq2"), NM * NC)
            nc.vector.reduce_sum(ss2, ssp.rearrange("p (m c) -> p m c", m=NM), axis=AX.X).then_inc(sem("ss2"), 1)
            dve.wait_ge(sem("small_in"), SMALL)
            dve.wait_ge(sem("logits"), NC)
            R = GROUPS + NE
            lp = [bank(6 + m, R) for m in range(NM)]

            def m_(t):
                return t.rearrange("p (m c) -> p m c", m=NM)

            def spread(t, n):
                return t.unsqueeze(2).to_broadcast([P, NM, n])

            def first(eq, cum, out, n):
                for m in range(NM):
                    i = nc.vector.tensor_tensor_scan(cum[:, m * n:(m + 1) * n], ones[:, 0:n], eq[:, m * n:(m + 1) * n],
                                                     0.0, ALU.mult, ALU.add)
                link(i)
                link(stt(out, cum, 1.0, eq, ALU.is_le, ALU.mult))

            wait(dve, ("rstd2", 1))
            for m in range(NM):
                stt(m_(rt["lg"])[:, m, :], lp[m][:, 0:GROUPS], rstd2[:, m:m + 1], brg, ALU.mult, ALU.add)
                i = stt(m_(rt["le"])[:, m, :], lp[m][:, GROUPS:R], rstd2[:, m:m + 1], bre, ALU.mult, ALU.add)
            link(i)
            link(nc.vector.reduce_max(rt["gm"], m_(rt["lg"]), axis=AX.X))
            tt(m_(rt["d"]), m_(rt["lg"]), spread(rt["gm"], GROUPS), ALU.subtract).then_inc(sem("r_d"), 1)
            dve.wait_ge(sem("r_d"), 1)
            link(ts(rt["eq"][:, 0:8], rt["d"], 0.0, None, ALU.is_equal))
            first(rt["eq"][:, 0:8], rt["cum"][:, 0:8], rt["fg"], GROUPS)
            fg4 = m_(rt["fg"]).unsqueeze(3).to_broadcast([P, NM, GROUPS, EPG])

            def mge(t):
                return t.rearrange("p (m g e) -> p m g e", m=NM, g=GROUPS)

            link(tt(mge(rt["pr"]), mge(rt["le"]), fg4, ALU.mult))
            link(nc.vector.tensor_reduce(m_(rt["ls"]), rt["pr"].rearrange("p (m g e) -> p m e g", m=NM, g=GROUPS),
                                         AX.X, ALU.add))
            link(nc.vector.reduce_max(rt["m1"], m_(rt["ls"]), axis=AX.X))
            link(tt(m_(rt["d1"]), m_(rt["ls"]), spread(rt["m1"], EPG), ALU.subtract))
            link(ts(rt["eq"], rt["d1"], 0.0, None, ALU.is_equal))
            first(rt["eq"], rt["cum"], rt["f1"], EPG)
            link(stt(rt["ls2"], rt["f1"], NEG, rt["ls"], ALU.mult, ALU.add))
            link(nc.vector.reduce_max(rt["m2"], m_(rt["ls2"]), axis=AX.X))
            tt(rt["dm"], rt["m2"], rt["m1"], ALU.subtract).then_inc(sem("r_dm"), 1)
            link(tt(m_(rt["d2"]), m_(rt["ls2"]), spread(rt["m2"], EPG), ALU.subtract))
            link(ts(rt["eq"], rt["d2"], 0.0, None, ALU.is_equal))
            first(rt["eq"], rt["cum"], rt["f2"], EPG)
            link(tt(rt["fs"], rt["f1"], rt["f2"], ALU.add))
            tt(mge(Mt), m_(rt["fs"]).unsqueeze(2).to_broadcast([P, NM, GROUPS, EPG]), fg4, ALU.mult)\
                .then_inc(sem("Mt"), 1)
            dve.wait_ge(sem("r_ed"), 1)
            link(nc.vector.reduce_sum(rt["den"], m_(rt["ed"]), axis=AX.X))
            dve.wait_ge(sem("r_e2"), 1)
            link(ts(rt["s2"], rt["e2"], 1.0, None, ALU.add))
            link(tt(rt["s2"], rt["s2"], rt["den"], ALU.mult))
            link(nc.vector.reciprocal(rt["r2"], rt["s2"]))
            link(ts(rt["w1"], rt["r2"], 0.5, None, ALU.mult))
            link(tt(rt["w2"], rt["w1"], rt["e2"], ALU.mult))
            tt(m_(rt["ws"]), m_(rt["f1"]), spread(rt["w1"], EPG), ALU.mult)
            link(tt(m_(rt["wa"]), m_(rt["f2"]), spread(rt["w2"], EPG), ALU.mult))
            link(tt(rt["ws"], rt["ws"], rt["wa"], ALU.add))
            tt(mge(Wt), m_(rt["ws"]).unsqueeze(2).to_broadcast([P, NM, GROUPS, EPG]), fg4, ALU.mult)
            dve.wait_ge(sem("ranks"), 1)
            dve.wait_ge(sem("Mt"), 1)
            link(tt(pos, bank(1, NM * NE), Mt, ALU.mult))
            link(ts(pos, pos, 1.0, None, ALU.subtract))
            link(nc.vector.reduce_max(rt["mx"], bank(2, NE), axis=AX.X))
            ts(rt["c1"], rt["mx"], float(CAP), None, ALU.is_gt)
            ts(rt["c2"], rt["mx"], float(2 * CAP), None, ALU.is_gt)
            link(ts(rt["c3"], rt["mx"], float(3 * CAP), 1.0, ALU.is_gt, ALU.add))
            link(tt(rt["c1"], rt["c1"], rt["c2"], ALU.add))
            stt(rounds_i[:, 1:2], rt["c3"], -1.0, rt["c1"], ALU.add, ALU.add)
            tt(rounds_i[:, 0:1], rt["c1"], rt["c3"], ALU.add).then_inc(sem("rounds_ready"), 1)
            dve.wait_ge(sem("rounds_ready"), 1)

            rounds = dve.value_load(rounds_i[0:1, 0:1], min_val=1, max_val=SEQ // CAP)
            with dve.Fori(0, rounds) as r:
                with dve.Fori(0, PAIRS) as p:
                    n = r * PAIRS + p
                    for b in range(4):
                        dve.wait_ge(sem("gath"), n * 4 + b + 1)
                        tt(xeT[:, 4 * b:4 * b + 4, :], bank(2 + b % 2).rearrange("p (k s) -> p k s", k=4),
                           nffn[:, 4 * b:4 * b + 4].unsqueeze(2).to_broadcast([P, 4, P]), ALU.mult)\
                            .then_inc(sem("xe"), 1)
                    dve.wait_ge(sem("hth"), n + 1)
                    stt(hs, hth, 1.0, bank(0), ALU.add, ALU.mult).then_inc(sem("hs"), 1)
                    dve.wait_ge(sem("hs"), n + 1)
                    dve.wait_ge(sem("slotM_free"), n * PER_PAIR + RING_M + 8)
                    tt(hid, hs, bank(1), ALU.mult).then_inc(sem("hid"), 1)
                    for k in range(NC):
                        for m in range(NM):
                            dve.wait_ge(sem("cmb"), n * 8 + 2 * k + m + 1)
                            tt(x1[:, m, k * CB:(k + 1) * CB], x1[:, m, k * CB:(k + 1) * CB], bank(6 + m),
                               ALU.add).then_inc(sem("xadd"), 1)
            dve.wait_ge(sem("xadd"), rounds * (8 * PAIRS) + 2)
            nc.vector.memset(rt["c1"], 0.0).then_inc(sem("loop_done"), 1)
            dve.wait_ge(sem("nfin_in"), 16)
            wait(dve, ("rstd3", 1))
            for m in range(NM):
                stt(x1[:, m, :], x1[:, m, :], rstd2[:, m:m + 1], nfin, ALU.mult, ALU.mult).then_inc(sem("y_ready"), 1)

        @block.tensor
        def _(pe):
            mm, tr = nc.tensor.matmul, nc.tensor.transpose

            def done(step, ins):
                ins.then_inc(sem(full(step)[0]), 1)

            def open_pair(step):
                i = STEPS.index(step)
                if i >= 2:
                    wait(pe, drained(STEPS[i - 2]))

            def chunk(x, m_banks, lhs, k0, start, stop):
                pe.wait_ge(sem("w_lo"), x + 1)
                wh, wl = w_hi[x % NSPLIT], w_lo[x % NSPLIT]
                for m in range(NM):
                    for k in range(CT):
                        cs, ms = slice(k * CB, (k + 1) * CB), slice(m * P, (m + 1) * P)
                        mm(m_banks[m], lhs[0][:, k0 + k, ms], wh[:, cs], start=(start and k == 0), stop=False)
                        mm(m_banks[m], lhs[0][:, k0 + k, ms], wl[:, cs], start=False, stop=False)
                        i = mm(m_banks[m], lhs[1][:, k0 + k, ms], wh[:, cs], start=False,
                               stop=(stop and k == CT - 1))
                i.then_inc(sem("chunk"), 1)

            def project(x):
                b, h = divmod(x, BCH)
                if h == 0 and b >= 2:
                    pe.wait_ge(sem("z"), b - 1)
                chunk(x, (bank(2 * (b % 2)), bank(2 * (b % 2) + 1)), (hTh, hTl), h * CT, h == 0, h == BCH - 1)

            def fill(step):
                for x in FILL[step]:
                    project(x)

            pe.wait_ge(sem("ident"), 1)
            for m in range(NM):
                pe.wait_ge(sem(f"x_in{m}"), 16)
            for i in range(8):
                for k in range(2):
                    for m in range(NM):
                        j = tr(bank(i)[:, (k * NM + m) * P:(k * NM + m + 1) * P], xs0[:, m, 2 * i + k::KT], ident)
                j.then_inc(sem("xTp"), 1)
            wait(pe, ("hTl", 8))
            for x in range(FIRST_BLOCKS * BCH):
                project(x)
            pe.wait_ge(sem("small_in"), SMALL)
            ws3 = wsm[:, 0:KT * NSM].rearrange("p (k c) -> p k c", k=KT)
            for k in range(KT):
                for part in (hTh, hTl):
                    i = mm(pair("small")[0:NSM, 0:SEQ], ws3[:, k, :], part[:, k, :].bitcast(F32),
                           start=(k == 0 and part is hTh), stop=(k == KT - 1 and part is hTl))
            done("small", i)
            fill("small")
            pe.wait_ge(sem("small_in"), SMALL)
            for j in range(3 * A_HEADS):
                i = tr(pair("cw")[:, j * TAPS:(j + 1) * TAPS], convw[:, j * P:(j + 1) * P], ident[0:TAPS, 0:TAPS])
            done("cw", i)
            fill("cw")
            wait(pe, ("small_t", 1))
            for m in range(NM):
                i = tr(pair("smallT")[:, m * NSM:(m + 1) * NSM], T_["bo"][0:NSM, m * P:(m + 1) * P],
                       ident[0:NSM, 0:NSM])
            done("smallT", i)
            fill("smallT")
            open_pair("blrT")
            wait(pe, ("zs", 1))
            for m in range(NM):
                i = tr(pair("blrT")[0:RANK, m * P:(m + 1) * P], zs3[:, m, 2 * A_HEADS:NSM], ident)
            done("blrT", i)
            fill("blrT")
            open_pair("gc")
            pe.wait_ge(sem("consts"), 1)
            wait(pe, ("gdec", 1))
            mm(pair("gc")[:, 0:half16], upT, gdec, start=True, stop=True)
            done("gc", mm(pair("gc")[:, half16:2 * half16], ones, gdec, start=True, stop=True))
            fill("gc")
            open_pair("gkT")
            pe.wait_ge(sem("small_in"), SMALL)
            wait(pe, ("blrT", 1))
            for h in range(B_HEADS):
                i = mm(pair("gkT")[:, h * SEQ:(h + 1) * SEQ], T_["wgk2"][0:RANK, h * P:(h + 1) * P],
                       T_["blrT"][0:RANK, :], start=True, stop=True)
            done("gkT", i)
            fill("gkT")
            for name, blk in (("bqT", 0), ("bkT", 1)):
                open_pair(name)
                pe.wait_ge(sem("z"), blk + 1)
                for h in range(B_HEADS):
                    for n in range(NM):
                        i = tr(pair(name)[:, (h * NM + n) * P:(h * NM + n + 1) * P],
                               zsl("gla", blk)[:, n, h * P:(h + 1) * P], ident)
                done(name, i)
                fill(name)
            open_pair("lv_eye")
            wait(pe, ("bqT", 1))
            wait(pe, ("bkT", 1))
            for u in range(GU):
                sl = slice(u * P, (u + 1) * P)
                i = mm(pair("lv_eye")[:, sl], T_["bkT"][:, sl], T_["bqT"][:, sl], start=True, stop=True)
            done("lv_eye", i)
            fill("lv_eye")
            qm, km = Z1[:, 0:1024], Z1[:, 1024:2048]
            for j, b in enumerate(LEVELS):
                st = f"lv{b}"
                open_pair(st)
                pe.wait_ge(sem("qkm"), j + 1)
                for u in range(GU):
                    sl = slice(u * P, (u + 1) * P)
                    i = mm(pair(st)[:, sl], km[:, sl], qm[:, sl], start=True, stop=True)
                done(st, i)
                fill(st)
            open_pair("kd")
            wait(pe, ("edge", 1))
            for h in range(B_HEADS):
                i = tr(pair("kd")[:, h * P:(h + 1) * P], T_["kdT"][:, h * P:(h + 1) * P], ident)
            done("kd", i)
            fill("kd")

            def vrow(n, h):
                return zsl("gla", 2 + h // 2)[:, n, (h % 2) * B_DV:(h % 2 + 1) * B_DV]

            open_pair("bS")
            wait(pe, ("kdtok", 1))
            pe.wait_ge(sem("z"), 4)
            for h in range(B_HEADS):
                i = mm(pair("bS")[:, h * B_DV:(h + 1) * B_DV], T_["kdtok"][:, h * P:(h + 1) * P], vrow(0, h),
                       start=True, stop=True)
            done("bS", i)
            fill("bS")
            wait(pe, ("attn", len(LEVELS)))
            for n in range(NM):
                st = f"bo{n}"
                open_pair(st)
                if n:
                    wait(pe, ("bS", 1))
                for h in range(B_HEADS):
                    u = h * NM + n
                    sl = slice(u * P, (u + 1) * P)
                    o = pair(st)[:, h * B_DV:(h + 1) * B_DV]
                    i = mm(o, T_["attn"][:, sl], vrow(n, h), start=True, stop=(n == 0))
                    if n:
                        i = mm(o, qm[:, sl], T_["bS"][:, h * B_DV:(h + 1) * B_DV], start=False, stop=True)
                done(st, i)
                fill(st)
            wait(pe, ("b_out", 1))
            for j in range(2):
                st = f"obT{j}"
                open_pair(st)
                for h in range(2):
                    for f in range(2):
                        for n in range(NM):
                            src = T_["bo"][:, n * 1024 + (2 * j + h) * B_DV + f * P:][:, 0:P]
                            i = tr(pair(st)[:, ((h * 2 + f) * NM + n) * P:((h * 2 + f) * NM + n + 1) * P], src, ident)
                done(st, i)
                fill(st)

            for g in range(NG):
                s = f".{g}"
                which = f"gdn{g}"
                first_block = 6 + 4 * g
                Zb = Z0 if g == 0 else Z1
                c = [Zb[:, i * 1024:(i + 1) * 1024] for i in range(3)]

                def per_u(step, f, us=range(GU)):
                    for u in us:
                        i = f(u, slice(u * P, (u + 1) * P))
                    done(step + s, i)
                    fill(step + s)

                def lvl(step, f):
                    open_pair(step + s)
                    o = pair(step + s)
                    per_u(step, lambda u, sl: f(o, u, sl))

                for j, w in enumerate(("zqT", "zkT", "zvT")):
                    open_pair(w + s)
                    pe.wait_ge(sem("z"), first_block + j + 1)
                    o = pair(w + s)
                    per_u(w, lambda u, sl: tr(o[:, sl], zsl(which, j)[:, u % NM, (u // NM) * P:(u // NM + 1) * P],
                                              ident))
                wait(pe, ("gB", g + 1))
                lvl("gcb", lambda o, u, sl: mm(o[:, sl], T_["gB"][:, sl], upT, start=True, stop=True))
                open_pair("ssq" + s)
                pe.wait_ge(sem("sq"), 2 * g + 2)
                o = pair("ssq" + s)
                for j in range(2):
                    for u in range(GU):
                        i = mm(o[:, 8 * j + u:8 * j + u + 1], T_[f"zT{j}"][:, u * P:(u + 1) * P], ones[:, 0:1],
                               start=True, stop=True)
                done("ssq" + s, i)
                fill("ssq" + s)
                lvl("ktok", lambda o, u, sl: tr(o[:, sl], c[1][:, sl], ident))
                pe.wait_ge(sem("silu"), 3 * g + 3)
                lvl("vtok", lambda o, u, sl: tr(o[:, sl], c[2][:, sl], ident))
                lvl("khT", lambda o, u, sl: tr(o[:, sl], T_["zT0"][:, sl], ident))
                wait(pe, ("khT", g + 1))
                kh = T_["zT1"]
                lvl("A", lambda o, u, sl: mm(o[:, sl], kh[:, sl], kh[:, sl], start=True, stop=True))
                lvl("PT", lambda o, u, sl: mm(o[:, sl], kh[:, sl], c[0][:, sl], start=True, stop=True))
                pe.wait_ge(sem("L"), 7 * g + 1)
                lvl("Y1", lambda o, u, sl: mm(o[:, sl], T_["gB"][:, sl], ident, start=True, stop=True))
                for j, b in enumerate(LEVELS[1:]):
                    L = T_["gB"] if (j + 1) % 2 == 0 else T_["L1"]
                    pe.wait_ge(sem("L"), 7 * g + j + 2)
                    pe.wait_ge(sem("U"), 7 * g + j + 1)
                    lvl(f"Y{b}", lambda o, u, sl: mm(o[:, sl], L[:, sl], T_["U"][:, sl], start=True, stop=True))
                    pe.wait_ge(sem("Y"), 6 * g + j + 1)
                    pe.wait_ge(sem("T"), 6 * g + j + 1)
                    lvl(f"dU{b}", lambda o, u, sl: mm(o[:, sl], T_["T"][:, sl], T_["Y"][:, sl], start=True,
                                                      stop=True))
                    if b != 64:
                        lvl(f"dT{b}", lambda o, u, sl: mm(o[:, sl], T_["Y"][:, sl], T_["T"][:, sl], start=True,
                                                          stop=True))
                pe.wait_ge(sem("U"), 7 * g + 7)
                pe.wait_ge(sem("kbg"), g + 1)
                pe.wait_ge(sem("kdec"), g + 1)
                kb = T_["kbg"]

                def per_head(step, f):
                    open_pair(step + s)
                    o = pair(step + s)
                    for h in range(GH):
                        i = f(o[:, h * P:(h + 1) * P], slice(h * P, (h + 1) * P), slice((2 * h) * P, (2 * h + 1) * P),
                              slice((2 * h + 1) * P, (2 * h + 2) * P))
                    done(step + s, i)
                    fill(step + s)

                v = T_["zT2"]
                per_head("wT", lambda o, hh, u0, u1: mm(o, kb[:, u1], T_["U"][:, u1], start=True, stop=True))
                per_head("u0", lambda o, hh, u0, u1: mm(o, T_["U"][:, u0], v[:, u0], start=True, stop=True))
                wait(pe, ("u0", g + 1))
                per_head("S", lambda o, hh, u0, u1: mm(o, T_["kdec"][:, hh], T_["T"][:, hh], start=True, stop=True))
                wait(pe, ("a_S", g + 1))
                wait(pe, ("wT", g + 1))

                def v1(o, hh, u0, u1):
                    mm(o, T_["U"][:, u1], v[:, u1], start=True, stop=False)
                    return mm(o, T_["nwT"][:, hh], T_["aS"][:, hh], start=False, stop=True)

                per_head("v1", v1)
                per_head("oi", lambda o, hh, u0, u1: mm(o, c[0][:, u1], T_["aS"][:, hh], start=True, stop=True))
                wait(pe, ("v1", g + 1))
                wait(pe, ("PT", g + 1))
                lvl("o", lambda o, u, sl: mm(o[:, sl], T_["DT"][:, sl],
                                             T_["T"][:, (u % NM) * 512 + (u // NM) * P:][:, 0:P], start=True,
                                             stop=True))
                wait(pe, ("a_out", g + 1))
                lvl("oaT", lambda o, u, sl: tr(o[:, sl], T_["Y"][:, sl], ident))

            x = CH_MIX
            wait(pe, ("oaT", NG))
            pe.wait_ge(sem("z"), len(BLOCKS))
            oh = [t.rearrange("p (k t) -> p k t", k=A_HEADS) for t in o_hi]
            ol = [t.rearrange("p (k t) -> p k t", k=A_HEADS) for t in o_lo]
            for j, (c, *_) in enumerate(MERGE):
                if c >= PRE:
                    if j:
                        pe.wait_ge(sem("tb"), j)
                    for h in range(BCH):
                        chunk(x, (bank(0), bank(1)), (hTh, hTl), h * CT, h == 0, h == BCH - 1)
                        x += 1
                for w, got in enumerate(("gya", "gyb")):
                    if j:
                        pe.wait_ge(sem(got), j)
                    else:
                        pe.wait_ge(sem("o_lo"), w + 1)
                    for h in range(A_HEADS // CT):
                        chunk(x, (bank(2 + 2 * w), bank(3 + 2 * w)), (oh[w], ol[w]), h * CT, h == 0,
                              h == A_HEADS // CT - 1)
                        x += 1
            wait(pe, ("merged", NC))
            for i in range(8):
                for k in range(2):
                    for m in range(NM):
                        j = tr(bank(i)[:, (k * NM + m) * P:(k * NM + m + 1) * P], gateA[:, m, 2 * i + k::KT], ident)
                j.then_inc(sem("mTp"), 1)
            wait(pe, ("mT", 8))
            R = GROUPS + NE
            wr = wsm.rearrange("p (k c) -> p k c", k=KT)

            def transpose_x1(c):
                pe.wait_ge(sem("x1"), 2 * (c + 1))
                if c:
                    wait(pe, ("x1T", c))
                for k in range(CT):
                    for m in range(NM):
                        i = tr(bank(4 + k // 2)[:, ((k % 2) * NM + m) * P:((k % 2) * NM + m + 1) * P],
                               x1[:, m, (CT * c + k) * P:(CT * c + k + 1) * P], ident)
                i.then_inc(sem("x1Tp"), 1)

            def route(c):
                wait(pe, ("wr", 1))
                wait(pe, ("x1T", c + 1))
                for m in range(NM):
                    for k in range(CT):
                        i = mm(bank(6 + m, R), x1c[c % 2][:, k, m * P:(m + 1) * P],
                               wr[:, CT * c + k, :], start=(c == 0 and k == 0), stop=(c == NC - 1 and k == CT - 1))
                i.then_inc(sem("logits"), 1)

            for c in range(NC):
                if c >= 2:
                    pe.wait_ge(sem("x1"), 2 * (c - 1))
                for h in range(BCH):
                    chunk(x, (bank(2 * (c % 2)), bank(2 * (c % 2) + 1)), (hTh, hTl), h * CT, h == 0, h == BCH - 1)
                    x += 1
                    if c and h == 1:
                        transpose_x1(c - 1)
                    if c and h == 2:
                        route(c - 1)
            assert x == CHUNKS
            transpose_x1(NC - 1)
            route(NC - 1)
            pe.sem_inc(sem("slotM_free"), 1)
            wait(pe, ("Mt", 1))
            mm(bank(1)[:, 0:NE], upT, Mt[:, 0:NE], start=True, stop=True)
            mm(bank(1)[:, NE:2 * NE], upT, Mt[:, NE:2 * NE], start=True, stop=False)
            mm(bank(1)[:, NE:2 * NE], ones, Mt[:, 0:NE], start=False, stop=True)
            mm(bank(2, NE), ones, Mt[:, 0:NE], start=True, stop=False)
            mm(bank(2, NE), ones, Mt[:, NE:2 * NE], start=False, stop=True).then_inc(sem("ranks"), 1)
            wait(pe, ("rounds_ready", 1))
            wait(pe, ("h2", 2))
            pe.sem_inc(sem("xadd"), 2)
            pe.sem_inc(sem("yev"), 2)
            pe.sem_inc(sem("combT"), 1)
            rounds = pe.value_load(rounds_i[0:1, 0:1], min_val=1, max_val=SEQ // CAP)
            with pe.Fori(0, rounds) as r:
                with pe.Fori(0, PAIRS) as p:
                    n = r * PAIRS + p
                    pe.wait_ge(sem("sel"), n + 1)
                    for b in range(4):
                        if b >= 2:
                            pe.wait_ge(sem("xe"), n * 4 + b - 1)
                        for k in range(4):
                            for m in range(NM):
                                i = mm(bank(2 + b % 2)[:, k * P:(k + 1) * P], h2[:, m, 4 * b + k::KT],
                                       sel[:, m * P:(m + 1) * P], start=(m == 0), stop=(m == NM - 1))
                        i.then_inc(sem("gath"), 1)
                    pe.wait_ge(sem("selg"), n + 1)
                    pe.wait_ge(sem("xe"), n * 4 + 3)
                    for m in range(NM):
                        i = tr(bank(2)[:, m * P:(m + 1) * P], selg[:, m * P:(m + 1) * P], ident)
                    i.then_inc(sem("combT"), 1)
                    pe.wait_ge(sem("xe"), n * 4 + 4)
                    j = 0
                    for w in range(2):
                        for h in range(2):
                            for e in range(2):
                                pe.wait_ge(sem(f"slotM{(j + e) % RING_M}"), n * 32 + 16 * ((j + e) // RING_M + 1))
                            for k in range(HT):
                                for e in range(2):
                                    i = mm(bank(w)[e * CAP:(e + 1) * CAP, :],
                                           xeT[:, h * HT + k, e * CAP:(e + 1) * CAP],
                                           ringM[:, (j + e) % RING_M, k * CB:(k + 1) * CB],
                                           start=(h == 0 and k == 0), stop=(h == 1 and k == HT - 1))
                            i.then_inc(sem("slotM_free"), 2)
                            j += 2
                    pe.wait_ge(sem("hid"), n + 1)
                    for t in range(FT):
                        i = tr(bank(3)[:, t * P:(t + 1) * P], hid[:, t::FT], ident)
                    i.then_inc(sem("actT"), 1)
                    pe.wait_ge(sem("aT"), n + 1)
                    pe.wait_ge(sem("comb"), n + 1)

                    def combine(k):
                        pe.wait_ge(sem("yev"), n * NC + k + 3)
                        for m in range(NM):
                            pe.wait_ge(sem("xadd"), n * 8 + 2 * k + m + 1)
                            mm(bank(6 + m), comb[:, m * P:(m + 1) * P], Ysb[:, k * CB:(k + 1) * CB], start=True,
                               stop=True).then_inc(sem("cmb"), 1)

                    for k in range(NC):
                        if k % 2 == 0:
                            for e in range(2):
                                pe.wait_ge(sem(f"slotM{(j + e) % RING_M}"), n * 32 + 16 * ((j + e) // RING_M + 1))
                        pe.wait_ge(sem("yev"), n * NC + k + 1)
                        for t in range(FT):
                            for e in range(2):
                                src = ringM[:, (j + e) % RING_M, :].rearrange("p (t n) -> p t n", t=FT)
                                i = mm(bank(4 + k % 2)[e * CAP:(e + 1) * CAP, :],
                                       aT[:, t * P + e * CAP:t * P + (e + 1) * CAP],
                                       src[:, t, (k % 2) * CB:(k % 2 + 1) * CB], start=(t == 0), stop=(t == FT - 1))
                        if k % 2 == 0:
                            i.then_inc(sem("down"), 1)
                        else:
                            i.then_inc(sem("slotM_free"), 2)
                            j += 2
                        if k:
                            combine(k - 1)
                    combine(NC - 1)


_INS = ["x", "norm_mix", "w_in", "conv_a", "a_log", "dt_bias", "a_norm", "w_gk2", "b_gk", "b_norm", "w_oa", "w_ob",
        "w_out", "norm_ffn", "w_rg", "b_rg", "w_re", "b_re", "w1", "w3", "w2", "norm_final"]


def kernel(**inputs):
    import numpy as _np
    import concourse.bacc as _bacc
    from concourse import mybir as _mybir
    from concourse.bass_utils import run_bass_kernel_spmd as _run

    nc = _bacc.Bacc("TRN2", target_bir_lowering=False, num_devices=1)
    arrays, args = {}, []
    for name in _INS:
        a = _np.ascontiguousarray(inputs[name])
        arrays[f"in_{name}"] = a
        args.append(nc.dram_tensor(f"in_{name}", a.shape, _mybir.dt.from_np(a.dtype), kind="ExternalInput").ap())
    args.append(nc.dram_tensor("out_y", (1, SEQ, D), _mybir.dt.float32, kind="ExternalOutput").ap())
    build(nc, *args)
    r = _run(nc, [arrays], core_ids=[0])
    return r.results[0]["out_y"]
```
